# Optimizing a Trainium2 kernel written in Bass

```python
import jax, jax.numpy as jnp
from jax import lax
import numpy as np
import math

D_MODEL = 1024
BATCH = 1
SEQ = 512
DEPTH = 1

CHUNK = 64
POOL_WIDTH = D_MODEL // 2
POOL_GROUPS = 4
POOL_GROUP_DIM = POOL_WIDTH // POOL_GROUPS
POOL_WINDOWS = (2, 4, 8, 16)
CONV_WIDTH = D_MODEL // 2
CONV_K = 31
D_FF = 4 * D_MODEL
IN_COLS = POOL_WIDTH + 2 * CONV_WIDTH + 2 * D_MODEL
EPS = 1e-6


def rmsnorm(x, g):
    xf = x.astype(jnp.float32)
    y = xf * lax.rsqrt(jnp.mean(xf * xf, axis=-1, keepdims=True) + EPS)
    return (y * g.astype(jnp.float32)).astype(x.dtype)

def layernorm(x, g, b):
    xf = x.astype(jnp.float32)
    mu = jnp.mean(xf, axis=-1, keepdims=True)
    var = jnp.mean(jnp.square(xf - mu), axis=-1, keepdims=True)
    y = (xf - mu) * lax.rsqrt(var + EPS)
    return (y * g.astype(jnp.float32) + b.astype(jnp.float32)).astype(x.dtype)

def trailing_mean_minus_self(u, window):
    uf = u.astype(jnp.float32)
    c = jnp.cumsum(uf, axis=1)
    c_prev = jnp.pad(c, ((0, 0), (window, 0), (0, 0)))[:, : u.shape[1], :]
    count = jnp.minimum(jnp.arange(1, u.shape[1] + 1, dtype=jnp.float32), float(window))
    mean = (c - c_prev) / count[None, :, None]
    return (mean - uf).astype(u.dtype)

def pool_mixer(u, pool_w, pool_scale, w_pool_out):
    groups = jnp.split(u, POOL_GROUPS, axis=-1)
    pooled = jnp.stack([trailing_mean_minus_self(g, w) for g, w in zip(groups, POOL_WINDOWS)], axis=2)
    mixed = jnp.einsum('bsgc,gcd->bsgd', pooled, pool_w)
    mixed = mixed.reshape(u.shape) * pool_scale
    return mixed @ w_pool_out

def conformer_conv(glu_in, conv_w, conv_b, ln_g, ln_b, w_conv_out):
    a, gate = jnp.split(glu_in, 2, axis=-1)
    v = a * jax.nn.sigmoid(gate)
    rhs = conv_w.astype(v.dtype)[:, None, :]
    v = lax.conv_general_dilated(v, rhs, window_strides=(1,), padding=[(CONV_K - 1, 0)],
                                 dimension_numbers=('NWC', 'WIO', 'NWC'),
                                 feature_group_count=CONV_WIDTH) + conv_b
    v = layernorm(v, ln_g, ln_b)
    v = jax.nn.silu(v)
    return v @ w_conv_out

def first_inputs(seed: int = 0) -> dict:
    key = jax.random.key(seed)
    ks = jax.random.split(key, 20)
    L, D = DEPTH, D_MODEL
    nrm = lambda k, shape, fan_in: jax.random.normal(k, shape, jnp.float32) * (fan_in ** -0.5)
    gain = lambda k, shape: 1.0 + 0.05 * jax.random.normal(k, shape, jnp.float32)
    return {
        "x": jax.random.normal(ks[0], (BATCH, SEQ, D), jnp.float32),
        "norm_mix_pre": gain(ks[1], (L, D)),
        "w_in": nrm(ks[2], (L, D, IN_COLS), D),
        "pool_w": nrm(ks[3], (L, POOL_GROUPS, POOL_GROUP_DIM, POOL_GROUP_DIM), POOL_GROUP_DIM),
        "pool_scale": gain(ks[4], (L, POOL_WIDTH)),
        "w_pool_out": nrm(ks[5], (L, POOL_WIDTH, D), POOL_WIDTH),
        "conv_w": nrm(ks[6], (L, CONV_K, CONV_WIDTH), CONV_K),
        "conv_b": 0.02 * jax.random.normal(ks[7], (L, CONV_WIDTH), jnp.float32),
        "conv_ln_g": gain(ks[8], (L, CONV_WIDTH)),
        "conv_ln_b": 0.02 * jax.random.normal(ks[9], (L, CONV_WIDTH), jnp.float32),
        "w_conv_out": nrm(ks[10], (L, CONV_WIDTH, D), CONV_WIDTH),
        "w_o": nrm(ks[11], (L, D, D), D),
        "norm_mix_post": gain(ks[12], (L, D)),
        "norm_mlp_pre": gain(ks[13], (L, D)),
        "w_up": nrm(ks[14], (L, D, D_FF), D),
        "w_down": nrm(ks[15], (L, D_FF, D), D_FF),
        "norm_mlp_post": gain(ks[16], (L, D)),
    }

def first_block(x, norm_mix_pre, w_in, pool_w, pool_scale, w_pool_out, conv_w, conv_b,
              conv_ln_g, conv_ln_b, w_conv_out, w_o, norm_mix_post, norm_mlp_pre,
              w_up, w_down, norm_mlp_post):
    for l in range(DEPTH):
        h = rmsnorm(x, norm_mix_pre[l])
        proj = h @ w_in[l]
        u_pool, u_glu, g_a, g_b = jnp.split(
            proj, [POOL_WIDTH, POOL_WIDTH + 2 * CONV_WIDTH, POOL_WIDTH + 2 * CONV_WIDTH + D_MODEL], axis=-1)
        branch_a = pool_mixer(u_pool, pool_w[l], pool_scale[l], w_pool_out[l])
        branch_b = conformer_conv(u_glu, conv_w[l], conv_b[l], conv_ln_g[l], conv_ln_b[l], w_conv_out[l])
        merged = jax.nn.sigmoid(g_a) * branch_a + jax.nn.sigmoid(g_b) * branch_b
        x = x + rmsnorm(merged @ w_o[l], norm_mix_post[l])
        h = rmsnorm(x, norm_mlp_pre[l])
        f = jnp.square(jax.nn.relu(h @ w_up[l])) @ w_down[l]
        x = x + rmsnorm(f, norm_mlp_post[l])
    return x


DEPTH_2 = 2

N_A_LAYERS = DEPTH_2 // 2
N_B_LAYERS = DEPTH_2 - N_A_LAYERS

A_HEADS = 8
A_DK = 128
A_DV = 128
A_CONV = 4
A_CHUNK = 64
A_QK = A_HEADS * A_DK
A_V = A_HEADS * A_DV
A_IN = 2 * A_QK + 2 * A_V + 2 * A_HEADS

B_HEADS = 16
B_KV_HEADS = 4
B_GROUP = B_HEADS // B_KV_HEADS
B_DH = 64
B_WINDOW = 128
B_BLOCK = 128

FFN_DIM = 2816
FFN_CONV = 3


def rmsnorm_2(x, g):
    xf = x.astype(jnp.float32)
    y = xf * lax.rsqrt(jnp.mean(xf * xf, axis=-1, keepdims=True) + EPS)
    return (y * g.astype(jnp.float32)).astype(x.dtype)

def l2norm(x):
    return x * lax.rsqrt(jnp.sum(x * x, axis=-1, keepdims=True) + EPS)

def causal_dwconv(x, w):
    K = w.shape[0]
    S = x.shape[1]
    xp = jnp.pad(x, ((0, 0), (K - 1, 0), (0, 0)))
    y = xp[:, K - 1:K - 1 + S] * w[K - 1]
    for j in range(K - 1):
        y = y + xp[:, j:j + S] * w[j]
    return y

def gated_delta_rule_chunked(q, k, v, beta, g):
    Bsz, S, H, DK = q.shape
    DV = v.shape[-1]
    C = A_CHUNK
    N = S // C

    def chunk(t):
        t = t.reshape((Bsz, N, C, H) + t.shape[3:])
        return jnp.moveaxis(t, 3, 1)

    q, k, v, beta, g = chunk(q), chunk(k), chunk(v), chunk(beta), chunk(g)
    gc = jnp.cumsum(g, axis=-1)
    idx = jnp.arange(C)
    strict = idx[:, None] > idx[None, :]
    incl = idx[:, None] >= idx[None, :]
    diff = gc[..., :, None] - gc[..., None, :]
    decay = jnp.exp(jnp.where(incl, diff, -jnp.inf))
    kb = k * beta[..., None]
    Lmat = jnp.where(strict, jnp.einsum('bhnid,bhnjd->bhnij', kb, k) * decay, 0.0)
    eye = jnp.eye(C, dtype=Lmat.dtype)
    rhs = jnp.concatenate([v * beta[..., None], kb * jnp.exp(gc)[..., None]], axis=-1)
    sol = lax.linalg.triangular_solve(eye + Lmat, rhs, left_side=True, lower=True, unit_diagonal=True)
    value, k_cumdecay = sol[..., :DV], sol[..., DV:]
    attn_intra = jnp.einsum('bhnid,bhnjd->bhnij', q, k) * decay
    q_dec = q * jnp.exp(gc)[..., None]
    k_dec = k * jnp.exp(gc[..., -1:] - gc)[..., None]
    g_last = jnp.exp(gc[..., -1])

    def step(state, xs):
        a_c, qd, kd, val, kcd, gl = xs
        v_new = val - jnp.einsum('bhcd,bhde->bhce', kcd, state)
        o = jnp.einsum('bhcd,bhde->bhce', qd, state) + jnp.einsum('bhij,bhje->bhie', a_c, v_new)
        state = state * gl[..., None, None] + jnp.einsum('bhcd,bhce->bhde', kd, v_new)
        return state, o

    xs = tuple(jnp.moveaxis(t, 2, 0) for t in (attn_intra, q_dec, k_dec, value, k_cumdecay, g_last))
    state0 = jnp.zeros((Bsz, H, DK, DV), jnp.float32)
    _, o = lax.scan(step, state0, xs)
    o = jnp.moveaxis(jnp.moveaxis(o, 0, 2), 1, 3)
    return o.reshape(Bsz, S, H, DV)

def deltanet_mixer(h, w_in, conv_w, A_log, dt_bias, onorm_g, w_out):
    Bsz, S, _ = h.shape
    f32 = jnp.float32
    p = h @ w_in
    qkv, gate, b_raw, a_raw = jnp.split(p, [2 * A_QK + A_V, 2 * A_QK + 2 * A_V, 2 * A_QK + 2 * A_V + A_HEADS], axis=-1)
    qkv = jax.nn.silu(causal_dwconv(qkv, conv_w))
    q, k, v = jnp.split(qkv, [A_QK, 2 * A_QK], axis=-1)
    q = l2norm(q.reshape(Bsz, S, A_HEADS, A_DK).astype(f32)) * (A_DK ** -0.5)
    k = l2norm(k.reshape(Bsz, S, A_HEADS, A_DK).astype(f32))
    v = v.reshape(Bsz, S, A_HEADS, A_DV).astype(f32)
    beta = jax.nn.sigmoid(b_raw.astype(f32))
    g = -jnp.exp(A_log.astype(f32)) * jax.nn.softplus(a_raw.astype(f32) + dt_bias.astype(f32))
    o = gated_delta_rule_chunked(q, k, v, beta, g)
    o = rmsnorm_2(o, onorm_g) * jax.nn.silu(gate.reshape(Bsz, S, A_HEADS, A_DV).astype(f32))
    return o.reshape(Bsz, S, A_V).astype(h.dtype) @ w_out

def swa_sink_attention(h, k_sh, v_sh, w_q, b_q, sinks, w_o, b_o):
    Bsz, S, _ = h.shape
    f32 = jnp.float32
    NB = S // B_BLOCK
    q = (h @ w_q + b_q).astype(f32) * (B_DH ** -0.5)
    q = q.reshape(Bsz, NB, B_BLOCK, B_KV_HEADS, B_GROUP, B_DH)

    def with_prev(t):
        t = t.astype(f32).reshape(Bsz, NB, B_BLOCK, B_KV_HEADS, B_DH)
        prev = jnp.pad(t, ((0, 0), (1, 0), (0, 0), (0, 0), (0, 0)))[:, :-1]
        return jnp.concatenate([prev, t], axis=2)

    kb, vb = with_prev(k_sh), with_prev(v_sh)
    slopes = (2.0 ** (-8.0 * jnp.arange(1, B_HEADS + 1, dtype=f32) / B_HEADS)).reshape(B_KV_HEADS, B_GROUP)
    qi = jnp.arange(B_BLOCK)[:, None]
    kj = jnp.arange(2 * B_BLOCK)[None, :]
    dist = qi + B_BLOCK - kj
    band = (dist >= 0) & (dist < B_WINDOW)
    bias = -slopes[:, :, None, None] * dist.astype(f32)
    sink = sinks.astype(f32).reshape(B_KV_HEADS, B_GROUP)[None, :, :, None]

    def block_attn(args):
        qb, kk, vv, blk = args
        s = jnp.einsum('bqkgd,bskd->bkgqs', qb, kk) + bias
        valid = band & ((blk > 0) | (kj >= B_BLOCK))
        s = jnp.where(valid, s, -jnp.inf)
        m = jnp.maximum(jnp.max(s, axis=-1), sink)
        p = jnp.exp(s - m[..., None])
        denom = jnp.sum(p, axis=-1) + jnp.exp(sink - m)
        o = jnp.einsum('bkgqs,bskd->bqkgd', p, vv)
        return o / jnp.transpose(denom, (0, 3, 1, 2))[..., None]

    xs = (jnp.moveaxis(q, 1, 0), jnp.moveaxis(kb, 1, 0), jnp.moveaxis(vb, 1, 0), jnp.arange(NB, dtype=jnp.int32))
    o = lax.map(block_attn, xs)
    o = jnp.moveaxis(o, 0, 1).reshape(Bsz, S, B_HEADS * B_DH)
    return o.astype(h.dtype) @ w_o + b_o

def conv_ffn(h, w_up, conv_w, conv_b, w_down):
    u = causal_dwconv(h @ w_up, conv_w) + conv_b
    gate, up = jnp.split(u, 2, axis=-1)
    return (jax.nn.silu(gate) * up) @ w_down

def second_inputs(seed: int = 0) -> dict:
    key = jax.random.key(seed)
    ks = jax.random.split(key, 24)
    f32 = jnp.float32

    def nrm(k, shape, fan_in):
        return jax.random.normal(k, shape, f32) * (fan_in ** -0.5)

    def gain(k, shape):
        return 1.0 + 0.05 * jax.random.normal(k, shape, f32)

    def small(k, shape):
        return 0.02 * jax.random.normal(k, shape, f32)

    x = jax.random.normal(ks[0], (BATCH, SEQ, D_MODEL), f32)
    a_norm = gain(ks[1], (N_A_LAYERS, D_MODEL))
    a_w_in = nrm(ks[2], (N_A_LAYERS, D_MODEL, A_IN), D_MODEL)
    a_conv_w = nrm(ks[3], (N_A_LAYERS, A_CONV, 2 * A_QK + A_V), A_CONV)
    a_A_log = jnp.log(jax.random.uniform(ks[4], (N_A_LAYERS, A_HEADS), f32, 1.0, 16.0))
    dt = jnp.exp(jax.random.uniform(ks[5], (N_A_LAYERS, A_HEADS), f32, math.log(1e-3), math.log(1e-1)))
    a_dt_bias = dt + jnp.log(-jnp.expm1(-dt))
    a_onorm = gain(ks[6], (N_A_LAYERS, A_DV))
    a_w_out = nrm(ks[7], (N_A_LAYERS, A_V, D_MODEL), A_V)
    kv_norm = gain(ks[8], (D_MODEL,))
    kv_w = nrm(ks[9], (D_MODEL, 2 * B_KV_HEADS * B_DH), D_MODEL)
    kv_b = small(ks[10], (2 * B_KV_HEADS * B_DH,))
    b_norm = gain(ks[11], (N_B_LAYERS, D_MODEL))
    b_w_q = nrm(ks[12], (N_B_LAYERS, D_MODEL, B_HEADS * B_DH), D_MODEL)
    b_b_q = small(ks[13], (N_B_LAYERS, B_HEADS * B_DH))
    b_sinks = jax.random.normal(ks[14], (N_B_LAYERS, B_HEADS), f32)
    b_w_o = nrm(ks[15], (N_B_LAYERS, B_HEADS * B_DH, D_MODEL), B_HEADS * B_DH)
    b_b_o = small(ks[16], (N_B_LAYERS, D_MODEL))
    f_norm = gain(ks[17], (DEPTH_2, D_MODEL))
    f_w_up = nrm(ks[18], (DEPTH_2, D_MODEL, 2 * FFN_DIM), D_MODEL)
    f_conv_w = nrm(ks[19], (DEPTH_2, FFN_CONV, 2 * FFN_DIM), FFN_CONV)
    f_conv_b = small(ks[20], (DEPTH_2, 2 * FFN_DIM))
    f_w_down = nrm(ks[21], (DEPTH_2, FFN_DIM, D_MODEL), FFN_DIM)
    final_norm = gain(ks[22], (D_MODEL,))
    return {'x': x, 'a_norm': a_norm, 'a_w_in': a_w_in, 'a_conv_w': a_conv_w, 'a_A_log': a_A_log,
            'a_dt_bias': a_dt_bias, 'a_onorm': a_onorm, 'a_w_out': a_w_out,
            'kv_norm': kv_norm, 'kv_w': kv_w, 'kv_b': kv_b,
            'b_norm': b_norm, 'b_w_q': b_w_q, 'b_b_q': b_b_q, 'b_sinks': b_sinks, 'b_w_o': b_w_o, 'b_b_o': b_b_o,
            'f_norm': f_norm, 'f_w_up': f_w_up, 'f_conv_w': f_conv_w, 'f_conv_b': f_conv_b, 'f_w_down': f_w_down,
            'final_norm': final_norm}

def second_block(x, a_norm, a_w_in, a_conv_w, a_A_log, a_dt_bias, a_onorm, a_w_out,
              kv_norm, kv_w, kv_b,
              b_norm, b_w_q, b_b_q, b_sinks, b_w_o, b_b_o,
              f_norm, f_w_up, f_conv_w, f_conv_b, f_w_down, final_norm):
    Bsz, S, _ = x.shape
    h = x
    k_sh = None
    v_sh = None
    for layer in range(DEPTH_2):
        if layer < N_A_LAYERS:
            i = layer
            h = h + deltanet_mixer(rmsnorm_2(h, a_norm[i]), a_w_in[i], a_conv_w[i], a_A_log[i],
                                   a_dt_bias[i], a_onorm[i], a_w_out[i])
        else:
            i = layer - N_A_LAYERS
            if i == 0:
                kv = rmsnorm_2(h, kv_norm) @ kv_w + kv_b
                k_sh, v_sh = jnp.split(kv, 2, axis=-1)
                k_sh = k_sh.reshape(Bsz, S, B_KV_HEADS, B_DH)
                v_sh = v_sh.reshape(Bsz, S, B_KV_HEADS, B_DH)
            h = h + swa_sink_attention(rmsnorm_2(h, b_norm[i]), k_sh, v_sh, b_w_q[i], b_b_q[i],
                                       b_sinks[i], b_w_o[i], b_b_o[i])
        h = h + conv_ffn(rmsnorm_2(h, f_norm[layer]), f_w_up[layer], f_conv_w[layer],
                         f_conv_b[layer], f_w_down[layer])
    return rmsnorm_2(h, final_norm)


def setup_inputs(seed=0):
    out = dict(first_inputs(seed))
    for name, value in second_inputs(seed + 1).items():
        if name != "x":
            out[name + "_2"] = value
    return out


def reference(
    x, norm_mix_pre, w_in, pool_w, pool_scale, w_pool_out, conv_w, conv_b, conv_ln_g, conv_ln_b,
    w_conv_out, w_o, norm_mix_post, norm_mlp_pre, w_up, w_down, norm_mlp_post, a_norm_2,
    a_w_in_2, a_conv_w_2, a_A_log_2, a_dt_bias_2, a_onorm_2, a_w_out_2, kv_norm_2, kv_w_2,
    kv_b_2, b_norm_2, b_w_q_2, b_b_q_2, b_sinks_2, b_w_o_2, b_b_o_2, f_norm_2, f_w_up_2,
    f_conv_w_2, f_conv_b_2, f_w_down_2, final_norm_2,
):
    x = first_block(
        x, norm_mix_pre, w_in, pool_w, pool_scale, w_pool_out, conv_w, conv_b, conv_ln_g,
        conv_ln_b, w_conv_out, w_o, norm_mix_post, norm_mlp_pre, w_up, w_down, norm_mlp_post,
    )
    return second_block(
        x, a_norm_2, a_w_in_2, a_conv_w_2, a_A_log_2, a_dt_bias_2, a_onorm_2, a_w_out_2,
        kv_norm_2, kv_w_2, kv_b_2, b_norm_2, b_w_q_2, b_b_q_2, b_sinks_2, b_w_o_2, b_b_o_2,
        f_norm_2, f_w_up_2, f_conv_w_2, f_conv_b_2, f_w_down_2, final_norm_2,
    )


_drawn_inputs = setup_inputs


def setup_inputs(seed=0):
    import zlib

    import numpy as np

    out = dict(_drawn_inputs(seed))
    spreads = {}
    factors = {'conv_ln_b': 5.376,
     'a_onorm_2': 3.128,
     'kv_norm_2': 4.917,
     'kv_b_2': 5.575,
     'b_norm_2': 8.0,
     'b_b_q_2': 8.0,
     'b_b_o_2': 14.699,
     'f_conv_b_2': 4.492,
     'b_sinks_2': 8.0}
    for name, (base, spread) in spreads.items():
        noise = np.random.default_rng([zlib.crc32(name.encode()), seed]).standard_normal(out[name].shape)
        drawn = base * np.exp(spread * noise) if base else spread * noise
        out[name] = __import__('jax').numpy.asarray(drawn.astype(out[name].dtype))
    for name, factor in factors.items():
        out[name] = (out[name] * factor).astype(out[name].dtype)
    return out
```

```python
from contextlib import ExitStack

import numpy as np

import concourse.bass as bass
from concourse import mybir
from concourse.alu_op_type import AluOpType as ALU

ACT = mybir.ActivationFunctionType
F32 = mybir.dt.float32
F32R = mybir.dt.float32r

P = 128
T = 512
NCH = T // P
D = 1024
KT = D // P
EPS = 1e-6
CONV_K = 31
FPAD = 2
APAD = 3
HEADS = 8
SLOTS = 4
LEAD = 2
ACC_TAPS = 8

U_GLU = 0
U_POOL = U_GLU + 8
U_GATE = U_POOL + 4
U_BRANCH = U_GATE + 16
U_WO = U_BRANCH + 8
U_MLP = U_WO + 8
U_DELTA = U_MLP + 64
U_AOUT = U_DELTA + 32
U_FFN0 = U_AOUT + 8
MID_GROUPS = (8, 8, 6)
U_KV = U_FFN0 + sum(2 * g + 8 for g in MID_GROUPS)
U_Q = U_KV + 4
U_BO = U_Q + 8
U_FFN1 = U_BO + 8
U_END = U_FFN1 + sum(2 * g + 8 for g in MID_GROUPS)

_cols = {}
_n = 0
for _name, _width in (
    ("mix_pre", KT), ("mix_post", KT), ("mlp_pre", KT), ("mlp_post", KT), ("a_norm", KT), ("kv_norm", KT),
    ("b_norm", KT), ("f_norm0", KT), ("f_norm1", KT), ("final", KT),
    ("pool_scale", 4), ("conv_w", 4 * CONV_K), ("conv_b", 4), ("ln_g", 4), ("ln_b", 4),
    ("a_conv", 24 * 4), ("onorm", 1), ("b_q", 8), ("kv_b", 4), ("b_o", 8),
    ("f_conv0", 44 * 3), ("f_bias0", 44), ("f_conv1", 44 * 3), ("f_bias1", 44),
):
    _cols[_name] = (_n, _width)
    _n += _width
NPAR = _n

C_ID = 0
C_TRI = C_ID + P
C_NEG = C_TRI + P
C_LVL = C_NEG + P
C_DIST = C_LVL + 7 * P
C_INV = C_DIST + 2 * P
NCONST = C_INV + 4 * 16
POOL_WINDOWS = (2, 4, 8, 16)
FAR = 1e30
ATT_TILE_HEADS = [(4 * (2 * a) + r, 4 * (2 * a + 1) + r) for r in range(4) for a in range(2)]


def build(nc, io):
    with ExitStack() as ctx:
        def sb(name, cols, dt=F32):
            return ctx.enter_context(nc.sbuf_tensor(name, [P, cols], dt))

        sems = {}

        NORMS = {}
        count = {"one": 0, "ss": 0, "hi": 0}
        for tag, squared, split in (("n0", 8, 8), ("ln", 4, 4), ("post0", 8, 0), ("n1", 8, 8), ("post1", 8, 0),
                                    ("na", 8, 8), ("nf0", 8, 8), ("kv", 8, 8), ("bn", 0, 8), ("n_f1", 8, 8),
                                    ("fin", 8, 0)):
            NORMS[tag] = dict(count)
            NORMS[tag]["R"] = count.get("R", 0)
            count["one"] += squared > 0
            count["ss"] += squared
            count["hi"] += split
            count["R"] = NORMS[tag]["R"] + (tag in ("n0", "n1", "na", "nf0", "kv", "n_f1"))
        KINDS = {"hi": "hi", "lo": "hi", "sq": "ss", "ss": "ss", "sum": "one", "ms": "one", "rt": "one", "row": "one",
                 "R": "R"}
        FFN_STEPS = dict(half=2, pad=2, c0=44, tap=88, th=22, gate=22, prod=22, hi=22, lo=22)

        def shared(name):
            tag, _, kind = name.rpartition("_")
            if tag in NORMS and kind in KINDS:
                return "norm_" + kind, NORMS[tag][KINDS[kind]]
            if tag in ("f0", "f1") and kind in FFN_STEPS:
                return "ffn_" + kind, FFN_STEPS[kind] if tag == "f1" else 0
            return name, 0

        def S(name):
            name = shared(name)[0]
            if name not in sems:
                sems[name] = ctx.enter_context(nc.semaphore(name))
            return sems[name]

        X = sb("X", KT * T)
        pairA = (sb("A_hi", KT * T, F32R), sb("A_lo", KT * T, F32R))
        pairB = (sb("B_hi", KT * T, F32R), sb("B_lo", KT * T, F32R))
        Y = sb("Y", KT * T)
        raw = sb("w_raw", SLOTS * 1024)
        w_hi = sb("w_hi", SLOTS * 1024, F32R)
        w_lo = sb("w_lo", SLOTS * 1024, F32R)
        par = sb("par", NPAR)
        half = sb("half", 8 + 96 + 22 * 3 + 22)
        cst = sb("cst", NCONST)
        ones = sb("ones", P)
        mhalf = sb("mhalf", 2 * NCH)
        R = sb("R", T)
        SQ = sb("SQ", 2 * T)
        SS = sb("SS", T)
        tok = sb("tok", 64)
        NSCR = 10260
        scr = sb("scr", NSCR)
        small = sb("small", 48 + KT * 16)
        rowp, tailw = small[:, 0:48], small[:, 48:48 + KT * 16]
        pw = (sb("pw_hi", 512, F32R), sb("pw_lo", 512, F32R))
        ps = [ctx.enter_context(nc.psum_tensor(f"ps{b}", [P, 512], F32)) for b in range(8)]

        def par_col(name, k=0):
            c = _cols[name][0] + k
            return par[:, c:c + 1] if isinstance(c, int) else par[:, bass.ds(c, 1)]

        def tile(buf, m, n=1):
            return buf[:, m * T:(m + n) * T] if isinstance(m, int) else buf[:, bass.ds(m * T, n * T)]

        ident = cst[:, C_ID:C_ID + P]
        tri = cst[:, C_TRI:C_TRI + P]

        o = 0

        def carve(n):
            nonlocal o
            o += n
            assert o <= NSCR, (o, NSCR)
            return scr[:, o - n:o]

        SG = carve(16 * T)
        UPW = T + 16
        VATH = carve(2 * T)
        VA, TH = VATH[:, 0:T], VATH[:, T:2 * T]
        TG = carve(2 * T)
        UP = [X[:, 4 * T + 2 * UPW:4 * T + 3 * UPW], VATH[:, 0:UPW]]
        pwraw = SG[:, 0:512]
        PO = [SG[:, (8 + g) * T:(9 + g) * T] for g in range(4)]
        VPW = T + CONV_K - 1
        VP = Y[:, 0:4 * VPW]
        CVB = Y[:, 4 * VPW:4 * VPW + T]
        CTMP = Y[:, 4 * VPW + T:4 * VPW + 3 * T]
        CV = X[:, 0:4 * T]
        PAB = [X[:, 4 * T:4 * T + UPW], X[:, 4 * T + UPW:4 * T + 2 * UPW]]
        MS = SG[:, 0:2 * T]
        assert 4 * VPW + 3 * T <= KT * T

        block = ctx.enter_context(nc.Block())

        CREDIT = {"o_lo": 1, "t_lo": 1}
        for s in range(SLOTS):
            CREDIT[f"unit_done{s}"] = 1
            CREDIT[f"evac{s}"] = 1
        for name in ("mlp_sq", "conv_acc", "conv_out", "gate_th"):
            CREDIT[name] = 4

        def count(name, n):
            return n + CREDIT.get(name, 0) + shared(name)[1]

        def credit(eng, *names):
            for name in names:
                eng.sem_inc(S(name), CREDIT[name])

        def rnd(base, i):
            assert base % SLOTS == 0
            return base // SLOTS + i

        def split_hi(act, r, s):
            act.wait_ge(S(f"raw_in{s}"), 16 * (r + 1))
            act.wait_ge(S(f"unit_done{s}"), count(f"unit_done{s}", r))
            c = slice(s * 1024, (s + 1) * 1024)
            nc.scalar.activation(w_hi[:, c], raw[:, c], ACT.Copy).then_inc(S(f"w_hi{s}"), 1)

        def split_lo(dve, r, s):
            dve.wait_ge(S(f"w_hi{s}"), count(f"w_hi{s}", r + 1))
            c = slice(s * 1024, (s + 1) * 1024)
            nc.vector.tensor_tensor(w_lo[:, c], raw[:, c], w_hi[:, c].bitcast(F32), ALU.subtract)\
                .then_inc(S(f"w_lo{s}"), 1)

        def ahead(eng, split, r, k):
            split(eng, r + (k + LEAD) // SLOTS, (k + LEAD) % SLOTS)

        def unit_wait(pe, r, s):
            pe.wait_ge(S(f"w_hi{s}"), count(f"w_hi{s}", r + 1))
            pe.wait_ge(S(f"w_lo{s}"), count(f"w_lo{s}", r + 1))
            pe.wait_ge(S(f"evac{(s + 2) % SLOTS}"), count(f"evac{(s + 2) % SLOTS}", r + 1 if s >= 2 else r))

        def blocks(pe, bank, s, pair, first, n, at=0, wait=None):
            for k in range(n):
                if wait:
                    wait(k)
                c = slice(s * 1024 + (at + k) * P, s * 1024 + (at + k + 1) * P)
                hi, lo = tile(pair[0], first + k), tile(pair[1], first + k)
                pe.matmul(ps[bank][:], w_hi[:, c], hi, start=k == 0, stop=False)
                pe.matmul(ps[bank][:], w_hi[:, c], lo, start=False, stop=False)
                last = pe.matmul(ps[bank][:], w_lo[:, c], hi, start=False, stop=k == n - 1)
            return last

        def unit(pe, r, s, pair, n=KT, wait=None):
            unit_wait(pe, r, s)
            blocks(pe, s % 2, s, pair, 0, n, wait=wait).then_inc(S(f"unit_done{s}"), 1)

        def evac_wait(eng, r, s):
            eng.wait_ge(S(f"unit_done{s}"), count(f"unit_done{s}", r + 1))

        def norm_act(act, tag, g, pair, xready, squares=True):
            for m in range(KT):
                xready(act, m)
                nc.scalar.activation(tile(pair[0], m), tile(X, m), ACT.Copy, scale=par_col(g, m))\
                    .then_inc(S(tag + "_hi"), 1)
                if squares:
                    square(act, tag, m, tile(X, m))

        def square(act, tag, m, src, scale=1.0):
            if m > 1:
                act.wait_ge(S(tag + "_ss"), count(tag + "_ss", m - 1))
            nc.scalar.activation(tile(SQ, m % 2), src, ACT.Square, scale=scale).then_inc(S(tag + "_sq"), 1)

        def norm_lo(dve, tag, g, pair, m):
            dve.wait_ge(S(tag + "_hi"), count(tag + "_hi", m + 1))
            nc.vector.scalar_tensor_tensor(out=tile(pair[1], m), in0=tile(X, m), scalar=par_col(g, m),
                                           in1=tile(pair[0], m).bitcast(F32), op0=ALU.mult, op1=ALU.subtract)\
                .then_inc(S(tag + "_lo"), 1)

        def sum_squares(pool, tag, n):
            for m in range(n):
                pool.wait_ge(S(tag + "_sq"), count(tag + "_sq", m + 1))
                if m == 0:
                    nc.gpsimd.tensor_copy(SS[:], tile(SQ, 0)).then_inc(S(tag + "_ss"), 1)
                else:
                    pool.wait_ge(S(tag + "_ss"), count(tag + "_ss", m))
                    nc.gpsimd.tensor_tensor(SS[:], SS[:], tile(SQ, m % 2), ALU.add).then_inc(S(tag + "_ss"), 1)

        def token_sums(pe, tag, n, bank):
            pe.wait_ge(S(tag + "_ss"), count(tag + "_ss", n))
            for c in range(NCH):
                last = pe.matmul(ps[bank][:, c:c + 1], SS[:, c * P:(c + 1) * P], ones[:, 0:1], start=True, stop=True)
            last.then_inc(S(tag + "_sum"), 1)

        def token_mean(dve, tag, bank, n):
            dve.wait_ge(S(tag + "_sum"), count(tag + "_sum", 1))
            nc.vector.tensor_scalar(tok[:, 0:NCH], ps[bank][:, 0:NCH], 1.0 / n, EPS, ALU.mult, ALU.add)\
                .then_inc(S(tag + "_ms"), 1)

        def token_rsqrt(pool, tag):
            pool.wait_ge(S(tag + "_ms"), count(tag + "_ms", 1))
            nc.gpsimd.tensor_tensor(tok[:, NCH:2 * NCH], tok[:, 0:NCH], mhalf[:, 0:NCH], ALU.pow)\
                .then_inc(S(tag + "_rt"), 1)

        def spread(pe, src, bank):
            for c in range(NCH):
                last = pe.matmul(ps[bank][:, c * P:(c + 1) * P], src[:, c:c + 1].broadcast_to([P, P]), ident,
                                 start=True, stop=True)
            return last

        def norm_pe(pe, tag, n=KT, bank=2):
            token_sums(pe, tag, n, bank)
            pe.wait_ge(S(tag + "_rt"), count(tag + "_rt", 1))
            spread(pe, tok[:, NCH:2 * NCH], bank + 1).then_inc(S(tag + "_row"), 1)

        def norm_row(act, tag, bank=2):
            act.wait_ge(S(tag + "_row"), count(tag + "_row", 1))
            nc.scalar.activation(R[:], ps[bank + 1][:], ACT.Copy).then_inc(S(tag + "_R"), 1)

        def pair_wait(tag):
            def wait(pe):
                def at(k):
                    pe.wait_ge(S(tag + "_hi"), count(tag + "_hi", k + 1))
                    pe.wait_ge(S(tag + "_lo"), count(tag + "_lo", k + 1))
                return at
            return wait

        def x_loaded(eng, m):
            eng.wait_ge(S("x_in"), count("x_in", 16))

        o = 0
        yo = 0

        def carve_y(n):
            nonlocal yo
            yo += n
            assert yo <= KT * T
            return Y[:, yo - n:yo]
        AU = [carve(T + APAD + 1) for _ in range(2)]
        AC = [carve(T) for _ in range(2)]
        AT = [carve(T) for _ in range(2)]
        KQ = carve(2 * T)
        KQv = KQ.rearrange("p (c n t) -> p c n t", c=NCH, n=2)
        VT, GT = carve(T), carve(T)
        KG, KD, VR = carve(T), carve(T), carve(T)
        DT, EG, QD = carve(T), carve(T), carve(T)
        LA = carve_y(2 * T)
        LAv = LA.rearrange("p (c n t) -> p c n t", c=NCH, n=2)
        XB, TB, TTB, WT = (carve_y(T) for _ in range(4))
        VN = [carve_y(P) for _ in range(2)]
        ST = [carve_y(P) for _ in range(2)]
        O2 = carve_y(T)
        HC = HEADS * NCH
        BA = carve(NCH * 16)
        BAv = BA.rearrange("p (c n) -> p n c", c=NCH)
        BETA, G, NGC, EGC, EGL, EKD, Z1, Z2 = (carve(HC) for _ in range(8))
        NEA = carve(HEADS)
        TK = carve(32)
        assert o <= NSCR

        def v3(ap):
            return ap.rearrange("p (c t) -> p c t", c=NCH)

        def over_tokens(ap):
            return ap.unsqueeze(2).broadcast_to([P, NCH, P])

        def over_chunks(ap):
            return ap.unsqueeze(1).broadcast_to([P, NCH, P])

        def level(l):
            return over_chunks(cst[:, C_LVL + l * P:C_LVL + (l + 1) * P])

        PER = dict(d_c0=3, d_tap=9, d_th=4, d_qkv=3, d_gate=1, d_sq=2, d_ssq=1, d_tr=1, d_gcol=1, d_gb=1, d_gram=1,
                   d_s1=4, d_sqk=1, d_mask=1, d_dt=4, d_eg=1, d_la=8, d_tt=7, d_t=6, d_ptr=1, d_px=6, d_x=7,
                   d_pt=6, d_pw=1, d_wt=1, d_pv=4, d_vn=4, d_po=1, d_ps=3, d_s=3, d_osq=1, d_os=1, d_oms=2,
                   d_orow=1, d_ro=1, d_o1=1, d_o2=1, o_hi=1, o_lo=1)

        def head_count(h):
            def at(name, k):
                return count(name, h * PER[name] + k)
            return at

        def chunk(ap, c):
            return ap[:, c * P:(c + 1) * P]

        def delta_pe(pe, h):
            at = head_count(h)
            pe.wait_ge(S("d_gcol"), at("d_gcol", 1))
            for c in range(NCH):
                last = pe.matmul(chunk(ps[5], c), TK[:, c:c + 1].broadcast_to([P, P]), tri, start=True, stop=True)
            last.then_inc(S("d_gb"), 1)
            pe.wait_ge(S("d_qkv"), at("d_qkv", 3))
            for c in range(NCH):
                last = pe.matmul(ps[6 + c // 2][:, (c % 2) * 256:(c % 2 + 1) * 256], KQv[:, c, 0, :],
                                 KQ[:, c * 256:(c + 1) * 256], start=True, stop=True)
            last.then_inc(S("d_gram"), 1)
            for c in range(NCH):
                pe.transpose(chunk(ps[3], c), KQv[:, c, 0, :], ident)
            for c in range(NCH):
                last = pe.transpose(chunk(ps[4], c), chunk(VT, c), ident)
            last.then_inc(S("d_tr"), 1)
            pe.wait_ge(S("d_sq"), at("d_sq", 2))
            for n in range(2):
                for c in range(NCH):
                    last = pe.matmul(ps[2][:, n * NCH + c:n * NCH + c + 1], SQ[:, n * T + c * P:n * T + (c + 1) * P],
                                     ones[:, 0:1], start=True, stop=True)
            last.then_inc(S("d_ssq"), 1)
            pe.wait_ge(S("d_tt"), at("d_tt", 1))
            for c in range(NCH):
                last = pe.transpose(chunk(ps[7], c), chunk(TTB, c), ident)
            last.then_inc(S("d_ptr"), 1)
            for l in range(1, 7):
                pe.wait_ge(S("d_t"), at("d_t", l))
                pe.wait_ge(S("d_tt"), at("d_tt", l))
                if l == 1:
                    pe.wait_ge(S("d_la"), at("d_la", 7))
                for c in range(NCH):
                    last = pe.matmul(chunk(ps[4], c), LAv[:, c, 0, :], chunk(TB, c), start=True, stop=True)
                last.then_inc(S("d_px"), 1)
                pe.wait_ge(S("d_x"), at("d_x", l + 1))
                if l < 6:
                    for c in range(NCH):
                        pe.matmul(chunk(ps[5], c), chunk(TTB, c), chunk(XB, c), start=True, stop=True)
                for c in range(NCH):
                    last = pe.matmul(chunk(ps[6], c), chunk(XB, c), chunk(TTB, c), start=True, stop=True)
                last.then_inc(S("d_pt"), 1)
            pe.wait_ge(S("d_tt"), at("d_tt", 7))
            for c in range(NCH):
                last = pe.matmul(chunk(ps[4], c), chunk(KG, c), chunk(TTB, c), start=True, stop=True)
            last.then_inc(S("d_pw"), 1)
            for c in range(NCH):
                out = chunk(ps[3], c % 2)
                last = pe.matmul(out, chunk(TTB, c), chunk(VR, c), start=True, stop=c == 0)
                if c:
                    if c == 1:
                        pe.wait_ge(S("d_wt"), at("d_wt", 1))
                    pe.wait_ge(S("d_s"), at("d_s", c))
                    last = pe.matmul(out, chunk(WT, c), ST[c % 2], start=False, stop=True)
                last.then_inc(S("d_pv"), 1)
                if c:
                    pe.matmul(chunk(ps[5], c), ST[c % 2], chunk(QD, c), start=True, stop=False)
                pe.wait_ge(S("d_vn"), at("d_vn", c + 1))
                if c < NCH - 1:
                    pe.matmul(chunk(ps[6], c % 2), chunk(KD, c), VN[c % 2], start=True, stop=True).then_inc(S("d_ps"), 1)
                last = pe.matmul(chunk(ps[5], c), VN[c % 2], LAv[:, c, 1, :], start=c == 0, stop=True)
            last.then_inc(S("d_po"), 1)
            pe.wait_ge(S("d_osq"), at("d_osq", 1))
            for c in range(NCH):
                last = pe.matmul(ps[2][:, 8 + c:9 + c], SQ[:, c * P:(c + 1) * P], ones[:, 0:1], start=True, stop=True)
            last.then_inc(S("d_os"), 1)
            pe.wait_ge(S("d_orow"), at("d_orow", 1))
            for c in range(NCH):
                last = pe.matmul(chunk(ps[7], c), TK[:, 28 + c:29 + c].broadcast_to([P, P]), ident,
                                 start=True, stop=True)
            last.then_inc(S("d_ro"), 1)

        def head_col(ap, h, c=0, n=1):
            return ap[:, bass.ds(h * NCH + c, n)]

        def delta_act(act, h):
            at = head_count(h)
            a = nc.scalar
            r = rnd(U_DELTA, h)
            for k in range(SLOTS):
                ahead(act, split_hi, r, k)
                act.wait_ge(S(f"evac{k}"), count(f"evac{k}", r + 1))
                if k < 3:
                    a.activation(AC[k % 2], AU[k % 2][:, APAD:APAD + T], ACT.Copy,
                                     scale=half[:, bass.ds(8 + (k * 8 + h) * 4 + 3, 1)]).then_inc(S("d_c0"), 1)
                    act.wait_ge(S("d_tap"), at("d_tap", 3 * (k + 1)))
                a.activation(AT[k % 2], AC[k % 2], ACT.Tanh).then_inc(S("d_th"), 1)
            act.wait_ge(S("d_qkv"), at("d_qkv", 3))
            for n in range(2):
                a.activation(v3(tile(SQ, n)), KQv[:, :, n, :], ACT.Square).then_inc(S("d_sq"), 1)
            act.wait_ge(S("d_gb"), at("d_gb", 1))
            a.activation(EG, ps[5][:], ACT.Exp).then_inc(S("d_eg"), 1)
            act.wait_ge(S("d_mask"), at("d_mask", 1))
            for c in range(NCH):
                a.activation(chunk(DT, c), chunk(DT, c), ACT.Exp, bias=head_col(NGC, h, c)).then_inc(S("d_dt"), 1)
            act.wait_ge(S("d_ptr"), at("d_ptr", 1))
            a.activation(TB, ps[7][:], ACT.Copy).then_inc(S("d_t"), 1)
            act.wait_ge(S("d_pw"), at("d_pw", 1))
            a.activation(WT, ps[4][:], ACT.Copy, scale=-1.0).then_inc(S("d_wt"), 1)
            act.wait_ge(S("d_po"), at("d_po", 1))
            a.activation(SQ[:, 0:T], ps[5][:], ACT.Square).then_inc(S("d_osq"), 1)
            act.wait_ge(S("d_o2"), at("d_o2", 1))
            a.activation(tile(pairB[0], h), O2, ACT.Copy).then_inc(S("o_hi"), 1)

        def delta_dve(dve, h):
            at = head_count(h)
            v = nc.vector
            r = rnd(U_DELTA, h)
            v.tensor_copy(TK[:, 0:4], head_col(G, h, 0, 4)).then_inc(S("d_gcol"), 1)
            for k in range(SLOTS):
                ahead(dve, split_lo, r, k)
                if k < 3:
                    evacuate(dve, r, k, AU[k % 2][:, APAD:APAD + T], 1.0, R[:])
                    dve.wait_ge(S("d_c0"), at("d_c0", k + 1))
                    for n, tap in enumerate((2, 1, 0)):
                        if n:
                            dve.wait_ge(S("d_tap"), at("d_tap", 3 * k + n))
                        v.scalar_tensor_tensor(out=AC[k % 2], in0=AU[k % 2][:, tap:tap + T],
                                                   scalar=half[:, bass.ds(8 + (k * 8 + h) * 4 + tap, 1)],
                                                   in1=AC[k % 2], op0=ALU.mult, op1=ALU.add).then_inc(S("d_tap"), 1)
                    dve.wait_ge(S("d_th"), at("d_th", k + 1))
                    out = [KQv[:, :, 1, :], KQv[:, :, 0, :], v3(VT)][k]
                    v.scalar_tensor_tensor(out=out, in0=v3(AT[k % 2]), scalar=1.0, in1=v3(AC[k % 2]),
                                               op0=ALU.add, op1=ALU.mult).then_inc(S("d_qkv"), 1)
                else:
                    evacuate(dve, r, k, AC[1], 0.5, R[:])
                    dve.wait_ge(S("d_th"), at("d_th", 4))
                    v.scalar_tensor_tensor(out=GT, in0=AT[1], scalar=1.0, in1=AC[1], op0=ALU.add,
                                               op1=ALU.mult).then_inc(S("d_gate"), 1)
            dve.wait_ge(S("d_eg"), at("d_eg", 1))
            v.tensor_tensor(v3(DT), v3(ps[5][:]), over_chunks(cst[:, C_NEG:C_NEG + P]), ALU.add).then_inc(S("d_mask"), 1)
            dve.wait_ge(S("d_ssq"), at("d_ssq", 1))
            v.tensor_scalar(TK[:, 4:12], ps[2][:, 0:8], EPS, None, ALU.add).then_inc(S("d_s1"), 1)
            dve.wait_ge(S("d_s1"), at("d_s1", 1))
            v.reciprocal(TK[:, 12:16], TK[:, 4:8]).then_inc(S("d_s1"), 1)
            dve.wait_ge(S("d_s1"), at("d_s1", 2))
            v.tensor_tensor(TK[:, 16:20], TK[:, 12:16], head_col(BETA, h, 0, 4), ALU.mult).then_inc(S("d_s1"), 1)
            dve.wait_ge(S("d_s1"), at("d_s1", 3))
            v.tensor_tensor(TK[:, 20:24], TK[:, 16:20], head_col(EKD, h, 0, 4), ALU.mult).then_inc(S("d_s1"), 1)
            dve.wait_ge(S("d_gram"), at("d_gram", 1))
            for c in range(NCH):
                dve.wait_ge(S("d_dt"), at("d_dt", c + 1))
                g = ps[6 + c // 2][:, (c % 2) * 256:(c % 2 + 1) * 256].rearrange("p (n t) -> p n t", n=2)
                v.scalar_tensor_tensor(out=LAv[:, c, :, :], in0=g, scalar=TK[:, 16 + c:17 + c],
                                           in1=chunk(DT, c).unsqueeze(1).broadcast_to([P, 2, P]),
                                           op0=ALU.mult, op1=ALU.mult).then_inc(S("d_la"), 1)
            dve.wait_ge(S("d_la"), at("d_la", 4))
            v.tensor_tensor(v3(XB), LAv[:, :, 0, :], level(0), ALU.mult).then_inc(S("d_x"), 1)
            dve.wait_ge(S("d_x"), at("d_x", 1))
            v.tensor_tensor(v3(TTB), over_chunks(ident), v3(XB), ALU.subtract).then_inc(S("d_tt"), 1)
            dve.wait_ge(S("d_tr"), at("d_tr", 1))
            v.tensor_tensor(v3(KG), v3(ps[3][:]), over_tokens(head_col(EGC, h, 0, 4)), ALU.mult).then_inc(S("d_la"), 1)
            dve.wait_ge(S("d_s1"), at("d_s1", 4))
            v.tensor_tensor(v3(KD), v3(ps[3][:]), over_tokens(TK[:, 20:24]), ALU.mult).then_inc(S("d_la"), 1)
            dve.wait_ge(S("d_sqk"), at("d_sqk", 1))
            v.tensor_tensor(v3(VR), v3(ps[4][:]), over_tokens(TK[:, 24:28]), ALU.mult).then_inc(S("d_la"), 1)
            dve.wait_ge(S("d_eg"), at("d_eg", 1))
            v.tensor_tensor(v3(QD), KQv[:, :, 1, :], v3(EG), ALU.mult).then_inc(S("d_la"), 1)
            for l in range(1, 7):
                dve.wait_ge(S("d_px"), at("d_px", l))
                v.tensor_tensor(v3(XB), v3(ps[4][:]), level(l), ALU.mult).then_inc(S("d_x"), 1)
                dve.wait_ge(S("d_pt"), at("d_pt", l))
                if l < 6:
                    v.tensor_tensor(TB, TB, ps[5][:], ALU.subtract).then_inc(S("d_t"), 1)
                v.tensor_tensor(TTB, TTB, ps[6][:], ALU.subtract).then_inc(S("d_tt"), 1)
            for c in range(NCH):
                dve.wait_ge(S("d_pv"), at("d_pv", c + 1))
                v.tensor_copy(VN[c % 2], chunk(ps[3], c % 2)).then_inc(S("d_vn"), 1)
                if c < NCH - 1:
                    dve.wait_ge(S("d_ps"), at("d_ps", c + 1))
                    if c == 0:
                        v.tensor_copy(ST[1], chunk(ps[6], 0)).then_inc(S("d_s"), 1)
                    else:
                        dve.wait_ge(S("d_s"), at("d_s", c))
                        v.scalar_tensor_tensor(out=ST[(c + 1) % 2], in0=ST[c % 2], scalar=head_col(EGL, h, c),
                                                   in1=chunk(ps[6], c % 2), op0=ALU.mult, op1=ALU.add).then_inc(S("d_s"), 1)
            v.tensor_scalar(TK[:, 4:8], TK[:, 8:12], EPS * P, None, ALU.mult).then_inc(S("d_oms"), 1)
            dve.wait_ge(S("d_oms"), at("d_oms", 1))
            dve.wait_ge(S("d_os"), at("d_os", 1))
            v.scalar_tensor_tensor(out=TK[:, 12:16], in0=ps[2][:, 8:12], scalar=1.0 / P, in1=TK[:, 4:8],
                                       op0=ALU.mult, op1=ALU.add).then_inc(S("d_oms"), 1)
            v.scalar_tensor_tensor(out=AC[0], in0=ps[5][:], scalar=par_col("onorm"), in1=GT,
                                       op0=ALU.mult, op1=ALU.mult).then_inc(S("d_o1"), 1)
            dve.wait_ge(S("d_o1"), at("d_o1", 1))
            dve.wait_ge(S("d_ro"), at("d_ro", 1))
            dve.wait_ge(S("o_lo"), at("o_lo", 0))
            v.tensor_tensor(O2, AC[0], ps[7][:], ALU.mult).then_inc(S("d_o2"), 1)

        def delta_pool(pool, h):
            at = head_count(h)
            pool.wait_ge(S("d_s1"), at("d_s1", 1))
            nc.gpsimd.tensor_tensor(TK[:, 24:28], TK[:, 4:8], mhalf[:, 4:8], ALU.pow).then_inc(S("d_sqk"), 1)
            pool.wait_ge(S("d_oms"), at("d_oms", 2))
            nc.gpsimd.tensor_tensor(TK[:, 28:32], TK[:, 12:16], mhalf[:, 0:4], ALU.pow).then_inc(S("d_orow"), 1)
            pool.wait_ge(S("o_hi"), at("o_hi", 1))
            nc.gpsimd.tensor_tensor(tile(pairB[1], h), O2, tile(pairB[0], h).bitcast(F32), ALU.subtract).then_inc(S("o_lo"), 1)

        def evacuate(dve, r, k, out, scalar, in1, op1=ALU.mult, op0=ALU.mult):
            evac_wait(dve, r, k)
            return nc.vector.scalar_tensor_tensor(out=out, in0=ps[k % 2][:], scalar=scalar, in1=in1,
                                                  op0=op0, op1=op1).then_inc(S(f"evac{k}"), 1)

        def residual_pe(pe, base, pair, wait, n=KT):
            for i in range(2):
                for s in range(SLOTS):
                    unit(pe, rnd(base, i), s, pair, n, wait=wait if i + s == 0 else None)

        def residual_act(act, base, tag, g, pair, end=False):
            for i in range(2):
                for k in range(SLOTS):
                    m, r = 4 * i + k, rnd(base, i)
                    if not (end and m >= KT - LEAD):
                        ahead(act, split_hi, r, k)
                    act.wait_ge(S(f"evac{k}"), count(f"evac{k}", r + 1))
                    if g:
                        nc.scalar.activation(tile(pair[0], m), tile(X, m), ACT.Copy, scale=par_col(g, m)).then_inc(S(tag + "_hi"), 1)
                    square(act, tag, m, tile(X, m))

        def residual_dve(dve, base, tag, g, pair, bias=None, end=False):
            for i in range(2):
                for k in range(SLOTS):
                    m, r = 4 * i + k, rnd(base, i)
                    if not (end and m >= KT - LEAD):
                        ahead(dve, split_lo, r, k)
                    evacuate(dve, r, k, tile(X, m), par_col(bias, m) if bias else 0.0, tile(X, m), ALU.add, ALU.add)
                    if g and m:
                        norm_lo(dve, tag, g, pair, m - 1)
            if g:
                norm_lo(dve, tag, g, pair, KT - 1)

        FU = [AU[0][:, 0:T + FPAD], AU[1][:, 0:T + FPAD]]
        FC = AC
        FT = AT[0]
        PR = [KQ[:, 0:T], KQ[:, T:2 * T]]

        def ffn_bases(base):
            first = 0
            for n in MID_GROUPS:
                yield base, base + 2 * n, first, n
                base, first = base + 2 * n + 8, first + n

        def hidden_rounds(eng, base, first, n, one_round):
            start = 0
            if first == 0:
                one_round(0, True)
                start = 1
            with eng.Fori(start, n // 2) as i:
                one_round(i, False)

        def ffn_pe(pe, L, base, inpair, mid, ntag, end=False):
            t = f"f{L}"
            for up, down, first, n in ffn_bases(base):
                def one_round(i, begin):
                    for s in range(SLOTS):
                        unit(pe, rnd(up, i), s, inpair, wait=pair_wait(ntag)(pe) if begin and s == 0 else None)
                        if begin and s == 0:
                            norm_pe(pe, ntag)
                hidden_rounds(pe, up, first, n, one_round)

                def wait_mid(k):
                    pe.wait_ge(S(t + "_hi"), count(t + "_hi", first + k + 1))
                    pe.wait_ge(S(t + "_lo"), count(t + "_lo", first + k + 1))
                residual_pe(pe, down, mid, wait_mid, n)

        def ffn_act(act, L, base, mid, ntag, next_tag, next_g, next_pair, end=False):
            t = f"f{L}"
            for up, down, first, n in ffn_bases(base):
                def one_round(i, begin):
                    for k in range(SLOTS):
                        r = rnd(up, i)
                        ahead(act, split_hi, r, k)
                        if begin and k == 0:
                            norm_row(act, ntag)
                            act.wait_ge(S(t + "_half"), count(t + "_half", 2))
                        q, side = first + 2 * i + k // 2, k % 2
                        act.wait_ge(S(f"evac{k}"), count(f"evac{k}", r + 1))
                        if not begin or k > 1:
                            act.wait_ge(S(t + "_prod"), count(t + "_prod", q))
                        if side == 0:
                            w3, b = half[:, bass.ds(104 + q * 3 + 2, 1)], half[:, bass.ds(170 + q, 1)]
                        else:
                            w3, b = par_col(f"f_conv{L}", (22 + q) * 3 + 2), par_col(f"f_bias{L}", 22 + q)
                        nc.scalar.activation(FC[side], FU[side][:, FPAD:FPAD + T], ACT.Identity, scale=w3, bias=b).then_inc(S(t + "_c0"), 1)
                        if side == 0:
                            act.wait_ge(S(t + "_tap"), count(t + "_tap", 4 * q + 2))
                            nc.scalar.activation(FT, FC[0], ACT.Tanh).then_inc(S(t + "_th"), 1)
                        else:
                            act.wait_ge(S(t + "_prod"), count(t + "_prod", q + 1))
                            nc.scalar.activation(tile(mid[0], 2 * i + k // 2), PR[k // 2], ACT.Copy).then_inc(S(t + "_hi"), 1)
                hidden_rounds(act, up, first, n, one_round)
                if first + n < 22:
                    with act.Fori(0, 2) as i:
                        for k in range(SLOTS):
                            ahead(act, split_hi, rnd(down, i), k)
                else:
                    residual_act(act, down, next_tag, next_g, next_pair, end)

        def ffn_dve(dve, L, base, mid, ntag, next_tag, next_g, next_pair, end=False):
            t = f"f{L}"
            v = nc.vector
            c, b = _cols[f"f_conv{L}"][0], _cols[f"f_bias{L}"][0]
            v.tensor_scalar(half[:, 104:170], par[:, c:c + 66], 0.5, None, ALU.mult).then_inc(S(t + "_half"), 1)
            v.tensor_scalar(half[:, 170:192], par[:, b:b + 22], 0.5, None, ALU.mult).then_inc(S(t + "_half"), 1)
            dve.wait_ge(S(t + "_half"), count(t + "_half", 2))
            for u in FU:
                v.memset(u[:, 0:FPAD], 0.0).then_inc(S(t + "_pad"), 1)
            token_mean(dve, ntag, 2, D)
            for up, down, first, n in ffn_bases(base):
                def one_round(i, begin):
                    for k in range(SLOTS):
                        r = rnd(up, i)
                        ahead(dve, split_lo, r, k)
                        if begin and k == 0:
                            dve.wait_ge(S(ntag + "_R"), count(ntag + "_R", 1))
                            dve.wait_ge(S(t + "_pad"), count(t + "_pad", 2))
                        q, side = first + 2 * i + k // 2, k % 2
                        evacuate(dve, r, k, FU[side][:, FPAD:FPAD + T], 1.0, R[:])
                        dve.wait_ge(S(t + "_c0"), count(t + "_c0", 2 * q + side + 1))
                        for n_, tap in enumerate((1, 0)):
                            w = half[:, bass.ds(104 + q * 3 + tap, 1)] if side == 0 else \
                                par_col(f"f_conv{L}", (22 + q) * 3 + tap)
                            if n_:
                                dve.wait_ge(S(t + "_tap"), count(t + "_tap", 4 * q + 2 * side + 1))
                            v.scalar_tensor_tensor(out=FC[side], in0=FU[side][:, tap:tap + T], scalar=w,
                                                       in1=FC[side], op0=ALU.mult, op1=ALU.add).then_inc(S(t + "_tap"), 1)
                        if side == 0:
                            continue
                        dve.wait_ge(S(t + "_th"), count(t + "_th", q + 1))
                        v.scalar_tensor_tensor(out=FC[0], in0=FT, scalar=1.0, in1=FC[0], op0=ALU.add,
                                                   op1=ALU.mult).then_inc(S(t + "_gate"), 1)
                        dve.wait_ge(S(t + "_gate"), count(t + "_gate", q + 1))
                        dve.wait_ge(S(t + "_tap"), count(t + "_tap", 4 * q + 4))
                        if not begin:
                            dve.wait_ge(S(t + "_lo"), count(t + "_lo", q - 1))
                        v.tensor_tensor(PR[k // 2], FC[0], FC[1], ALU.mult).then_inc(S(t + "_prod"), 1)
                hidden_rounds(dve, up, first, n, one_round)
                if first + n < 22:
                    with dve.Fori(0, 2) as i:
                        for k in range(SLOTS):
                            r = rnd(down, i)
                            ahead(dve, split_lo, r, k)
                            evacuate(dve, r, k, tile(X, 4 * i + k), 0.0, tile(X, 4 * i + k), ALU.add, ALU.add)
                else:
                    residual_dve(dve, down, next_tag, next_g, next_pair, end=end)

        def ffn_pool(pool, L, base, mid):
            t = f"f{L}"
            for up, down, first, n in ffn_bases(base):
                with pool.Fori(0, n // 2) as i:
                    for j in range(2):
                        pool.wait_ge(S(t + "_hi"), count(t + "_hi", first + 2 * i + j + 1))
                        nc.gpsimd.tensor_tensor(tile(mid[1], 2 * i + j), PR[j],
                                                    tile(mid[0], 2 * i + j).bitcast(F32), ALU.subtract).then_inc(S(t + "_lo"), 1)

        o = 0
        KA = [carve(T) for _ in range(2)]
        VF = carve(T)
        VA_T = [carve(T) for _ in range(2)]
        QT = [carve(T) for _ in range(2)]
        AW = carve(T)
        SC = [carve(2 * T) for _ in range(2)]
        PT = [carve(2 * T) for _ in range(2)]
        MX = carve(64)
        DD = carve(T)
        APER = dict(q_t=1, q_w=1, s_p=4, s_sc=4, s_mx=4, s_e=10, s_n=8, s_tr=4, s_pt=4, s_o=1, t_hi=1, t_lo=1)

        def sc3(e):
            return SC[e].rearrange("p (b s) -> p b s", b=NCH)

        def tile_count(t):
            def at(name, k):
                return count(name, t * APER[name] + k)
            return at

        def half_rows(ap, e):
            return ap[64 * e:64 * e + 64, :]

        def att_scores_pe(pe, t, a, qb):
            at = tile_count(t)
            pe.wait_ge(S("q_t"), at("q_t", 1))
            for e in range(2):
                for pairno in range(2):
                    bank = 2 + 2 * e + pairno
                    for b in (2 * pairno, 2 * pairno + 1):
                        lo = max(b - 1, 0) * P
                        n = P if b == 0 else 2 * P
                        out = ps[bank][:, (b % 2) * 256 + 256 - n:(b % 2) * 256 + 256]
                        last = pe.matmul(out, half_rows(QT[qb], e)[:, b * P:(b + 1) * P],
                                         half_rows(KA[a], e)[:, lo:lo + n], start=True, stop=True)
                    last.then_inc(S("s_p"), 1)

        def att_out_pe(pe, t, a):
            at = tile_count(t)
            for e in range(2):
                pe.wait_ge(S("s_n"), at("s_n", 4 * e + 4))
                for pairno in range(2):
                    for b in (2 * pairno, 2 * pairno + 1):
                        for j in range(2):
                            if b == 0 and j == 0:
                                continue
                            last = pe.transpose(ps[2 + 2 * e + pairno][:, (b % 2) * 256 + j * P:(b % 2) * 256 + (j + 1) * P],
                                                SC[e][:, b * 256 + j * P:b * 256 + (j + 1) * P], ident)
                    last.then_inc(S("s_tr"), 1)
            pe.wait_ge(S("t_lo"), at("t_lo", 0))
            for e in range(2):
                for b in range(NCH):
                    if b % 2 == 0:
                        pe.wait_ge(S("s_pt"), at("s_pt", 2 * e + b // 2 + 1))
                    for j in range(2):
                        if b == 0 and j == 0:
                            continue
                        last = pe.matmul(ps[6][64 * e:64 * e + 64, b * P:(b + 1) * P],
                                         VA_T[a][:, (b - 1 + j) * P + 64 * e:(b - 1 + j) * P + 64 * e + 64],
                                         PT[e][:, b * 256 + j * P:b * 256 + (j + 1) * P],
                                         start=j == 0 or b == 0, stop=j == 1)
            last.then_inc(S("s_o"), 1)

        def attention_pe(pe):
            for s in range(SLOTS):
                unit(pe, rnd(U_KV, 0), s, pairA, wait=pair_wait("kv")(pe) if s == 0 else None)
                if s == 0:
                    norm_pe(pe, "kv")
            for m in range(2):
                pe.wait_ge(S("v_f"), count("v_f", m + 1))
                if m:
                    pe.wait_ge(S("v_t"), count("v_t", m))
                for c in range(NCH):
                    last = pe.transpose(chunk(ps[4], c), chunk(VF, c), ident)
                last.then_inc(S("v_tr"), 1)

            pe.wait_ge(S("v_t"), count("v_t", 2))
            pe.wait_ge(S("bn_lo"), count("bn_lo", 8))
            with pe.Fori(0, 2) as i:
                r = rnd(U_Q, i)
                unit(pe, r, 0, pairB)
                for k in range(SLOTS):
                    t = 4 * i + k
                    att_scores_pe(pe, t, k % 2, k % 2)
                    if k < 3:
                        unit(pe, r, k + 1, pairB)
                    att_out_pe(pe, t, k % 2)

            def wait_o(k):
                pe.wait_ge(S("t_hi"), count("t_hi", k + 1))
                pe.wait_ge(S("t_lo"), count("t_lo", k + 1))
            residual_pe(pe, U_BO, pairA, wait_o)

        def attention_act(act):
            a = nc.scalar
            for k in range(SLOTS):
                ahead(act, split_hi, rnd(U_KV, 0), k)
                if k == 0:
                    norm_row(act, "kv")
                for m in (2 * k, 2 * k + 1):
                    a.activation(tile(pairB[0], m), tile(X, m), ACT.Copy, scale=par_col("b_norm", m)).then_inc(S("bn_hi"), 1)
            for m in range(2):
                act.wait_ge(S("v_tr"), count("v_tr", m + 1))
                a.activation(VA_T[m], ps[4][:], ACT.Copy).then_inc(S("v_t"), 1)
            with act.Fori(0, 2) as i:
                for k in range(SLOTS):
                    t = 4 * i + k
                    at = tile_count(t)
                    ahead(act, split_hi, rnd(U_Q, i), k)
                    for e in range(2):
                        act.wait_ge(S("s_mx"), at("s_mx", 2 * e + 2))
                        den = MX[:, 8 * e:8 * e + 8]
                        neg = MX[:, 16 + 4 * e:20 + 4 * e]
                        a.activation(MX[:, 24 + 4 * e:28 + 4 * e], neg, ACT.Exp,
                                         bias=rowp[:, bass.ds(16 + 2 * t + e, 1)]).then_inc(S("s_e"), 1)
                        for b in range(NCH):
                            sc = SC[e][:, b * 256 + (0 if b else P):(b + 1) * 256]
                            a.activation(sc, sc, ACT.Exp, bias=neg[:, b:b + 1],
                                             accum_out=den[:, b:b + 1]).then_inc(S("s_e"), 1)
                    for e in range(2):
                        for pairno in range(2):
                            act.wait_ge(S("s_tr"), at("s_tr", 2 * e + pairno + 1))
                            lo = P if pairno == 0 else 0
                            a.activation(PT[e][:, pairno * T + lo:(pairno + 1) * T],
                                             ps[2 + 2 * e + pairno][:, lo:T], ACT.Copy).then_inc(S("s_pt"), 1)
                    act.wait_ge(S("s_o"), at("s_o", 1))
                    a.activation(tile(pairA[0], t), ps[6][:], ACT.Copy).then_inc(S("t_hi"), 1)
            residual_act(act, U_BO, "n_f1", "f_norm1", pairB)

        def attention_dve(dve):
            v = nc.vector
            token_mean(dve, "kv", 2, D)
            for e in range(2):
                v.memset(SC[e][:, 0:P], -FAR).then_inc(S("sc_far"), 1)
                v.tensor_copy(DD[:, e * 256:(e + 1) * 256], cst[:, C_DIST:C_DIST + 256]).then_inc(S("sc_far"), 1)
            dve.wait_ge(S("sc_far"), count("sc_far", 4))
            for k in range(SLOTS):
                r = rnd(U_KV, 0)
                ahead(dve, split_lo, r, k)
                if k == 0:
                    dve.wait_ge(S("kv_R"), count("kv_R", 1))
                evacuate(dve, r, k, AW, 1.0, R[:])
                dve.wait_ge(S(f"evac{k}"), count(f"evac{k}", r + 1))
                if k > 2:
                    dve.wait_ge(S("v_tr"), count("v_tr", k - 2))
                v.tensor_scalar(KA[k] if k < 2 else VF, AW, par_col("kv_b", k), None, ALU.add).then_inc(S("k_f" if k < 2 else "v_f"), 1)
                for m in (2 * k, 2 * k + 1):
                    norm_lo(dve, "bn", "b_norm", pairB, m)
                dve.wait_ge(S("k_f" if k < 2 else "v_f"), count("k_f" if k < 2 else "v_f", k % 2 + 1))

            def q_tile(i, k):
                r = rnd(U_Q, i)
                if k:
                    dve.wait_ge(S("q_t"), count("q_t", 4 * i + k))
                evacuate(dve, r, k, AW, 1.0, R[:])
                dve.wait_ge(S(f"evac{k}"), count(f"evac{k}", r + 1))
                v.tensor_scalar(QT[k % 2], AW, par_col("b_q", 4 * i + k), 0.125, ALU.add, ALU.mult).then_inc(S("q_t"), 1)
            with dve.Fori(0, 2) as i:
                q_tile(i, 0)
                for k in range(SLOTS):
                    t = 4 * i + k
                    at = tile_count(t)
                    for e in range(2):
                        nslope = rowp[:, bass.ds(32 + 2 * t + e, 1)]
                        for pairno in range(2):
                            dve.wait_ge(S("s_p"), at("s_p", 2 * e + pairno + 1))
                            lo = P if pairno == 0 else 0
                            v.scalar_tensor_tensor(out=SC[e][:, pairno * T + lo:(pairno + 1) * T],
                                                       in0=DD[:, lo:T], scalar=nslope,
                                                       in1=ps[2 + 2 * e + pairno][:, lo:T],
                                                       op0=ALU.mult, op1=ALU.add).then_inc(S("s_sc"), 1)
                        if e == 0:
                            ahead(dve, split_lo, rnd(U_Q, i), k)
                        dve.wait_ge(S("s_sc"), at("s_sc", 2 * e + 2))
                        mx = MX[:, 32 + 4 * e:36 + 4 * e]
                        v.tensor_reduce(mx, sc3(e), mybir.AxisListType.X, ALU.max).then_inc(S("s_mx"), 1)
                        dve.wait_ge(S("s_mx"), at("s_mx", 2 * e + 1))
                        v.tensor_scalar(MX[:, 16 + 4 * e:20 + 4 * e], mx, rowp[:, bass.ds(16 + 2 * t + e, 1)],
                                            -1.0, ALU.max, ALU.mult).then_inc(S("s_mx"), 1)
                    if k < 3:
                        q_tile(i, k + 1)
                    for e in range(2):
                        dve.wait_ge(S("s_e"), at("s_e", 5 * e + 5))
                        den = MX[:, 40 + 4 * e:44 + 4 * e]
                        v.tensor_tensor(den, MX[:, 8 * e:8 * e + 4], MX[:, 24 + 4 * e:28 + 4 * e], ALU.add).then_inc(S("s_n"), 1)
                        dve.wait_ge(S("s_n"), at("s_n", 4 * e + 1))
                        v.reciprocal(MX[:, 52 + 4 * e:56 + 4 * e], den).then_inc(S("s_n"), 1)
                        dve.wait_ge(S("s_n"), at("s_n", 4 * e + 2))
                        v.tensor_scalar(SC[e][:, P:2 * P], SC[e][:, P:2 * P], MX[:, 52 + 4 * e:53 + 4 * e], None,
                                            ALU.mult).then_inc(S("s_n"), 1)
                        v.tensor_tensor(sc3(e)[:, 1:NCH], sc3(e)[:, 1:NCH], MX[:, 53 + 4 * e:56 + 4 * e]
                                            .unsqueeze(2).broadcast_to([P, NCH - 1, 256]), ALU.mult).then_inc(S("s_n"), 1)
                    dve.wait_ge(S("t_hi"), at("t_hi", 1))
                    v.tensor_tensor(tile(pairA[1], t), ps[6][:], tile(pairA[0], t).bitcast(F32), ALU.subtract).then_inc(S("t_lo"), 1)
            residual_dve(dve, U_BO, "n_f1", "f_norm1", pairB, bias="b_o")

        def second_block_pe(pe):
            pe.wait_ge(S("row_in"), count("row_in", 32))
            pe.wait_ge(S("na_lo"), count("na_lo", KT))
            for c in range(NCH):
                for k in range(KT):
                    for part in range(2):
                        cols = tile(pairA[part], k)[:, c * P:(c + 1) * P].bitcast(F32)
                        last = pe.matmul(ps[6][:, c * 16:(c + 1) * 16], cols, tailw[:, k * 16:(k + 1) * 16],
                                         start=k + part == 0, stop=k == KT - 1 and part == 1)
            last.then_inc(S("tail"), 1)
            norm_pe(pe, "na")
            pe.wait_ge(S("g_tok"), count("g_tok", 1))
            pe.matmul(ps[6][:, 64:64 + HC], tri, G, start=True, stop=True)
            pe.matmul(ps[6][:, 128:128 + HC], ones[:], G, start=True, stop=True).then_inc(S("g_sum"), 1)
            pe.wait_ge(S("g_done"), count("g_done", 4))
            pe.wait_ge(S("ekd_sub"), count("ekd_sub", 1))
            with pe.Fori(0, HEADS) as h:
                for s in range(SLOTS):
                    unit(pe, rnd(U_DELTA, h), s, pairA)
                delta_pe(pe, h)

            def wait_o(k):
                pe.wait_ge(S("o_hi"), count("o_hi", k + 1))
                pe.wait_ge(S("o_lo"), count("o_lo", k + 1))
            residual_pe(pe, U_AOUT, pairB, wait_o)
            ffn_pe(pe, 0, U_FFN0, pairA, pairB, "nf0")
            attention_pe(pe)
            ffn_pe(pe, 1, U_FFN1, pairB, pairA, "n_f1", end=True)
            norm_pe(pe, "fin", bank=4)

        def second_block_act(act):
            a = nc.scalar
            norm_act(act, "na", "a_norm", pairA, lambda e, m: e.wait_ge(S("x2"), count("x2", m + 1)))
            norm_row(act, "na")
            act.wait_ge(S("row_in"), count("row_in", 32))
            a.activation(NEA, rowp[:, 0:8], ACT.Exp).then_inc(S("g_act"), 1)
            act.wait_ge(S("g_z"), count("g_z", 1))
            a.activation(Z2, Z1, ACT.Exp, scale=-1.0).then_inc(S("g_act"), 1)
            a.activation(BETA, BETA, ACT.Tanh, scale=0.5).then_inc(S("g_act"), 1)
            act.wait_ge(S("g_act"), count("g_act", 2))
            a.activation(Z2, Z2, ACT.Ln, bias=1.0).then_inc(S("g_act"), 1)
            act.wait_ge(S("g_sum"), count("g_sum", 1))
            a.activation(EGC, ps[6][:, 64:64 + HC], ACT.Exp).then_inc(S("g_done"), 1)
            a.activation(EGL, ps[6][:, 128:128 + HC], ACT.Exp).then_inc(S("g_done"), 1)
            a.activation(NGC, ps[6][:, 64:64 + HC], ACT.Copy, scale=-1.0).then_inc(S("g_done"), 1)
            act.wait_ge(S("ekd_sub"), count("ekd_sub", 1))
            a.activation(EKD, EKD, ACT.Exp).then_inc(S("g_done"), 1)
            with act.Fori(0, HEADS) as h:
                delta_act(act, h)
            residual_act(act, U_AOUT, "nf0", "f_norm0", pairA)
            ffn_act(act, 0, U_FFN0, pairB, "nf0", "kv", "kv_norm", pairA)
            attention_act(act)
            ffn_act(act, 1, U_FFN1, pairA, "n_f1", "fin", None, None, end=True)

        def second_block_dve(dve):
            v = nc.vector
            for m in range(KT):
                dve.wait_ge(S("x2"), count("x2", m + 1))
                norm_lo(dve, "na", "a_norm", pairA, m)
            token_mean(dve, "na", 2, D)
            for u in AU:
                v.memset(u[:, 0:APAD], 0.0).then_inc(S("a_pad"), 1)
            dve.wait_ge(S("na_rt"), count("na_rt", 1))
            dve.wait_ge(S("tail"), count("tail", 1))
            for c in range(NCH):
                v.tensor_scalar(BA[:, c * 16:(c + 1) * 16], ps[6][:, c * 16:(c + 1) * 16],
                                    tok[:, NCH + c:NCH + c + 1], None, ALU.mult).then_inc(S("g_v"), 1)
            dve.wait_ge(S("g_v"), count("g_v", 4))
            dve.wait_ge(S("row_in"), count("row_in", 32))

            def hc(ap):
                return ap.rearrange("p (h c) -> p h c", c=NCH)
            v.tensor_copy(hc(BETA), BAv[:, 0:8, :]).then_inc(S("g_v"), 1)
            v.tensor_tensor(hc(G), BAv[:, 8:16, :], rowp[:, 8:16].unsqueeze(2).broadcast_to([P, HEADS, NCH]),
                                ALU.add).then_inc(S("g_v"), 1)
            dve.wait_ge(S("g_v"), count("g_v", 6))
            v.scalar_tensor_tensor(out=Z1, in0=G, scalar=-1.0, in1=G, op0=ALU.mult, op1=ALU.max).then_inc(S("g_z"), 1)
            dve.wait_ge(S("g_act"), count("g_act", 4))
            v.scalar_tensor_tensor(out=Z1, in0=G, scalar=0.0, in1=Z2, op0=ALU.max, op1=ALU.add).then_inc(S("g_v"), 1)
            v.tensor_scalar(BETA, BETA, 0.5, 0.5, ALU.mult, ALU.add).then_inc(S("g_v"), 1)
            dve.wait_ge(S("g_v"), count("g_v", 8))
            v.tensor_tensor(hc(Z2), hc(Z1), NEA.unsqueeze(2).broadcast_to([P, HEADS, NCH]), ALU.mult).then_inc(S("g_v"), 1)
            dve.wait_ge(S("g_v"), count("g_v", 9))
            v.tensor_scalar(G, Z2, -1.0, None, ALU.mult).then_inc(S("g_tok"), 1)
            dve.wait_ge(S("g_sum"), count("g_sum", 1))
            dve.wait_ge(S("g_done"), count("g_done", 3))
            v.tensor_tensor(EKD, ps[6][:, 128:128 + HC], NGC, ALU.add).then_inc(S("ekd_sub"), 1)
            dve.wait_ge(S("g_done"), count("g_done", 4))
            dve.wait_ge(S("na_R"), count("na_R", 1))
            dve.wait_ge(S("a_pad"), count("a_pad", 2))
            with dve.Fori(0, HEADS) as h:
                delta_dve(dve, h)
            residual_dve(dve, U_AOUT, "nf0", "f_norm0", pairA)
            ffn_dve(dve, 0, U_FFN0, pairB, "nf0", "kv", "kv_norm", pairA)
            attention_dve(dve)
            ffn_dve(dve, 1, U_FFN1, pairA, "n_f1", "fin", None, None, end=True)
            token_mean(dve, "fin", 4, D)
            dve.wait_ge(S("fin_row"), count("fin_row", 1))
            dve.wait_ge(S("fin_sq"), count("fin_sq", 8))
            for m in range(KT):
                v.scalar_tensor_tensor(out=tile(X, m), in0=tile(X, m), scalar=par_col("final", m), in1=ps[5][:],
                                           op0=ALU.mult, op1=ALU.mult).then_inc(S("final"), 1)

        def second_block_pool(pool):
            sum_squares(pool, "na", KT)
            token_rsqrt(pool, "na")
            with pool.Fori(0, HEADS) as h:
                delta_pool(pool, h)
            sum_squares(pool, "nf0", KT)
            token_rsqrt(pool, "nf0")
            ffn_pool(pool, 0, U_FFN0, pairB)
            sum_squares(pool, "kv", KT)
            token_rsqrt(pool, "kv")
            sum_squares(pool, "n_f1", KT)
            token_rsqrt(pool, "n_f1")
            ffn_pool(pool, 1, U_FFN1, pairA)
            sum_squares(pool, "fin", KT)
            token_rsqrt(pool, "fin")

        @block.sync
        def _(sp):
            sp.dma_start(X[:], io["xT"]).then_inc(S("x_in"), 16)
            sp.dma_start(par[:], io["par"]).then_inc(S("par_in"), 16)
            for s in range(SLOTS):
                sp.dma_start(raw[:, s * 1024:(s + 1) * 1024], io["ws"][s]).then_inc(S(f"raw_in{s}"), 16)
                if s == 0:
                    sp.dma_start(cst[:], io["cst"]).then_inc(S("cst_in"), 16)
                    sp.dma_start(rowp, io["row"].broadcast_to([P, 48])).then_inc(S("row_in"), 16)
                    sp.dma_start(tailw, io["tail"]).then_inc(S("row_in"), 16)
                    sp.dma_start(pwraw, io["pw"]).then_inc(S("pw_in"), 16)
            with sp.Fori(1, U_END // SLOTS) as r:
                for s in range(SLOTS):
                    sp.wait_ge(S(f"w_lo{s}"), count(f"w_lo{s}", r))
                    sp.dma_start(raw[:, s * 1024:(s + 1) * 1024],
                                 io["ws"][bass.ds(r * SLOTS + s, 1)].rearrange("a p n -> p (a n)"))\
                        .then_inc(S(f"raw_in{s}"), 16)
            sp.wait_ge(S("final"), count("final", KT))
            sp.dma_start(io["out"], X[:]).then_inc(S("out"), 16)
            sp.wait_ge(S("out"), 16)

        @block.tensor
        def _(pe):
            credit(pe, *(f"unit_done{s}" for s in range(SLOTS)))
            pe.wait_ge(S("const"), count("const", 2))
            pe.wait_ge(S("cst_in"), count("cst_in", 16))

            def glu_round(i, first):
                for s in range(SLOTS):
                    begin = first and s == 0
                    unit(pe, rnd(U_GLU, i), s, pairA, wait=pair_wait("n0")(pe) if begin else None)
                    if begin:
                        norm_pe(pe, "n0")
            glu_round(0, True)
            glu_round(1, False)
            for s in range(SLOTS):
                unit(pe, rnd(U_POOL, 0), s, pairA)
            with pe.Fori(0, 4) as i:
                for s in range(SLOTS):
                    unit(pe, rnd(U_GATE, i), s, pairA)
            pe.wait_ge(S("pw_hi"), count("pw_hi", 1))
            pe.wait_ge(S("pw_lo"), count("pw_lo", 1))
            for g in range(4):
                pe.wait_ge(S("pooled_lo"), count("pooled_lo", g + 1))
                if g > 1:
                    pe.wait_ge(S("mixed_lo"), count("mixed_lo", g - 1))
                c = slice(g * P, (g + 1) * P)
                hi, lo = tile(pairB[0], g), tile(pairB[1], g)
                b = 4 + g % 2
                pe.matmul(ps[b][:], pw[0][:, c], hi, start=True, stop=False)
                pe.matmul(ps[b][:], pw[0][:, c], lo, start=False, stop=False)
                pe.matmul(ps[b][:], pw[1][:, c], hi, start=False, stop=True).then_inc(S("mix_done"), 1)
            for j in range(4):
                pe.wait_ge(S("conv_out"), count("conv_out", j + 1))
                last = pe.matmul(ps[6][:], ones[:], tile(CV, j), start=j == 0, stop=j == 3)
            last.then_inc(S("ln_mean"), 1)
            norm_pe(pe, "ln", 4)
            for i in range(2):
                for s in range(SLOTS):
                    unit_wait(pe, rnd(U_BRANCH, i), s)
                    if i + s == 0:
                        pe.wait_ge(S("mixed_lo"), count("mixed_lo", 4))
                        pe.wait_ge(S("cv_scaled"), count("cv_scaled", 4))
                    blocks(pe, s % 2, s, pairB, 4, 4, 0)
                    blocks(pe, 2 + s % 2, s, pairB, 0, 4, 4, wait=pair_wait("ln")(pe) if i + s == 0 else None)\
                        .then_inc(S(f"unit_done{s}"), 1)
            for i in range(2):
                for s in range(SLOTS):
                    unit(pe, rnd(U_WO, i), s, pairA, wait=pair_wait("br")(pe) if i + s == 0 else None)
            norm_pe(pe, "post0", bank=4)
            def mlp_group(g, first):
                for i in range(2):
                    for s in range(SLOTS):
                        begin = first and i + s == 0
                        unit(pe, rnd(U_MLP, g * 4 + i), s, pairA, wait=pair_wait("n1")(pe) if begin else None)
                        if begin:
                            norm_pe(pe, "n1")
                for i in range(2):
                    for s in range(SLOTS):
                        def wait_mid(k):
                            pe.wait_ge(S("mlp_hi"), count("mlp_hi", g * 8 + k + 1))
                            pe.wait_ge(S("mlp_lo"), count("mlp_lo", g * 8 + k + 1))
                        unit(pe, rnd(U_MLP, g * 4 + 2 + i), s, pairB, wait=wait_mid if i + s == 0 else None)
            mlp_group(0, True)
            with pe.Fori(1, 3) as g:
                mlp_group(g, False)
            mlp_group(3, False)
            norm_pe(pe, "post1", bank=4)
            second_block_pe(pe)

        @block.scalar
        def _(act):
            act.wait_ge(S("par_in"), count("par_in", 16))
            norm_act(act, "n0", "mix_pre", pairA, x_loaded)
            split_hi(act, 0, 0)
            split_hi(act, 0, 1)
            act.wait_ge(S("pw_in"), count("pw_in", 16))
            nc.scalar.activation(pw[0][:], pwraw, ACT.Copy).then_inc(S("pw_hi"), 1)

            def glu_round(i, first):
                for k in range(SLOTS):
                    ahead(act, split_hi, rnd(U_GLU, i), k)
                    if first and k == 0:
                        norm_row(act, "n0")
                    if k % 2:
                        act.wait_ge(S(f"evac{k}"), count(f"evac{k}", rnd(U_GLU, i) + 1))
                        nc.scalar.activation(TH, TG[:, 0:T], ACT.Tanh, scale=0.5).then_inc(S("glu_th"), 1)
            glu_round(0, True)
            glu_round(1, False)
            for k in range(SLOTS):
                ahead(act, split_hi, rnd(U_POOL, 0), k)
            act.wait_ge(S("glu_v"), count("glu_v", 4))

            def conv_tap(j, t):
                act.wait_ge(S("conv_acc"), count("conv_acc", j * (ACC_TAPS - 1) + (max(1, t - 2) if t >= 2 else 0)))
                nc.scalar.activation(CTMP[:, (t % 2) * T:(t % 2 + 1) * T], VP[:, bass.ds(j * VPW + t, T)],
                                     ACT.Copy, scale=par_col("conv_w", j * CONV_K + t)).then_inc(S("conv_tmp"), 1)

            def gate_round(i):
                for k in range(SLOTS):
                    ahead(act, split_hi, rnd(U_GATE, i), k)
                    for t in (2 * k, 2 * k + 1):
                        conv_tap(i, t)
                    act.wait_ge(S(f"evac{k}"), count(f"evac{k}", rnd(U_GATE, i) + 1))
                    nc.scalar.activation(SG[:, bass.ds((4 * i + k) * T, T)], TG[:, (k % 2) * T:(k % 2 + 1) * T],
                                         ACT.Tanh, scale=0.5).then_inc(S("gate_th"), 1)
            with act.Fori(0, 2) as i:
                gate_round(i)
            for g in range(4):
                act.wait_ge(S("pooled"), count("pooled", g + 1))
                nc.scalar.activation(tile(pairB[0], g), PO[g], ACT.Copy).then_inc(S("pooled_hi"), 1)
            act.wait_ge(S("pooled_lo"), count("pooled_lo", 4))
            with act.Fori(2, 4) as i:
                gate_round(i)
            for g in range(4):
                act.wait_ge(S("mix_done"), count("mix_done", g + 1))
                nc.scalar.activation(tile(pairB[0], 4 + g), ps[4 + g % 2][:], ACT.Copy,
                                     scale=par_col("pool_scale", g)).then_inc(S("mixed_hi"), 1)
            for j in range(4):
                act.wait_ge(S("cv_centred"), count("cv_centred", j + 1))
                square(act, "ln", j, tile(CV, j))
            for j in range(4):
                act.wait_ge(S("cv_scaled"), count("cv_scaled", j + 1))
                if j > 1:
                    act.wait_ge(S("ln_z"), count("ln_z", j - 1))
                nc.scalar.activation(TG[:, (j % 2) * T:(j % 2 + 1) * T], tile(CV, j), ACT.Identity,
                                     scale=half[:, j:j + 1], bias=half[:, 4 + j:5 + j]).then_inc(S("ln_y"), 1)
                act.wait_ge(S("ln_y"), count("ln_y", j + 1))
                nc.scalar.activation([VA, TH][j % 2], TG[:, (j % 2) * T:(j % 2 + 1) * T], ACT.Tanh)\
                    .then_inc(S("ln_th"), 1)
                act.wait_ge(S("ln_z"), count("ln_z", j + 1))
                nc.scalar.activation(tile(pairB[0], j), tile(CV, j), ACT.Copy).then_inc(S("ln_hi"), 1)
            act.wait_ge(S("ln_lo"), count("ln_lo", 4))
            act.dma_start(X[:], io["xT"]).then_inc(S("x_back"), 16)
            for i in range(2):
                for k in range(SLOTS):
                    ahead(act, split_hi, rnd(U_BRANCH, i), k)
                    m = 4 * i + k
                    act.wait_ge(S("br_sum"), count("br_sum", m + 1))
                    nc.scalar.activation(tile(pairA[0], m), CTMP[:, (k % 2) * T:(k % 2 + 1) * T], ACT.Copy)\
                        .then_inc(S("br_hi"), 1)
            act.wait_ge(S("br_lo"), count("br_lo", 8))
            for i in range(2):
                for k in range(SLOTS):
                    m = 4 * i + k
                    ahead(act, split_hi, rnd(U_WO, i), k)
                    evac_wait(act, rnd(U_WO, i), k)
                    nc.scalar.activation(tile(Y, m), ps[k % 2][:], ACT.Copy, scale=0.5).then_inc(S(f"evac{k}"), 1)
                    act.wait_ge(S(f"evac{k}"), count(f"evac{k}", rnd(U_WO, i) + 1))
                    square(act, "post0", m, tile(Y, m))
            norm_act(act, "n1", "mlp_pre", pairA, lambda e, m: e.wait_ge(S("x1"), count("x1", m + 1)))

            def mlp_group(g, first, last):
                for i in range(2):
                    for k in range(SLOTS):
                        r = rnd(U_MLP, g * 4 + i)
                        ahead(act, split_hi, r, k)
                        if first and i + k == 0:
                            norm_row(act, "n1")
                        n = g * 8 + 4 * i + k
                        evac_wait(act, r, k)
                        act.wait_ge(S("mlp_sq"), count("mlp_sq", n - 1))
                        nc.scalar.activation(TG[:, (k % 2) * T:(k % 2 + 1) * T], ps[k % 2][:], ACT.Relu)\
                            .then_inc(S(f"evac{k}"), 1)
                        act.wait_ge(S("mlp_sq"), count("mlp_sq", n + 1))
                        nc.scalar.activation(tile(pairB[0], 4 * i + k), MS[:, (k % 2) * T:(k % 2 + 1) * T], ACT.Copy)\
                            .then_inc(S("mlp_hi"), 1)
                for i in range(2):
                    for k in range(SLOTS):
                        ahead(act, split_hi, rnd(U_MLP, g * 4 + 2 + i), k)
                        if last:
                            act.wait_ge(S(f"evac{k}"), count(f"evac{k}", rnd(U_MLP, g * 4 + 2 + i) + 1))
                            square(act, "post1", 4 * i + k, tile(Y, 4 * i + k))
            mlp_group(0, True, False)
            with act.Fori(1, 3) as g:
                mlp_group(g, False, False)
            mlp_group(3, False, True)
            second_block_act(act)

        @block.vector
        def _(dve):
            v = nc.vector
            credit(dve, *(f"evac{s}" for s in range(SLOTS)))
            credit(dve, "mlp_sq", "conv_out", "t_lo")
            v.memset(ones[:], 1.0).then_inc(S("const"), 1)
            v.memset(mhalf[:, 0:NCH], -0.5)
            v.memset(mhalf[:, NCH:2 * NCH], 0.5).then_inc(S("const"), 1)
            v.memset(VP, 0.0).then_inc(S("zeros"), 1)
            dve.wait_ge(S("par_in"), count("par_in", 16))

            def par_range(name, n):
                return par[:, _cols[name][0]:_cols[name][0] + n]
            for at, name, n in ((0, "ln_g", 4), (4, "ln_b", 4), (8, "a_conv", 96)):
                v.tensor_scalar(half[:, at:at + n], par_range(name, n), 0.5, None, ALU.mult).then_inc(S("halved"), 1)
            dve.wait_ge(S("x_in"), count("x_in", 16))
            for m in range(KT):
                norm_lo(dve, "n0", "mix_pre", pairA, m)
            split_lo(dve, 0, 0)
            split_lo(dve, 0, 1)
            dve.wait_ge(S("pw_hi"), count("pw_hi", 1))
            v.tensor_tensor(pw[1][:], pwraw, pw[0][:].bitcast(F32), ALU.subtract).then_inc(S("pw_lo"), 1)
            token_mean(dve, "n0", 2, D)

            def glu_round(i, first):
                for k in range(SLOTS):
                    r = rnd(U_GLU, i)
                    ahead(dve, split_lo, r, k)
                    n = 2 * i + k // 2
                    if k % 2 == 0:
                        if first and k == 0:
                            dve.wait_ge(S("n0_R"), count("n0_R", 1))
                            dve.wait_ge(S("zeros"), count("zeros", 1))
                        evacuate(dve, r, k, VA, 0.5, R[:])
                    else:
                        evacuate(dve, r, k, TG[:, 0:T], 1.0, R[:])
                        dve.wait_ge(S("glu_th"), count("glu_th", n + 1))
                        at = n * VPW + CONV_K - 1
                        v.scalar_tensor_tensor(out=VP[:, at:at + T], in0=TH, scalar=1.0, in1=VA,
                                               op0=ALU.add, op1=ALU.mult).then_inc(S("glu_v"), 1)
                        dve.wait_ge(S("glu_v"), count("glu_v", n + 1))
            glu_round(0, True)
            glu_round(1, False)
            for u in UP:
                v.memset(u[:, 0:16], 0.0).then_inc(S("zeros"), 1)
            for k in range(SLOTS):
                r = rnd(U_POOL, 0)
                ahead(dve, split_lo, r, k)
                if k > 1:
                    dve.wait_ge(S("pooled"), count("pooled", k - 1))
                evacuate(dve, r, k, UP[k % 2][:, 16:UPW], 1.0, R[:])

            def gate_round(i):
                for k in range(SLOTS):
                    r = rnd(U_GATE, i)
                    ahead(dve, split_lo, r, k)
                    dve.wait_ge(S("gate_th"), count("gate_th", 4 * i + k - 1))
                    evacuate(dve, r, k, TG[:, (k % 2) * T:(k % 2 + 1) * T], 1.0, R[:])
                    for t in range(ACC_TAPS + (k * 23 + 3) // 4, ACC_TAPS + ((k + 1) * 23 + 3) // 4):
                        if t >= CONV_K:
                            continue
                        x = VP[:, bass.ds(i * VPW + t, T)]
                        w = par_col("conv_w", i * CONV_K + t)
                        n = i * 23 + t - ACC_TAPS
                        if t == ACC_TAPS:
                            v.tensor_scalar(tile(CV, i), x, w, par_col("conv_b", i), ALU.mult, ALU.add)\
                                .then_inc(S("conv_step"), 1)
                        else:
                            dve.wait_ge(S("conv_step"), count("conv_step", n))
                            v.scalar_tensor_tensor(out=tile(CV, i), in0=x, scalar=w, in1=tile(CV, i),
                                                   op0=ALU.mult, op1=ALU.add).then_inc(S("conv_step"), 1)
                dve.wait_ge(S("conv_step"), count("conv_step", 23 * (i + 1)))
                dve.wait_ge(S("conv_acc"), count("conv_acc", (ACC_TAPS - 1) * (i + 1)))
                v.tensor_tensor(tile(CV, i), tile(CV, i), CVB, ALU.add).then_inc(S("conv_out"), 1)
            with dve.Fori(0, 4) as i:
                gate_round(i)
            for g in range(4):
                dve.wait_ge(S("mixed_hi"), count("mixed_hi", g + 1))
                v.scalar_tensor_tensor(out=tile(pairB[1], 4 + g), in0=ps[4 + g % 2][:], scalar=par_col("pool_scale", g),
                                       in1=tile(pairB[0], 4 + g).bitcast(F32), op0=ALU.mult, op1=ALU.subtract)\
                    .then_inc(S("mixed_lo"), 1)
            dve.wait_ge(S("ln_mean"), count("ln_mean", 1))
            for j in range(4):
                v.scalar_tensor_tensor(out=tile(CV, j), in0=ps[6][:], scalar=-1.0 / (4 * P), in1=tile(CV, j),
                                       op0=ALU.mult, op1=ALU.add).then_inc(S("cv_centred"), 1)
            token_mean(dve, "ln", 2, 4 * P)
            dve.wait_ge(S("ln_row"), count("ln_row", 1))
            for j in range(4):
                dve.wait_ge(S("ln_sq"), count("ln_sq", j + 1))
                v.tensor_tensor(tile(CV, j), tile(CV, j), ps[3][:], ALU.mult).then_inc(S("cv_scaled"), 1)
            for j in range(4):
                dve.wait_ge(S("ln_th"), count("ln_th", j + 1))
                v.scalar_tensor_tensor(out=tile(CV, j), in0=[VA, TH][j % 2], scalar=1.0,
                                       in1=TG[:, (j % 2) * T:(j % 2 + 1) * T], op0=ALU.add, op1=ALU.mult)\
                    .then_inc(S("ln_z"), 1)
                dve.wait_ge(S("ln_hi"), count("ln_hi", j + 1))
                v.tensor_tensor(tile(pairB[1], j), tile(CV, j), tile(pairB[0], j).bitcast(F32), ALU.subtract)\
                    .then_inc(S("ln_lo"), 1)
            for i in range(2):
                for k in range(SLOTS):
                    r = rnd(U_BRANCH, i)
                    m = 4 * i + k
                    ahead(dve, split_lo, r, k)
                    evac_wait(dve, r, k)
                    if m > 1:
                        dve.wait_ge(S("br_lo"), count("br_lo", m - 1))
                    half_sum = CTMP[:, (k % 2) * T:(k % 2 + 1) * T]
                    v.scalar_tensor_tensor(out=half_sum, in0=tile(SG, m), scalar=1.0, in1=ps[k % 2][:],
                                           op0=ALU.add, op1=ALU.mult).then_inc(S("br_part"), 1)
                    v.scalar_tensor_tensor(out=VA, in0=tile(SG, 8 + m), scalar=1.0, in1=ps[2 + k % 2][:],
                                           op0=ALU.add, op1=ALU.mult).then_inc(S(f"evac{k}"), 1)
                    dve.wait_ge(S("br_part"), count("br_part", m + 1))
                    dve.wait_ge(S(f"evac{k}"), count(f"evac{k}", r + 1))
                    v.tensor_tensor(half_sum, half_sum, VA, ALU.add).then_inc(S("br_sum"), 1)
                    dve.wait_ge(S("br_sum"), count("br_sum", m + 1))
            for i in range(2):
                for k in range(SLOTS):
                    ahead(dve, split_lo, rnd(U_WO, i), k)

            def add_normed(tag, xtag, g, bank):
                dve.wait_ge(S(tag + "_row"), count(tag + "_row", 1))
                for m in range(KT):
                    t = TG[:, (m % 2) * T:(m % 2 + 1) * T]
                    if m > 1:
                        dve.wait_ge(S(xtag), count(xtag, m - 1))
                    v.scalar_tensor_tensor(out=t, in0=tile(Y, m), scalar=par_col(g, m), in1=ps[bank][:],
                                           op0=ALU.mult, op1=ALU.mult).then_inc(S(tag + "_t"), 1)
                    dve.wait_ge(S(tag + "_t"), count(tag + "_t", m + 1))
                    v.tensor_tensor(tile(X, m), tile(X, m), t, ALU.add).then_inc(S(xtag), 1)
            dve.wait_ge(S("post0_ss"), count("post0_ss", 8))
            token_mean(dve, "post0", 4, D)
            dve.wait_ge(S("x_back"), count("x_back", 16))
            add_normed("post0", "x1", "mix_post", 5)
            for m in range(KT):
                dve.wait_ge(S("x1"), count("x1", m + 1))
                norm_lo(dve, "n1", "mlp_pre", pairA, m)
            token_mean(dve, "n1", 2, D)

            def mlp_group(g, first):
                for i in range(2):
                    for k in range(SLOTS):
                        ahead(dve, split_lo, rnd(U_MLP, g * 4 + i), k)
                        n = g * 8 + 4 * i + k
                        dve.wait_ge(S(f"evac{k}"), count(f"evac{k}", rnd(U_MLP, g * 4 + i) + 1))
                        t = TG[:, (k % 2) * T:(k % 2 + 1) * T]
                        if not (first and 4 * i + k < 2):
                            dve.wait_ge(S("mlp_lo"), count("mlp_lo", n - 1))
                        v.tensor_tensor(MS[:, (k % 2) * T:(k % 2 + 1) * T], t, t, ALU.mult).then_inc(S("mlp_sq"), 1)
                for i in range(2):
                    for k in range(SLOTS):
                        r = rnd(U_MLP, g * 4 + 2 + i)
                        m = 4 * i + k
                        ahead(dve, split_lo, r, k)
                        evac_wait(dve, r, k)
                        if first:
                            v.tensor_copy(tile(Y, m), ps[k % 2][:]).then_inc(S(f"evac{k}"), 1)
                        else:
                            v.tensor_tensor(tile(Y, m), ps[k % 2][:], tile(Y, m), ALU.add).then_inc(S(f"evac{k}"), 1)
            mlp_group(0, True)
            with dve.Fori(1, 3) as g:
                mlp_group(g, False)
            mlp_group(3, False)
            r1, r2, r4 = tok[:, NCH:2 * NCH], tok[:, 8:12], tok[:, 12:16]
            v.tensor_tensor(r2, r1, r1, ALU.mult).then_inc(S("r_power"), 1)
            dve.wait_ge(S("r_power"), count("r_power", 1))
            v.tensor_tensor(r4, r2, r2, ALU.mult).then_inc(S("r_power"), 1)
            dve.wait_ge(S("r_power"), count("r_power", 2))
            dve.wait_ge(S("post1_sum"), count("post1_sum", 1))
            v.scalar_tensor_tensor(out=tok[:, 16:20], in0=ps[4][:, 0:NCH], scalar=1.0 / D, in1=r4,
                                   op0=ALU.mult, op1=ALU.mult).then_inc(S("r_power"), 1)
            dve.wait_ge(S("r_power"), count("r_power", 3))
            v.tensor_scalar(tok[:, 0:NCH], tok[:, 16:20], EPS, None, ALU.add).then_inc(S("post1_ms"), 1)
            add_normed("post1", "x2", "mlp_post", 5)
            second_block_dve(dve)

        @block.gpsimd
        def _(pool):
            g_ = nc.gpsimd
            credit(pool, "conv_acc", "o_lo")
            pool.sem_inc(S("gate_th"), CREDIT["gate_th"])
            pool.wait_ge(S("const"), count("const", 2))
            pool.wait_ge(S("cst_in"), count("cst_in", 16))
            sum_squares(pool, "n0", KT)
            token_rsqrt(pool, "n0")
            step = 0
            for g, window in enumerate(POOL_WINDOWS):
                u = UP[g % 2]
                pool.wait_ge(S(f"evac{g}"), count(f"evac{g}", rnd(U_POOL, 0) + 1))
                pool.wait_ge(S("zeros"), count("zeros", 3))
                src, shift = u, 1
                while shift < window:
                    dst = PAB[step % 2]
                    lo = 2 * shift - 1
                    if step:
                        pool.wait_ge(S("pool_step"), count("pool_step", step))
                    g_.tensor_tensor(dst[:, lo:UPW], src[:, lo:UPW], src[:, lo - shift:UPW - shift], ALU.add)\
                        .then_inc(S("pool_step"), 1)
                    step += 1
                    src, shift = dst, 2 * shift
                pool.wait_ge(S("pool_step"), count("pool_step", step))
                dst = PAB[step % 2]
                g_.tensor_scalar(dst[:, 16:UPW], src[:, 16:UPW], 1.0 / window, 0.0, ALU.mult, ALU.add)\
                    .then_inc(S("pool_step"), 1)
                step += 1
                pool.wait_ge(S("pool_step"), count("pool_step", step))
                inv = cst[:, C_INV + 16 * g:C_INV + 16 * (g + 1)]
                g_.tensor_tensor(dst[:, 16:32], src[:, 16:32], inv, ALU.mult).then_inc(S("pool_step"), 1)
                step += 1
                pool.wait_ge(S("pool_step"), count("pool_step", step))
                g_.tensor_tensor(PO[g], dst[:, 16:UPW], u[:, 16:UPW], ALU.subtract).then_inc(S("pooled"), 1)
                pool.wait_ge(S("pooled"), count("pooled", g + 1))

            def conv_sum(i):
                for t in range(1, ACC_TAPS):
                    pool.wait_ge(S("conv_tmp"), count("conv_tmp", ACC_TAPS * i + t + 1))
                    tmp = CTMP[:, (t % 2) * T:(t % 2 + 1) * T]
                    if t == 1:
                        pool.wait_ge(S("conv_out"), count("conv_out", i))
                    else:
                        pool.wait_ge(S("conv_acc"), count("conv_acc", (ACC_TAPS - 1) * i + t - 1))
                    g_.tensor_tensor(CVB, CTMP[:, 0:T] if t == 1 else CVB, tmp, ALU.add).then_inc(S("conv_acc"), 1)
            with pool.Fori(0, 2) as i:
                conv_sum(i)
            for g in range(4):
                pool.wait_ge(S("pooled_hi"), count("pooled_hi", g + 1))
                g_.tensor_tensor(tile(pairB[1], g), PO[g], tile(pairB[0], g).bitcast(F32), ALU.subtract)\
                    .then_inc(S("pooled_lo"), 1)
            with pool.Fori(2, 4) as i:
                conv_sum(i)
            sum_squares(pool, "ln", 4)
            token_rsqrt(pool, "ln")

            def lo_part(tag, m, src, dst, ready=None):
                pool.wait_ge(S(tag + "_hi"), count(tag + "_hi", ready if ready is not None else m + 1))
                g_.tensor_tensor(tile(dst[1], m), src, tile(dst[0], m).bitcast(F32), ALU.subtract)\
                    .then_inc(S(tag + "_lo"), 1)
            for m in range(8):
                lo_part("br", m, CTMP[:, (m % 2) * T:(m % 2 + 1) * T], pairA)
            sum_squares(pool, "post0", KT)
            token_rsqrt(pool, "post0")
            sum_squares(pool, "n1", KT)
            token_rsqrt(pool, "n1")
            with pool.Fori(0, 4) as g:
                for m in range(8):
                    lo_part("mlp", m, MS[:, (m % 2) * T:(m % 2 + 1) * T], pairB, g * 8 + m + 1)
            sum_squares(pool, "post1", KT)
            pool.wait_ge(S("post1_ms"), count("post1_ms", 1))
            g_.tensor_tensor(tok[:, 20:24], tok[:, 0:NCH], mhalf[:, 0:NCH], ALU.pow).then_inc(S("post1_pow"), 1)
            pool.wait_ge(S("post1_pow"), count("post1_pow", 1))
            g_.tensor_tensor(tok[:, NCH:2 * NCH], tok[:, 20:24], tok[:, 8:12], ALU.mult).then_inc(S("post1_rt"), 1)
            second_block_pool(pool)


def _blocks(w, k0, n, m):
    b = w[k0 * P:(k0 + n) * P, m * P:(m + 1) * P].reshape(n, P, P)
    return b.transpose(1, 0, 2).reshape(P, n * P)


def _pack(inp):
    f = np.float32
    ws = np.zeros((U_END, P, 1024), f)
    at = [0]

    def put(*parts):
        a = np.concatenate(parts, axis=1)
        ws[at[0], :, :a.shape[1]] = a
        at[0] += 1
    w_in = inp["w_in"][0]
    for j in range(4):
        put(_blocks(w_in, 0, 8, 4 + j))
        put(_blocks(w_in, 0, 8, 8 + j))
    for j in range(4):
        put(_blocks(w_in, 0, 8, j))
    for j in range(16):
        put(_blocks(w_in, 0, 8, 12 + j))
    for m in range(8):
        put(_blocks(inp["w_pool_out"][0], 0, 4, m), _blocks(inp["w_conv_out"][0], 0, 4, m))
    for m in range(8):
        put(_blocks(inp["w_o"][0], 0, 8, m))
    for g in range(4):
        for m in range(8):
            put(_blocks(inp["w_up"][0], 0, 8, 8 * g + m))
        for m in range(8):
            put(_blocks(inp["w_down"][0], 8 * g, 8, m))
    a_in = inp["a_w_in_2"][0]
    for h in range(HEADS):
        for part in range(4):
            put(_blocks(a_in, 0, 8, 8 * part + h))
    for m in range(8):
        put(_blocks(inp["a_w_out_2"][0], 0, 8, m))

    def ffn(layer):
        up, down = inp["f_w_up_2"][layer], inp["f_w_down_2"][layer]
        first = 0
        for n in MID_GROUPS:
            for m in range(first, first + n):
                put(_blocks(up, 0, 8, m))
                put(_blocks(up, 0, 8, 22 + m))
            for m in range(8):
                put(_blocks(down, first, n, m))
            first += n
    ffn(0)
    for m in range(4):
        put(_blocks(inp["kv_w_2"], 0, 8, m))
    heads = [h for pair in ATT_TILE_HEADS for h in pair]
    by_head = lambda w, axis: np.concatenate(
        [np.take(w, range(64 * h, 64 * h + 64), axis=axis) for h in heads], axis=axis)
    wq = by_head(inp["b_w_q_2"][0], 1)
    for m in range(8):
        put(_blocks(wq, 0, 8, m))
    wo = by_head(inp["b_w_o_2"][0], 0)
    for m in range(8):
        put(_blocks(wo, 0, 8, m))
    ffn(1)
    assert at[0] == U_END, at

    par = np.zeros((P, NPAR), f)

    def col(name, vec):
        c, n = _cols[name]
        par[:, c:c + n] = np.asarray(vec).reshape(n, P).T
    for name, key in (("mix_pre", "norm_mix_pre"), ("mix_post", "norm_mix_post"), ("mlp_pre", "norm_mlp_pre"),
                      ("mlp_post", "norm_mlp_post"), ("a_norm", "a_norm_2"), ("kv_norm", "kv_norm_2"),
                      ("b_norm", "b_norm_2"), ("final", "final_norm_2"), ("pool_scale", "pool_scale"),
                      ("conv_b", "conv_b"), ("ln_g", "conv_ln_g"), ("ln_b", "conv_ln_b"), ("onorm", "a_onorm_2"),
                      ("kv_b", "kv_b_2"), ("b_o", "b_b_o_2")):
        col(name, inp[key])
    col("b_q", by_head(inp["b_b_q_2"][0], 0))
    for layer in range(2):
        col(f"f_norm{layer}", inp["f_norm_2"][layer])
        col(f"f_bias{layer}", inp["f_conv_b_2"][layer])

    def taps(name, w):
        c, n = _cols[name]
        par[:, c:c + n] = w.reshape(w.shape[0], -1, P).transpose(2, 1, 0).reshape(P, n)
    taps("conv_w", inp["conv_w"][0])
    taps("a_conv", inp["a_conv_w_2"][0])
    taps("f_conv0", inp["f_conv_w_2"][0])
    taps("f_conv1", inp["f_conv_w_2"][1])

    cst = np.zeros((P, NCONST), f)
    i, j = np.arange(P)[:, None], np.arange(P)[None, :]
    cst[:, C_ID:C_ID + P] = i == j
    cst[:, C_TRI:C_TRI + P] = i <= j
    cst[:, C_NEG:C_NEG + P] = np.where(j >= i, 0, -FAR)
    for lvl in range(7):
        m = (i >> (lvl + 1) == j >> (lvl + 1)) & ((i >> lvl) & 1 == 1) & ((j >> lvl) & 1 == 0)
        cst[:, C_LVL + lvl * P:C_LVL + (lvl + 1) * P] = m.T if lvl == 0 else m
    dist = i + P - np.arange(2 * P)[None, :]
    cst[:, C_DIST:C_DIST + 2 * P] = np.where((dist >= 0) & (dist < P), dist, FAR)
    for g, window in enumerate(POOL_WINDOWS):
        cst[:, C_INV + 16 * g:C_INV + 16 * g + 16] = 1.0 / np.minimum(np.arange(16) + 1, window)
    slopes = (2.0 ** (-8.0 * np.arange(1, 17) / 16)).astype(f)
    row = np.concatenate([inp["a_A_log_2"][0], inp["a_dt_bias_2"][0], inp["b_sinks_2"][0][heads], -slopes[heads]])
    return {
        "xT": np.asarray(inp["x"])[0].T.reshape(KT, P, T).transpose(1, 0, 2).reshape(P, KT * T),
        "ws": ws, "par": par, "cst": cst,
        "pw": np.asarray(inp["pool_w"])[0].transpose(1, 0, 2).reshape(P, 4 * P),
        "tail": a_in[:, 4 * D:].reshape(KT, P, 16).transpose(1, 0, 2).reshape(P, KT * 16),
        "row": row.reshape(1, 48),
    }


def kernel(**inputs):
    import concourse.bacc as bacc
    from concourse.bass_utils import run_bass_kernel_spmd

    packed = {k: np.ascontiguousarray(v) for k, v in _pack({k: np.asarray(v) for k, v in inputs.items()}).items()}
    nc = bacc.Bacc("TRN2", target_bir_lowering=False, num_devices=1)
    io = {k: nc.dram_tensor("d_" + k, v.shape, F32, kind="ExternalInput").ap() for k, v in packed.items()}
    io["out"] = nc.dram_tensor("d_out", (P, KT * T), F32, kind="ExternalOutput").ap()
    build(nc, io)
    r = run_bass_kernel_spmd(nc, [{"d_" + k: v for k, v in packed.items()}], core_ids=[0])
    out = r.results[0]["d_out"]
    return out.reshape(P, KT, T).transpose(2, 1, 0).reshape(1, T, D)
```

```python
from contextlib import ExitStack

import numpy as np

import concourse.bass as bass
from concourse import mybir
from concourse.alu_op_type import AluOpType as ALU

ACT = mybir.ActivationFunctionType
F32 = mybir.dt.float32
F32R = mybir.dt.float32r

P = 128
T = 512
NCH = T // P
D = 1024
KT = D // P
EPS = 1e-6
CONV_K = 31
FPAD = 2
APAD = 3
HEADS = 8
SLOTS = 4
LEAD = 2
ACC_TAPS = 8

U_GLU = 0
U_POOL = U_GLU + 8
U_GATE = U_POOL + 4
U_BRANCH = U_GATE + 16
U_WO = U_BRANCH + 8
U_MLP = U_WO + 8
U_DELTA = U_MLP + 64
U_AOUT = U_DELTA + 32
U_FFN0 = U_AOUT + 8
MID_GROUPS = (8, 8, 6)
U_KV = U_FFN0 + sum(2 * g + 8 for g in MID_GROUPS)
U_Q = U_KV + 4
U_BO = U_Q + 8
U_FFN1 = U_BO + 8
U_END = U_FFN1 + sum(2 * g + 8 for g in MID_GROUPS)

_cols = {}
_n = 0
for _name, _width in (
    ("mix_pre", KT), ("mix_post", KT), ("mlp_pre", KT), ("mlp_post", KT), ("a_norm", KT), ("kv_norm", KT),
    ("b_norm", KT), ("f_norm0", KT), ("f_norm1", KT), ("final", KT),
    ("pool_scale", 4), ("conv_w", 4 * CONV_K), ("conv_b", 4), ("ln_g", 4), ("ln_b", 4),
    ("a_conv", 24 * 4), ("onorm", 1), ("b_q", 8), ("kv_b", 4), ("b_o", 8),
    ("f_conv0", 44 * 3), ("f_bias0", 44), ("f_conv1", 44 * 3), ("f_bias1", 44),
):
    _cols[_name] = (_n, _width)
    _n += _width
NPAR = _n

C_ID = 0
C_TRI = C_ID + P
C_NEG = C_TRI + P
C_LVL = C_NEG + P
C_DIST = C_LVL + 7 * P
C_INV = C_DIST + 2 * P
NCONST = C_INV + 4 * 16
POOL_WINDOWS = (2, 4, 8, 16)
FAR = 1e30
ATT_TILE_HEADS = [(4 * (2 * a) + r, 4 * (2 * a + 1) + r) for r in range(4) for a in range(2)]


def build(nc, io):
    with ExitStack() as ctx:
        def sb(name, cols, dt=F32):
            return ctx.enter_context(nc.sbuf_tensor(name, [P, cols], dt))

        sems = {}

        NORMS = {}
        count = {"one": 0, "ss": 0, "hi": 0}
        for tag, squared, split in (("n0", 8, 8), ("ln", 4, 4), ("post0", 8, 0), ("n1", 8, 8), ("post1", 8, 0),
                                    ("na", 8, 8), ("nf0", 8, 8), ("kv", 8, 8), ("bn", 0, 8), ("n_f1", 8, 8),
                                    ("fin", 8, 0)):
            NORMS[tag] = dict(count)
            NORMS[tag]["R"] = count.get("R", 0)
            count["one"] += squared > 0
            count["ss"] += squared
            count["hi"] += split
            count["R"] = NORMS[tag]["R"] + (tag in ("n0", "n1", "na", "nf0", "kv", "n_f1"))
        KINDS = {"hi": "hi", "lo": "hi", "sq": "ss", "ss": "ss", "sum": "one", "ms": "one", "rt": "one", "row": "one",
                 "R": "R"}
        FFN_STEPS = dict(half=2, pad=2, c0=44, tap=88, th=22, gate=22, prod=22, hi=22, lo=22)

        def shared(name):
            tag, _, kind = name.rpartition("_")
            if tag in NORMS and kind in KINDS:
                return "norm_" + kind, NORMS[tag][KINDS[kind]]
            if tag in ("f0", "f1") and kind in FFN_STEPS:
                return "ffn_" + kind, FFN_STEPS[kind] if tag == "f1" else 0
            return name, 0

        def S(name):
            name = shared(name)[0]
            if name not in sems:
                sems[name] = ctx.enter_context(nc.semaphore(name))
            return sems[name]

        X = sb("X", KT * T)
        pairA = (sb("A_hi", KT * T, F32R), sb("A_lo", KT * T, F32R))
        pairB = (sb("B_hi", KT * T, F32R), sb("B_lo", KT * T, F32R))
        Y = sb("Y", KT * T)
        raw = sb("w_raw", SLOTS * 1024)
        w_hi = sb("w_hi", SLOTS * 1024, F32R)
        w_lo = sb("w_lo", SLOTS * 1024, F32R)
        par = sb("par", NPAR)
        half = sb("half", 8 + 96 + 22 * 3 + 22)
        cst = sb("cst", NCONST)
        ones = sb("ones", P)
        mhalf = sb("mhalf", 2 * NCH)
        R = sb("R", T)
        SQ = sb("SQ", 2 * T)
        SS = sb("SS", T)
        tok = sb("tok", 64)
        NSCR = 10260
        scr = sb("scr", NSCR)
        small = sb("small", 48 + KT * 16)
        rowp, tailw = small[:, 0:48], small[:, 48:48 + KT * 16]
        pw = (sb("pw_hi", 512, F32R), sb("pw_lo", 512, F32R))
        ps = [ctx.enter_context(nc.psum_tensor(f"ps{b}", [P, 512], F32)) for b in range(8)]

        def par_col(name, k=0):
            c = _cols[name][0] + k
            return par[:, c:c + 1] if isinstance(c, int) else par[:, bass.ds(c, 1)]

        def tile(buf, m, n=1):
            return buf[:, m * T:(m + n) * T] if isinstance(m, int) else buf[:, bass.ds(m * T, n * T)]

        ident = cst[:, C_ID:C_ID + P]
        tri = cst[:, C_TRI:C_TRI + P]

        o = 0

        def carve(n):
            nonlocal o
            o += n
            assert o <= NSCR, (o, NSCR)
            return scr[:, o - n:o]

        SG = carve(16 * T)
        UPW = T + 16
        VATH = carve(2 * T)
        VA, TH = VATH[:, 0:T], VATH[:, T:2 * T]
        TG = carve(2 * T)
        UP = [X[:, 4 * T + 2 * UPW:4 * T + 3 * UPW], VATH[:, 0:UPW]]
        pwraw = SG[:, 0:512]
        PO = [SG[:, (8 + g) * T:(9 + g) * T] for g in range(4)]
        VPW = T + CONV_K - 1
        VP = Y[:, 0:4 * VPW]
        CVB = Y[:, 4 * VPW:4 * VPW + T]
        CTMP = Y[:, 4 * VPW + T:4 * VPW + 3 * T]
        CV = X[:, 0:4 * T]
        PAB = [X[:, 4 * T:4 * T + UPW], X[:, 4 * T + UPW:4 * T + 2 * UPW]]
        MS = SG[:, 0:2 * T]
        assert 4 * VPW + 3 * T <= KT * T

        block = ctx.enter_context(nc.Block())

        CREDIT = {"o_lo": 1, "t_lo": 1, "d_o1": 1, "d_o2": 1, "d_os": 1}
        for s in range(SLOTS):
            CREDIT[f"unit_done{s}"] = 1
            CREDIT[f"evac{s}"] = 1
        for name in ("mlp_sq", "conv_acc", "conv_out", "gate_th"):
            CREDIT[name] = 4

        def count(name, n):
            return n + CREDIT.get(name, 0) + shared(name)[1]

        def credit(eng, *names):
            for name in names:
                eng.sem_inc(S(name), CREDIT[name])

        def rnd(base, i):
            assert base % SLOTS == 0
            return base // SLOTS + i

        def split_hi(act, r, s):
            act.wait_ge(S(f"raw_in{s}"), 16 * (r + 1))
            act.wait_ge(S(f"unit_done{s}"), count(f"unit_done{s}", r))
            c = slice(s * 1024, (s + 1) * 1024)
            nc.scalar.activation(w_hi[:, c], raw[:, c], ACT.Copy).then_inc(S(f"w_hi{s}"), 1)

        def split_lo(dve, r, s):
            dve.wait_ge(S(f"w_hi{s}"), count(f"w_hi{s}", r + 1))
            c = slice(s * 1024, (s + 1) * 1024)
            nc.vector.tensor_tensor(w_lo[:, c], raw[:, c], w_hi[:, c].bitcast(F32), ALU.subtract)\
                .then_inc(S(f"w_lo{s}"), 1)

        def ahead(eng, split, r, k):
            split(eng, r + (k + LEAD) // SLOTS, (k + LEAD) % SLOTS)

        def unit_wait(pe, r, s):
            pe.wait_ge(S(f"w_hi{s}"), count(f"w_hi{s}", r + 1))
            pe.wait_ge(S(f"w_lo{s}"), count(f"w_lo{s}", r + 1))
            pe.wait_ge(S(f"evac{(s + 2) % SLOTS}"), count(f"evac{(s + 2) % SLOTS}", r + 1 if s >= 2 else r))

        def blocks(pe, bank, s, pair, first, n, at=0, wait=None):
            for k in range(n):
                if wait:
                    wait(k)
                c = slice(s * 1024 + (at + k) * P, s * 1024 + (at + k + 1) * P)
                hi, lo = tile(pair[0], first + k), tile(pair[1], first + k)
                pe.matmul(ps[bank][:], w_hi[:, c], hi, start=k == 0, stop=False)
                pe.matmul(ps[bank][:], w_hi[:, c], lo, start=False, stop=False)
                last = pe.matmul(ps[bank][:], w_lo[:, c], hi, start=False, stop=k == n - 1)
            return last

        def part_blocks(pe, bank, s, pair, first, n):
            for k in range(first, first + n):
                c = slice(s * 1024 + k * P, s * 1024 + (k + 1) * P)
                hi, lo = tile(pair[0], k), tile(pair[1], k)
                pe.matmul(ps[bank][:], w_hi[:, c], hi, start=k == 0, stop=False)
                pe.matmul(ps[bank][:], w_hi[:, c], lo, start=False, stop=False)
                last = pe.matmul(ps[bank][:], w_lo[:, c], hi, start=False, stop=k == KT - 1)
            return last

        def unit(pe, r, s, pair, n=KT, wait=None):
            unit_wait(pe, r, s)
            blocks(pe, s % 2, s, pair, 0, n, wait=wait).then_inc(S(f"unit_done{s}"), 1)

        def evac_wait(eng, r, s):
            eng.wait_ge(S(f"unit_done{s}"), count(f"unit_done{s}", r + 1))

        def norm_act(act, tag, g, pair, xready, squares=True):
            for m in range(KT):
                xready(act, m)
                nc.scalar.activation(tile(pair[0], m), tile(X, m), ACT.Copy, scale=par_col(g, m))\
                    .then_inc(S(tag + "_hi"), 1)
                if squares:
                    square(act, tag, m, tile(X, m))

        def square(act, tag, m, src, scale=1.0):
            if m > 1:
                act.wait_ge(S(tag + "_ss"), count(tag + "_ss", m - 1))
            nc.scalar.activation(tile(SQ, m % 2), src, ACT.Square, scale=scale).then_inc(S(tag + "_sq"), 1)

        def norm_lo(dve, tag, g, pair, m):
            dve.wait_ge(S(tag + "_hi"), count(tag + "_hi", m + 1))
            nc.vector.scalar_tensor_tensor(out=tile(pair[1], m), in0=tile(X, m), scalar=par_col(g, m),
                                           in1=tile(pair[0], m).bitcast(F32), op0=ALU.mult, op1=ALU.subtract)\
                .then_inc(S(tag + "_lo"), 1)

        def sum_squares(pool, tag, n):
            for m in range(n):
                pool.wait_ge(S(tag + "_sq"), count(tag + "_sq", m + 1))
                if m == 0:
                    nc.gpsimd.tensor_copy(SS[:], tile(SQ, 0)).then_inc(S(tag + "_ss"), 1)
                else:
                    pool.wait_ge(S(tag + "_ss"), count(tag + "_ss", m))
                    nc.gpsimd.tensor_tensor(SS[:], SS[:], tile(SQ, m % 2), ALU.add).then_inc(S(tag + "_ss"), 1)

        def token_sums(pe, tag, n, bank):
            pe.wait_ge(S(tag + "_ss"), count(tag + "_ss", n))
            for c in range(NCH):
                last = pe.matmul(ps[bank][:, c:c + 1], SS[:, c * P:(c + 1) * P], ones[:, 0:1], start=True, stop=True)
            last.then_inc(S(tag + "_sum"), 1)

        def token_mean(dve, tag, bank, n):
            dve.wait_ge(S(tag + "_sum"), count(tag + "_sum", 1))
            nc.vector.tensor_scalar(tok[:, 0:NCH], ps[bank][:, 0:NCH], 1.0 / n, EPS, ALU.mult, ALU.add)\
                .then_inc(S(tag + "_ms"), 1)

        def token_rsqrt(pool, tag):
            pool.wait_ge(S(tag + "_ms"), count(tag + "_ms", 1))
            nc.gpsimd.tensor_tensor(tok[:, NCH:2 * NCH], tok[:, 0:NCH], mhalf[:, 0:NCH], ALU.pow)\
                .then_inc(S(tag + "_rt"), 1)

        def spread(pe, src, bank):
            for c in range(NCH):
                last = pe.matmul(ps[bank][:, c * P:(c + 1) * P], src[:, c:c + 1].broadcast_to([P, P]), ident,
                                 start=True, stop=True)
            return last

        def norm_pe(pe, tag, n=KT, bank=2):
            token_sums(pe, tag, n, bank)
            pe.wait_ge(S(tag + "_rt"), count(tag + "_rt", 1))
            spread(pe, tok[:, NCH:2 * NCH], bank + 1).then_inc(S(tag + "_row"), 1)

        def norm_row(act, tag, bank=2):
            act.wait_ge(S(tag + "_row"), count(tag + "_row", 1))
            nc.scalar.activation(R[:], ps[bank + 1][:], ACT.Copy).then_inc(S(tag + "_R"), 1)

        def pair_wait(tag):
            def wait(pe):
                def at(k):
                    pe.wait_ge(S(tag + "_hi"), count(tag + "_hi", k + 1))
                    pe.wait_ge(S(tag + "_lo"), count(tag + "_lo", k + 1))
                return at
            return wait

        def x_loaded(eng, m):
            eng.wait_ge(S("x_in"), count("x_in", 16))

        o = 0
        yo = 0

        def carve_y(n):
            nonlocal yo
            yo += n
            assert yo <= KT * T
            return Y[:, yo - n:yo]
        AU = [carve(T + APAD + 1) for _ in range(2)]
        AC = [carve(T) for _ in range(2)]
        AT = [carve(T) for _ in range(2)]
        KQ = carve(2 * T)
        KQv = KQ.rearrange("p (c n t) -> p c n t", c=NCH, n=2)
        VT, GT = carve(T), carve(T)
        KG, KD, VR = carve(T), carve(T), carve(T)
        DT, EG, QD = carve(T), carve(T), carve(T)
        LA = carve_y(2 * T)
        LAv = LA.rearrange("p (c n t) -> p c n t", c=NCH, n=2)
        XB, WT = carve_y(T), carve_y(T)
        TX = carve_y(2 * T)
        VN = [carve_y(P) for _ in range(2)]
        ST = [carve_y(P) for _ in range(2)]
        O2 = carve_y(T)
        HC = HEADS * NCH
        BA = carve(NCH * 16)
        BAv = BA.rearrange("p (c n) -> p n c", c=NCH)
        BETA, G, NGC, EGC, EGL, EKD, Z1, Z2 = (carve(HC) for _ in range(8))
        NEA = carve(HEADS)
        TK = carve(32)
        assert o <= NSCR

        def v3(ap):
            return ap.rearrange("p (c t) -> p c t", c=NCH)

        def over_tokens(ap):
            return ap.unsqueeze(2).broadcast_to([P, NCH, P])

        def over_chunks(ap):
            return ap.unsqueeze(1).broadcast_to([P, NCH, P])

        PER = dict(d_c0=3, d_tap=9, d_th=4, d_qkv=3, d_gate=1, d_sq=2, d_ssq=2, d_tr=2, d_gcol=1, d_gb=1, d_gram=1,
                   d_s1=4, d_sq_eps=1, d_sqk=1, d_mask=1, d_dt=4, d_eg=1, d_la=8, d_tt=14, d_t=2, d_ptr=2, d_px=12,
                   d_x=14, d_pt=12, d_pw=2, d_wt=2, d_pv=4, d_vn=4, d_po=1, d_ps=3, d_s=3, d_osq=1, d_os=1, d_oms=1,
                   d_orow=1, d_ro=1, d_o1=1, d_o2=1, o_hi=1, o_lo=1)

        def head_count(h):
            def at(name, k):
                return count(name, h * PER[name] + k)
            return at

        def chunk(ap, c):
            return ap[:, c * P:(c + 1) * P]

        def halfx(i):
            return TX[:, i * T:(i + 1) * T]

        def t_of(c):
            return TX[:, (c // 2) * T + (c % 2) * P:(c // 2) * T + (c % 2 + 1) * P]

        def tt_of(c):
            return TX[:, (c // 2) * T + (c % 2 + 2) * P:(c // 2) * T + (c % 2 + 3) * P]

        def two(ap):
            return ap.rearrange("p (c t) -> p c t", c=2)

        def level(l):
            return cst[:, C_LVL + l * P:C_LVL + (l + 1) * P].unsqueeze(1).broadcast_to([P, 2, P])

        def delta_pe(pe, h, more):
            at = head_count(h)
            r = rnd(U_DELTA, h + 1)

            def part(s, first, n):
                if not more:
                    return
                if first == 0:
                    unit_wait(pe, r, s)
                last = part_blocks(pe, s % 2, s, pairA, first, n)
                if first + n == KT:
                    last.then_inc(S(f"unit_done{s}"), 1)
            pe.wait_ge(S("d_gcol"), at("d_gcol", 1))
            for c in range(NCH):
                last = pe.matmul(chunk(ps[5], c), TK[:, c:c + 1].broadcast_to([P, P]), tri, start=True, stop=True)
            last.then_inc(S("d_gb"), 1)
            pe.wait_ge(S("d_sq"), at("d_sq", 1))
            for c in range(NCH):
                last = pe.matmul(ps[2][:, c:c + 1], SQ[:, T + c * P:T + (c + 1) * P], ones[:, 0:1], start=True, stop=True)
            last.then_inc(S("d_ssq"), 1)
            pe.wait_ge(S("d_qkv"), at("d_qkv", 2))
            for c in range(NCH):
                last = pe.matmul(ps[4 - c // 2][:, (c % 2) * 256:(c % 2 + 1) * 256], KQv[:, c, 0, :],
                                 KQ[:, c * 256:(c + 1) * 256], start=True, stop=True)
            last.then_inc(S("d_gram"), 1)
            part(0, 0, 3)
            pe.wait_ge(S("d_o1"), at("d_o1", 0))
            for c in range(NCH):
                last = pe.transpose(chunk(ps[6], c), KQv[:, c, 0, :], ident)
            last.then_inc(S("d_tr"), 1)
            pe.wait_ge(S("d_qkv"), at("d_qkv", 3))
            pe.wait_ge(S("d_o2"), at("d_o2", 0))
            for c in range(NCH):
                last = pe.transpose(chunk(ps[7], c), chunk(VT, c), ident)
            last.then_inc(S("d_tr"), 1)
            part(0, 3, 3)
            pe.wait_ge(S("d_sq"), at("d_sq", 2))
            pe.wait_ge(S("d_s1"), at("d_s1", 1))
            for c in range(NCH):
                last = pe.matmul(ps[2][:, NCH + c:NCH + c + 1], SQ[:, c * P:(c + 1) * P], ones[:, 0:1],
                                 start=True, stop=True)
            last.then_inc(S("d_ssq"), 1)
            for i in range(2):
                pe.wait_ge(S("d_tt"), at("d_tt", i + 1))
                for c in (2 * i, 2 * i + 1):
                    last = pe.transpose(chunk(ps[4 + i], c % 2), tt_of(c), ident)
                last.then_inc(S("d_ptr"), 1)
                if i == 0:
                    part(0, 6, 2)
            for l in range(1, 7):
                for i in range(2):
                    pe.wait_ge(S("d_tt"), at("d_tt", 2 * l - 1 + i))
                    if l == 1:
                        pe.wait_ge(S("d_t"), at("d_t", i + 1))
                    for c in (2 * i, 2 * i + 1):
                        last = pe.matmul(chunk(ps[4 + i], c % 2), LAv[:, c, 0, :], t_of(c), start=True, stop=True)
                    last.then_inc(S("d_px"), 1)
                if l < 5:
                    part(1, 2 * (l - 1), 2)
                else:
                    part(2, 2 * (l - 5), 2)
                for i in range(2):
                    pe.wait_ge(S("d_x"), at("d_x", 2 * l + 1 + i))
                    if l == 1:
                        pe.wait_ge(S("d_la"), at("d_la", 7))
                    for c in (2 * i, 2 * i + 1):
                        if l < 6:
                            pe.matmul(chunk(ps[6 + i], c % 2), tt_of(c), chunk(XB, c), start=True, stop=True)
                        last = pe.matmul(chunk(ps[6 + i], c % 2 + 2), chunk(XB, c), tt_of(c), start=True, stop=True)
                    last.then_inc(S("d_pt"), 1)
            for i in range(2):
                pe.wait_ge(S("d_tt"), at("d_tt", 13 + i))
                if i == 0:
                    pe.matmul(chunk(ps[3], 0), tt_of(0), chunk(VR, 0), start=True, stop=True).then_inc(S("d_pv"), 1)
                for c in (2 * i, 2 * i + 1):
                    last = pe.matmul(chunk(ps[4 + i], c % 2), chunk(KG, c), tt_of(c), start=True, stop=True)
                last.then_inc(S("d_pw"), 1)
            for c in range(NCH):
                val = ps[3 + 4 * (c % 2)][:, 0:P]
                if c:
                    pe.wait_ge(S("d_wt"), at("d_wt", c // 2 + 1))
                    pe.wait_ge(S("d_s"), at("d_s", c))
                    pe.matmul(val, chunk(WT, c), ST[c % 2], start=False, stop=True).then_inc(S("d_pv"), 1)
                    pe.matmul(chunk(ps[6], c), ST[c % 2], chunk(QD, c), start=True, stop=False)
                if c < NCH - 1:
                    pe.matmul(ps[3 + 4 * ((c + 1) % 2)][:, 0:P], tt_of(c + 1), chunk(VR, c + 1), start=True, stop=False)
                part(2, 4 + c, 1)
                pe.wait_ge(S("d_vn"), at("d_vn", c + 1))
                if c < NCH - 1:
                    pe.matmul(ps[2][:, (c % 2 + 1) * P:(c % 2 + 2) * P], chunk(KD, c), VN[c % 2],
                              start=True, stop=True).then_inc(S("d_ps"), 1)
                last = pe.matmul(chunk(ps[6], c), VN[c % 2], LAv[:, c, 1, :], start=c == 0, stop=True)
            last.then_inc(S("d_po"), 1)
            part(3, 0, 3)
            pe.wait_ge(S("d_osq"), at("d_osq", 1))
            for c in range(NCH):
                last = pe.matmul(ps[2][:, 8 + c:9 + c], SQ[:, c * P:(c + 1) * P], ones[:, 0:1], start=True, stop=True)
            last.then_inc(S("d_os"), 1)
            part(3, 3, 3)
            pe.wait_ge(S("d_orow"), at("d_orow", 1))
            for c in range(NCH):
                last = pe.matmul(chunk(ps[7], c), TK[:, 28 + c:29 + c].broadcast_to([P, P]), ident,
                                 start=True, stop=True)
            last.then_inc(S("d_ro"), 1)
            part(3, 6, 2)

        def head_col(ap, h, c=0, n=1):
            return ap[:, bass.ds(h * NCH + c, n)]

        def conv_act(act, h, k):
            at = head_count(h)
            act.wait_ge(S(f"evac{k}"), count(f"evac{k}", rnd(U_DELTA, h) + 1))
            if k < 3:
                nc.scalar.activation(AC[k % 2], AU[k % 2][:, APAD:APAD + T], ACT.Copy,
                                     scale=half[:, bass.ds(8 + (k * 8 + h) * 4 + 3, 1)]).then_inc(S("d_c0"), 1)
                act.wait_ge(S("d_tap"), at("d_tap", 3 * (k + 1)))
            nc.scalar.activation(AT[k % 2], AC[k % 2], ACT.Tanh).then_inc(S("d_th"), 1)

        def delta_act(act, h, more):
            at = head_count(h)
            a = nc.scalar
            r = rnd(U_DELTA, h + 1)

            def square_of(n):
                a.activation(v3(tile(SQ, 1 - n)), KQv[:, :, n, :], ACT.Square).then_inc(S("d_sq"), 1)
            act.wait_ge(S("d_qkv"), at("d_qkv", 2))
            square_of(0)
            act.wait_ge(S("d_gb"), at("d_gb", 1))
            a.activation(EG, ps[5][:], ACT.Exp).then_inc(S("d_eg"), 1)
            act.wait_ge(S("d_mask"), at("d_mask", 1))
            for c in range(NCH):
                a.activation(chunk(DT, c), chunk(DT, c), ACT.Exp, bias=head_col(NGC, h, c)).then_inc(S("d_dt"), 1)
            act.wait_ge(S("d_os"), at("d_os", 0))
            square_of(1)
            if more:
                ahead(act, split_hi, r, 0)
            for i in range(2):
                act.wait_ge(S("d_ptr"), at("d_ptr", i + 1))
                a.activation(halfx(i)[:, 0:2 * P], ps[4 + i][:, 0:2 * P], ACT.Copy).then_inc(S("d_t"), 1)
            if more:
                ahead(act, split_hi, r, 1)
                conv_act(act, h + 1, 0)
                ahead(act, split_hi, r, 2)
                conv_act(act, h + 1, 1)
                ahead(act, split_hi, r, 3)
            for i in range(2):
                act.wait_ge(S("d_pw"), at("d_pw", i + 1))
                a.activation(WT[:, 2 * i * P:2 * (i + 1) * P], ps[4 + i][:, 0:2 * P], ACT.Copy, scale=-1.0)\
                    .then_inc(S("d_wt"), 1)
            act.wait_ge(S("d_po"), at("d_po", 1))
            a.activation(SQ[:, 0:T], ps[6][:], ACT.Square).then_inc(S("d_osq"), 1)
            if more:
                conv_act(act, h + 1, 2)
            act.wait_ge(S("d_o2"), at("d_o2", 1))
            a.activation(tile(pairB[0], h), O2, ACT.Copy).then_inc(S("o_hi"), 1)
            if more:
                conv_act(act, h + 1, 3)

        def conv_dve(dve, h, k, step):
            at = head_count(h)
            v = nc.vector
            if step == 0:
                evacuate(dve, rnd(U_DELTA, h), k, AU[k % 2][:, APAD:APAD + T], 1.0, R[:])
            elif step < 4:
                tap = 3 - step
                if step == 1:
                    dve.wait_ge(S("d_c0"), at("d_c0", k + 1))
                else:
                    dve.wait_ge(S("d_tap"), at("d_tap", 3 * k + step - 1))
                v.scalar_tensor_tensor(out=AC[k % 2], in0=AU[k % 2][:, tap:tap + T],
                                       scalar=half[:, bass.ds(8 + (k * 8 + h) * 4 + tap, 1)],
                                       in1=AC[k % 2], op0=ALU.mult, op1=ALU.add).then_inc(S("d_tap"), 1)
            else:
                dve.wait_ge(S("d_th"), at("d_th", k + 1))
                out = [KQv[:, :, 1, :], KQv[:, :, 0, :], v3(VT)][k]
                v.scalar_tensor_tensor(out=out, in0=v3(AT[k % 2]), scalar=1.0, in1=v3(AC[k % 2]),
                                       op0=ALU.add, op1=ALU.mult).then_inc(S("d_qkv"), 1)

        def delta_dve(dve, h, more):
            at = head_count(h)
            v = nc.vector
            r = rnd(U_DELTA, h + 1)

            def conv(k, *steps):
                if more:
                    for step in steps:
                        conv_dve(dve, h + 1, k, step)

            def split(k):
                if more:
                    ahead(dve, split_lo, r, k)
            v.tensor_copy(TK[:, 0:4], head_col(G, h, 0, 4)).then_inc(S("d_gcol"), 1)
            dve.wait_ge(S("d_th"), at("d_th", 4))
            v.scalar_tensor_tensor(out=GT, in0=AT[1], scalar=1.0, in1=AC[1], op0=ALU.add, op1=ALU.mult)\
                .then_inc(S("d_gate"), 1)
            dve.wait_ge(S("d_eg"), at("d_eg", 1))
            v.tensor_tensor(v3(DT), v3(ps[5][:]), over_chunks(cst[:, C_NEG:C_NEG + P]), ALU.add)\
                .then_inc(S("d_mask"), 1)
            dve.wait_ge(S("d_ssq"), at("d_ssq", 1))
            v.tensor_scalar(TK[:, 4:8], ps[2][:, 0:4], EPS, None, ALU.add).then_inc(S("d_s1"), 1)
            dve.wait_ge(S("d_s1"), at("d_s1", 1))
            v.reciprocal(TK[:, 12:16], TK[:, 4:8]).then_inc(S("d_s1"), 1)
            dve.wait_ge(S("d_s1"), at("d_s1", 2))
            v.tensor_tensor(TK[:, 16:20], TK[:, 12:16], head_col(BETA, h, 0, 4), ALU.mult).then_inc(S("d_s1"), 1)
            dve.wait_ge(S("d_s1"), at("d_s1", 3))
            v.tensor_tensor(TK[:, 20:24], TK[:, 16:20], head_col(EKD, h, 0, 4), ALU.mult).then_inc(S("d_s1"), 1)
            dve.wait_ge(S("d_gram"), at("d_gram", 1))
            for c in range(NCH):
                dve.wait_ge(S("d_dt"), at("d_dt", c + 1))
                g = ps[4 - c // 2][:, (c % 2) * 256:(c % 2 + 1) * 256].rearrange("p (n t) -> p n t", n=2)
                v.scalar_tensor_tensor(out=LAv[:, c, :, :], in0=g, scalar=TK[:, 16 + c:17 + c],
                                       in1=chunk(DT, c).unsqueeze(1).broadcast_to([P, 2, P]),
                                       op0=ALU.mult, op1=ALU.mult).then_inc(S("d_la"), 1)
                if c % 2:
                    i = c // 2
                    x = XB[:, 2 * i * P:2 * (i + 1) * P]
                    dve.wait_ge(S("d_la"), at("d_la", c + 1))
                    v.tensor_tensor(two(x), LAv[:, 2 * i:2 * i + 2, 0, :], level(0), ALU.mult).then_inc(S("d_x"), 1)
                    dve.wait_ge(S("d_x"), at("d_x", i + 1))
                    v.tensor_tensor(two(halfx(i)[:, 2 * P:4 * P]), ident.unsqueeze(1).broadcast_to([P, 2, P]), two(x),
                                    ALU.subtract).then_inc(S("d_tt"), 1)
            dve.wait_ge(S("d_tr"), at("d_tr", 1))
            v.tensor_tensor(v3(KG), v3(ps[6][:]), over_tokens(head_col(EGC, h, 0, 4)), ALU.mult).then_inc(S("d_la"), 1)
            dve.wait_ge(S("d_s1"), at("d_s1", 4))
            v.tensor_tensor(v3(KD), v3(ps[6][:]), over_tokens(TK[:, 20:24]), ALU.mult).then_inc(S("d_la"), 1)
            dve.wait_ge(S("d_sqk"), at("d_sqk", 1))
            dve.wait_ge(S("d_tr"), at("d_tr", 2))
            v.tensor_tensor(v3(VR), v3(ps[7][:]), over_tokens(TK[:, 24:28]), ALU.mult).then_inc(S("d_la"), 1)
            v.tensor_tensor(v3(QD), KQv[:, :, 1, :], v3(EG), ALU.mult).then_inc(S("d_la"), 1)
            split(0)
            for l in range(1, 7):
                for i in range(2):
                    dve.wait_ge(S("d_px"), at("d_px", 2 * l - 1 + i))
                    v.tensor_tensor(two(XB[:, 2 * i * P:2 * (i + 1) * P]), two(ps[4 + i][:, 0:2 * P]), level(l), ALU.mult)\
                        .then_inc(S("d_x"), 1)
                if l == 1:
                    dve.wait_ge(S("d_ssq"), at("d_ssq", 2))
                    v.tensor_scalar(TK[:, 8:12], ps[2][:, 4:8], EPS, EPS * P, ALU.add, ALU.mult)\
                        .then_inc(S("d_sq_eps"), 1)
                    conv(0, 0)
                elif l == 2:
                    split(1)
                elif l == 4:
                    dve.wait_ge(S("d_la"), at("d_la", 8))
                    dve.wait_ge(S("d_sq"), at("d_sq", 2))
                    conv(0, 4)
                elif l == 5:
                    conv(1, 0)
                elif l == 6:
                    conv(1, 2)
                for i in range(2):
                    dve.wait_ge(S("d_pt"), at("d_pt", 2 * l - 1 + i))
                    lo = 0 if l < 6 else 2 * P
                    v.tensor_tensor(halfx(i)[:, lo:T], halfx(i)[:, lo:T], ps[6 + i][:, lo:T], ALU.subtract)\
                        .then_inc(S("d_tt"), 1)
                if l == 2:
                    conv(0, 1)
                elif l == 3:
                    conv(0, 2, 3)
                elif l == 4:
                    split(2)
                elif l == 5:
                    conv(1, 1)
                elif l == 6:
                    conv(1, 3)
            for c in range(NCH):
                dve.wait_ge(S("d_pv"), at("d_pv", c + 1))
                v.tensor_copy(VN[c % 2], ps[3 + 4 * (c % 2)][:, 0:P]).then_inc(S("d_vn"), 1)
                if c < NCH - 1:
                    dve.wait_ge(S("d_ps"), at("d_ps", c + 1))
                    add = ps[2][:, (c % 2 + 1) * P:(c % 2 + 2) * P]
                    if c == 0:
                        v.tensor_copy(ST[1], add).then_inc(S("d_s"), 1)
                    else:
                        dve.wait_ge(S("d_s"), at("d_s", c))
                        v.scalar_tensor_tensor(out=ST[(c + 1) % 2], in0=ST[c % 2], scalar=head_col(EGL, h, c),
                                               in1=add, op0=ALU.mult, op1=ALU.add).then_inc(S("d_s"), 1)
                if c == 1:
                    conv(1, 4)
            split(3)
            conv(2, 0)
            dve.wait_ge(S("d_os"), at("d_os", 1))
            dve.wait_ge(S("d_sq_eps"), at("d_sq_eps", 1))
            v.scalar_tensor_tensor(out=TK[:, 12:16], in0=ps[2][:, 8:12], scalar=1.0 / P, in1=TK[:, 8:12],
                                   op0=ALU.mult, op1=ALU.add).then_inc(S("d_oms"), 1)
            dve.wait_ge(S("o_lo"), at("o_lo", 0))
            v.scalar_tensor_tensor(out=O2, in0=ps[6][:], scalar=par_col("onorm"), in1=GT,
                                   op0=ALU.mult, op1=ALU.mult).then_inc(S("d_o1"), 1)
            conv(2, 1, 2)
            dve.wait_ge(S("d_o1"), at("d_o1", 1))
            dve.wait_ge(S("d_ro"), at("d_ro", 1))
            v.tensor_tensor(O2, O2, ps[7][:], ALU.mult).then_inc(S("d_o2"), 1)
            conv(2, 3)
            if more:
                evacuate(dve, r, 3, AC[1], 0.5, R[:])
            conv(2, 4)

        def delta_pool(pool, h):
            at = head_count(h)
            pool.wait_ge(S("d_s1"), at("d_s1", 1))
            nc.gpsimd.tensor_tensor(TK[:, 24:28], TK[:, 4:8], mhalf[:, 4:8], ALU.pow).then_inc(S("d_sqk"), 1)
            pool.wait_ge(S("d_oms"), at("d_oms", 1))
            nc.gpsimd.tensor_tensor(TK[:, 28:32], TK[:, 12:16], mhalf[:, 0:4], ALU.pow).then_inc(S("d_orow"), 1)
            pool.wait_ge(S("o_hi"), at("o_hi", 1))
            nc.gpsimd.tensor_tensor(tile(pairB[1], h), O2, tile(pairB[0], h).bitcast(F32), ALU.subtract).then_inc(S("o_lo"), 1)

        def evacuate(dve, r, k, out, scalar, in1, op1=ALU.mult, op0=ALU.mult):
            evac_wait(dve, r, k)
            return nc.vector.scalar_tensor_tensor(out=out, in0=ps[k % 2][:], scalar=scalar, in1=in1,
                                                  op0=op0, op1=op1).then_inc(S(f"evac{k}"), 1)

        def residual_pe(pe, base, pair, wait, n=KT):
            for i in range(2):
                for s in range(SLOTS):
                    unit(pe, rnd(base, i), s, pair, n, wait=wait if i + s == 0 else None)

        def residual_act(act, base, tag, g, pair, end=False):
            for i in range(2):
                for k in range(SLOTS):
                    m, r = 4 * i + k, rnd(base, i)
                    if not (end and m >= KT - LEAD):
                        ahead(act, split_hi, r, k)
                    act.wait_ge(S(f"evac{k}"), count(f"evac{k}", r + 1))
                    if g:
                        nc.scalar.activation(tile(pair[0], m), tile(X, m), ACT.Copy, scale=par_col(g, m)).then_inc(S(tag + "_hi"), 1)
                    square(act, tag, m, tile(X, m))

        def residual_dve(dve, base, tag, g, pair, bias=None, end=False):
            for i in range(2):
                for k in range(SLOTS):
                    m, r = 4 * i + k, rnd(base, i)
                    if not (end and m >= KT - LEAD):
                        ahead(dve, split_lo, r, k)
                    evacuate(dve, r, k, tile(X, m), par_col(bias, m) if bias else 0.0, tile(X, m), ALU.add, ALU.add)
                    if g and m:
                        norm_lo(dve, tag, g, pair, m - 1)
            if g:
                norm_lo(dve, tag, g, pair, KT - 1)

        FU = [AU[0][:, 0:T + FPAD], AU[1][:, 0:T + FPAD]]
        FC = AC
        FT = AT[0]
        PR = [KQ[:, 0:T], KQ[:, T:2 * T]]

        def ffn_bases(base):
            first = 0
            for n in MID_GROUPS:
                yield base, base + 2 * n, first, n
                base, first = base + 2 * n + 8, first + n

        def hidden_rounds(eng, base, first, n, one_round):
            start = 0
            if first == 0:
                one_round(0, True)
                start = 1
            with eng.Fori(start, n // 2) as i:
                one_round(i, False)

        def ffn_pe(pe, L, base, inpair, mid, ntag, end=False):
            t = f"f{L}"
            for up, down, first, n in ffn_bases(base):
                def one_round(i, begin):
                    for s in range(SLOTS):
                        unit(pe, rnd(up, i), s, inpair, wait=pair_wait(ntag)(pe) if begin and s == 0 else None)
                        if begin and s == 0:
                            norm_pe(pe, ntag)
                hidden_rounds(pe, up, first, n, one_round)

                def wait_mid(k):
                    pe.wait_ge(S(t + "_hi"), count(t + "_hi", first + k + 1))
                    pe.wait_ge(S(t + "_lo"), count(t + "_lo", first + k + 1))
                residual_pe(pe, down, mid, wait_mid, n)

        def ffn_act(act, L, base, mid, ntag, next_tag, next_g, next_pair, end=False):
            t = f"f{L}"
            for up, down, first, n in ffn_bases(base):
                def one_round(i, begin):
                    for k in range(SLOTS):
                        r = rnd(up, i)
                        ahead(act, split_hi, r, k)
                        if begin and k == 0:
                            norm_row(act, ntag)
                            act.wait_ge(S(t + "_half"), count(t + "_half", 2))
                        q, side = first + 2 * i + k // 2, k % 2
                        act.wait_ge(S(f"evac{k}"), count(f"evac{k}", r + 1))
                        if not begin or k > 1:
                            act.wait_ge(S(t + "_prod"), count(t + "_prod", q))
                        if side == 0:
                            w3, b = half[:, bass.ds(104 + q * 3 + 2, 1)], half[:, bass.ds(170 + q, 1)]
                        else:
                            w3, b = par_col(f"f_conv{L}", (22 + q) * 3 + 2), par_col(f"f_bias{L}", 22 + q)
                        nc.scalar.activation(FC[side], FU[side][:, FPAD:FPAD + T], ACT.Identity, scale=w3, bias=b).then_inc(S(t + "_c0"), 1)
                        if side == 0:
                            act.wait_ge(S(t + "_tap"), count(t + "_tap", 4 * q + 2))
                            nc.scalar.activation(FT, FC[0], ACT.Tanh).then_inc(S(t + "_th"), 1)
                        else:
                            act.wait_ge(S(t + "_prod"), count(t + "_prod", q + 1))
                            nc.scalar.activation(tile(mid[0], 2 * i + k // 2), PR[k // 2], ACT.Copy).then_inc(S(t + "_hi"), 1)
                hidden_rounds(act, up, first, n, one_round)
                if first + n < 22:
                    with act.Fori(0, 2) as i:
                        for k in range(SLOTS):
                            ahead(act, split_hi, rnd(down, i), k)
                else:
                    residual_act(act, down, next_tag, next_g, next_pair, end)

        def ffn_dve(dve, L, base, mid, ntag, next_tag, next_g, next_pair, end=False):
            t = f"f{L}"
            v = nc.vector
            c, b = _cols[f"f_conv{L}"][0], _cols[f"f_bias{L}"][0]
            v.tensor_scalar(half[:, 104:170], par[:, c:c + 66], 0.5, None, ALU.mult).then_inc(S(t + "_half"), 1)
            v.tensor_scalar(half[:, 170:192], par[:, b:b + 22], 0.5, None, ALU.mult).then_inc(S(t + "_half"), 1)
            dve.wait_ge(S(t + "_half"), count(t + "_half", 2))
            for u in FU:
                v.memset(u[:, 0:FPAD], 0.0).then_inc(S(t + "_pad"), 1)
            token_mean(dve, ntag, 2, D)
            for up, down, first, n in ffn_bases(base):
                def one_round(i, begin):
                    for k in range(SLOTS):
                        r = rnd(up, i)
                        ahead(dve, split_lo, r, k)
                        if begin and k == 0:
                            dve.wait_ge(S(ntag + "_R"), count(ntag + "_R", 1))
                            dve.wait_ge(S(t + "_pad"), count(t + "_pad", 2))
                        q, side = first + 2 * i + k // 2, k % 2
                        evacuate(dve, r, k, FU[side][:, FPAD:FPAD + T], 1.0, R[:])
                        dve.wait_ge(S(t + "_c0"), count(t + "_c0", 2 * q + side + 1))
                        for n_, tap in enumerate((1, 0)):
                            w = half[:, bass.ds(104 + q * 3 + tap, 1)] if side == 0 else \
                                par_col(f"f_conv{L}", (22 + q) * 3 + tap)
                            if n_:
                                dve.wait_ge(S(t + "_tap"), count(t + "_tap", 4 * q + 2 * side + 1))
                            v.scalar_tensor_tensor(out=FC[side], in0=FU[side][:, tap:tap + T], scalar=w,
                                                       in1=FC[side], op0=ALU.mult, op1=ALU.add).then_inc(S(t + "_tap"), 1)
                        if side == 0:
                            continue
                        dve.wait_ge(S(t + "_th"), count(t + "_th", q + 1))
                        v.scalar_tensor_tensor(out=FC[0], in0=FT, scalar=1.0, in1=FC[0], op0=ALU.add,
                                                   op1=ALU.mult).then_inc(S(t + "_gate"), 1)
                        dve.wait_ge(S(t + "_gate"), count(t + "_gate", q + 1))
                        dve.wait_ge(S(t + "_tap"), count(t + "_tap", 4 * q + 4))
                        if not begin:
                            dve.wait_ge(S(t + "_lo"), count(t + "_lo", q - 1))
                        v.tensor_tensor(PR[k // 2], FC[0], FC[1], ALU.mult).then_inc(S(t + "_prod"), 1)
                hidden_rounds(dve, up, first, n, one_round)
                if first + n < 22:
                    with dve.Fori(0, 2) as i:
                        for k in range(SLOTS):
                            r = rnd(down, i)
                            ahead(dve, split_lo, r, k)
                            evacuate(dve, r, k, tile(X, 4 * i + k), 0.0, tile(X, 4 * i + k), ALU.add, ALU.add)
                else:
                    residual_dve(dve, down, next_tag, next_g, next_pair, end=end)

        def ffn_pool(pool, L, base, mid):
            t = f"f{L}"
            for up, down, first, n in ffn_bases(base):
                with pool.Fori(0, n // 2) as i:
                    for j in range(2):
                        pool.wait_ge(S(t + "_hi"), count(t + "_hi", first + 2 * i + j + 1))
                        nc.gpsimd.tensor_tensor(tile(mid[1], 2 * i + j), PR[j],
                                                    tile(mid[0], 2 * i + j).bitcast(F32), ALU.subtract).then_inc(S(t + "_lo"), 1)

        o = 0
        KA = [carve(T) for _ in range(2)]
        VF = carve(T)
        VA_T = [carve(T) for _ in range(2)]
        QT = [carve(T) for _ in range(2)]
        AW = carve(T)
        SC = [carve(2 * T) for _ in range(2)]
        PT = [carve(2 * T) for _ in range(2)]
        MX = carve(64)
        DD = carve(T)
        APER = dict(q_t=1, q_w=1, s_p=4, s_sc=4, s_mx=4, s_e=10, s_n=8, s_tr=4, s_pt=4, s_o=1, t_hi=1, t_lo=1)

        def sc3(e):
            return SC[e].rearrange("p (b s) -> p b s", b=NCH)

        def tile_count(t):
            def at(name, k):
                return count(name, t * APER[name] + k)
            return at

        def half_rows(ap, e):
            return ap[64 * e:64 * e + 64, :]

        def att_scores_pe(pe, t, a, qb):
            at = tile_count(t)
            pe.wait_ge(S("q_t"), at("q_t", 1))
            for e in range(2):
                for pairno in range(2):
                    bank = 2 + 2 * e + pairno
                    for b in (2 * pairno, 2 * pairno + 1):
                        lo = max(b - 1, 0) * P
                        n = P if b == 0 else 2 * P
                        out = ps[bank][:, (b % 2) * 256 + 256 - n:(b % 2) * 256 + 256]
                        last = pe.matmul(out, half_rows(QT[qb], e)[:, b * P:(b + 1) * P],
                                         half_rows(KA[a], e)[:, lo:lo + n], start=True, stop=True)
                    last.then_inc(S("s_p"), 1)

        def att_out_pe(pe, t, a):
            at = tile_count(t)
            for e in range(2):
                pe.wait_ge(S("s_n"), at("s_n", 4 * e + 4))
                for pairno in range(2):
                    for b in (2 * pairno, 2 * pairno + 1):
                        for j in range(2):
                            if b == 0 and j == 0:
                                continue
                            last = pe.transpose(ps[2 + 2 * e + pairno][:, (b % 2) * 256 + j * P:(b % 2) * 256 + (j + 1) * P],
                                                SC[e][:, b * 256 + j * P:b * 256 + (j + 1) * P], ident)
                    last.then_inc(S("s_tr"), 1)
            pe.wait_ge(S("t_lo"), at("t_lo", 0))
            for e in range(2):
                for b in range(NCH):
                    if b % 2 == 0:
                        pe.wait_ge(S("s_pt"), at("s_pt", 2 * e + b // 2 + 1))
                    for j in range(2):
                        if b == 0 and j == 0:
                            continue
                        last = pe.matmul(ps[6][64 * e:64 * e + 64, b * P:(b + 1) * P],
                                         VA_T[a][:, (b - 1 + j) * P + 64 * e:(b - 1 + j) * P + 64 * e + 64],
                                         PT[e][:, b * 256 + j * P:b * 256 + (j + 1) * P],
                                         start=j == 0 or b == 0, stop=j == 1)
            last.then_inc(S("s_o"), 1)

        def attention_pe(pe):
            for s in range(SLOTS):
                unit(pe, rnd(U_KV, 0), s, pairA, wait=pair_wait("kv")(pe) if s == 0 else None)
                if s == 0:
                    norm_pe(pe, "kv")
            for m in range(2):
                pe.wait_ge(S("v_f"), count("v_f", m + 1))
                if m:
                    pe.wait_ge(S("v_t"), count("v_t", m))
                for c in range(NCH):
                    last = pe.transpose(chunk(ps[4], c), chunk(VF, c), ident)
                last.then_inc(S("v_tr"), 1)

            pe.wait_ge(S("v_t"), count("v_t", 2))
            pe.wait_ge(S("bn_lo"), count("bn_lo", 8))
            with pe.Fori(0, 2) as i:
                r = rnd(U_Q, i)
                unit(pe, r, 0, pairB)
                for k in range(SLOTS):
                    t = 4 * i + k
                    att_scores_pe(pe, t, k % 2, k % 2)
                    if k < 3:
                        unit(pe, r, k + 1, pairB)
                    att_out_pe(pe, t, k % 2)

            def wait_o(k):
                pe.wait_ge(S("t_hi"), count("t_hi", k + 1))
                pe.wait_ge(S("t_lo"), count("t_lo", k + 1))
            residual_pe(pe, U_BO, pairA, wait_o)

        def attention_act(act):
            a = nc.scalar
            for k in range(SLOTS):
                ahead(act, split_hi, rnd(U_KV, 0), k)
                if k == 0:
                    norm_row(act, "kv")
                for m in (2 * k, 2 * k + 1):
                    a.activation(tile(pairB[0], m), tile(X, m), ACT.Copy, scale=par_col("b_norm", m)).then_inc(S("bn_hi"), 1)
            for m in range(2):
                act.wait_ge(S("v_tr"), count("v_tr", m + 1))
                a.activation(VA_T[m], ps[4][:], ACT.Copy).then_inc(S("v_t"), 1)
            with act.Fori(0, 2) as i:
                for k in range(SLOTS):
                    t = 4 * i + k
                    at = tile_count(t)
                    ahead(act, split_hi, rnd(U_Q, i), k)
                    for e in range(2):
                        act.wait_ge(S("s_mx"), at("s_mx", 2 * e + 2))
                        den = MX[:, 8 * e:8 * e + 8]
                        neg = MX[:, 16 + 4 * e:20 + 4 * e]
                        a.activation(MX[:, 24 + 4 * e:28 + 4 * e], neg, ACT.Exp,
                                         bias=rowp[:, bass.ds(16 + 2 * t + e, 1)]).then_inc(S("s_e"), 1)
                        for b in range(NCH):
                            sc = SC[e][:, b * 256 + (0 if b else P):(b + 1) * 256]
                            a.activation(sc, sc, ACT.Exp, bias=neg[:, b:b + 1],
                                             accum_out=den[:, b:b + 1]).then_inc(S("s_e"), 1)
                    for e in range(2):
                        for pairno in range(2):
                            act.wait_ge(S("s_tr"), at("s_tr", 2 * e + pairno + 1))
                            lo = P if pairno == 0 else 0
                            a.activation(PT[e][:, pairno * T + lo:(pairno + 1) * T],
                                             ps[2 + 2 * e + pairno][:, lo:T], ACT.Copy).then_inc(S("s_pt"), 1)
                    act.wait_ge(S("s_o"), at("s_o", 1))
                    a.activation(tile(pairA[0], t), ps[6][:], ACT.Copy).then_inc(S("t_hi"), 1)
            residual_act(act, U_BO, "n_f1", "f_norm1", pairB)

        def attention_dve(dve):
            v = nc.vector
            token_mean(dve, "kv", 2, D)
            for e in range(2):
                v.memset(SC[e][:, 0:P], -FAR).then_inc(S("sc_far"), 1)
                v.tensor_copy(DD[:, e * 256:(e + 1) * 256], cst[:, C_DIST:C_DIST + 256]).then_inc(S("sc_far"), 1)
            dve.wait_ge(S("sc_far"), count("sc_far", 4))
            for k in range(SLOTS):
                r = rnd(U_KV, 0)
                ahead(dve, split_lo, r, k)
                if k == 0:
                    dve.wait_ge(S("kv_R"), count("kv_R", 1))
                evacuate(dve, r, k, AW, 1.0, R[:])
                dve.wait_ge(S(f"evac{k}"), count(f"evac{k}", r + 1))
                if k > 2:
                    dve.wait_ge(S("v_tr"), count("v_tr", k - 2))
                v.tensor_scalar(KA[k] if k < 2 else VF, AW, par_col("kv_b", k), None, ALU.add).then_inc(S("k_f" if k < 2 else "v_f"), 1)
                for m in (2 * k, 2 * k + 1):
                    norm_lo(dve, "bn", "b_norm", pairB, m)
                dve.wait_ge(S("k_f" if k < 2 else "v_f"), count("k_f" if k < 2 else "v_f", k % 2 + 1))

            def q_tile(i, k):
                r = rnd(U_Q, i)
                if k:
                    dve.wait_ge(S("q_t"), count("q_t", 4 * i + k))
                evacuate(dve, r, k, AW, 1.0, R[:])
                dve.wait_ge(S(f"evac{k}"), count(f"evac{k}", r + 1))
                v.tensor_scalar(QT[k % 2], AW, par_col("b_q", 4 * i + k), 0.125, ALU.add, ALU.mult).then_inc(S("q_t"), 1)
            with dve.Fori(0, 2) as i:
                q_tile(i, 0)
                for k in range(SLOTS):
                    t = 4 * i + k
                    at = tile_count(t)
                    for e in range(2):
                        nslope = rowp[:, bass.ds(32 + 2 * t + e, 1)]
                        for pairno in range(2):
                            dve.wait_ge(S("s_p"), at("s_p", 2 * e + pairno + 1))
                            lo = P if pairno == 0 else 0
                            v.scalar_tensor_tensor(out=SC[e][:, pairno * T + lo:(pairno + 1) * T],
                                                       in0=DD[:, lo:T], scalar=nslope,
                                                       in1=ps[2 + 2 * e + pairno][:, lo:T],
                                                       op0=ALU.mult, op1=ALU.add).then_inc(S("s_sc"), 1)
                        if e == 0:
                            ahead(dve, split_lo, rnd(U_Q, i), k)
                        dve.wait_ge(S("s_sc"), at("s_sc", 2 * e + 2))
                        mx = MX[:, 32 + 4 * e:36 + 4 * e]
                        v.tensor_reduce(mx, sc3(e), mybir.AxisListType.X, ALU.max).then_inc(S("s_mx"), 1)
                        dve.wait_ge(S("s_mx"), at("s_mx", 2 * e + 1))
                        v.tensor_scalar(MX[:, 16 + 4 * e:20 + 4 * e], mx, rowp[:, bass.ds(16 + 2 * t + e, 1)],
                                            -1.0, ALU.max, ALU.mult).then_inc(S("s_mx"), 1)
                    if k < 3:
                        q_tile(i, k + 1)
                    for e in range(2):
                        dve.wait_ge(S("s_e"), at("s_e", 5 * e + 5))
                        den = MX[:, 40 + 4 * e:44 + 4 * e]
                        v.tensor_tensor(den, MX[:, 8 * e:8 * e + 4], MX[:, 24 + 4 * e:28 + 4 * e], ALU.add).then_inc(S("s_n"), 1)
                        dve.wait_ge(S("s_n"), at("s_n", 4 * e + 1))
                        v.reciprocal(MX[:, 52 + 4 * e:56 + 4 * e], den).then_inc(S("s_n"), 1)
                        dve.wait_ge(S("s_n"), at("s_n", 4 * e + 2))
                        v.tensor_scalar(SC[e][:, P:2 * P], SC[e][:, P:2 * P], MX[:, 52 + 4 * e:53 + 4 * e], None,
                                            ALU.mult).then_inc(S("s_n"), 1)
                        v.tensor_tensor(sc3(e)[:, 1:NCH], sc3(e)[:, 1:NCH], MX[:, 53 + 4 * e:56 + 4 * e]
                                            .unsqueeze(2).broadcast_to([P, NCH - 1, 256]), ALU.mult).then_inc(S("s_n"), 1)
                    dve.wait_ge(S("t_hi"), at("t_hi", 1))
                    v.tensor_tensor(tile(pairA[1], t), ps[6][:], tile(pairA[0], t).bitcast(F32), ALU.subtract).then_inc(S("t_lo"), 1)
            residual_dve(dve, U_BO, "n_f1", "f_norm1", pairB, bias="b_o")

        def second_block_pe(pe):
            pe.wait_ge(S("row_in"), count("row_in", 32))
            pe.wait_ge(S("na_lo"), count("na_lo", KT))
            for c in range(NCH):
                for k in range(KT):
                    for part in range(2):
                        cols = tile(pairA[part], k)[:, c * P:(c + 1) * P].bitcast(F32)
                        last = pe.matmul(ps[6][:, c * 16:(c + 1) * 16], cols, tailw[:, k * 16:(k + 1) * 16],
                                         start=k + part == 0, stop=k == KT - 1 and part == 1)
            last.then_inc(S("tail"), 1)
            norm_pe(pe, "na")
            pe.wait_ge(S("g_tok"), count("g_tok", 1))
            pe.matmul(ps[6][:, 64:64 + HC], tri, G, start=True, stop=True)
            pe.matmul(ps[6][:, 128:128 + HC], ones[:], G, start=True, stop=True).then_inc(S("g_sum"), 1)
            pe.wait_ge(S("g_done"), count("g_done", 4))
            pe.wait_ge(S("ekd_sub"), count("ekd_sub", 1))
            for s in range(SLOTS):
                unit(pe, rnd(U_DELTA, 0), s, pairA)
            with pe.Fori(0, HEADS - 1) as h:
                delta_pe(pe, h, True)
            delta_pe(pe, HEADS - 1, False)

            def wait_o(k):
                pe.wait_ge(S("o_hi"), count("o_hi", k + 1))
                pe.wait_ge(S("o_lo"), count("o_lo", k + 1))
            residual_pe(pe, U_AOUT, pairB, wait_o)
            ffn_pe(pe, 0, U_FFN0, pairA, pairB, "nf0")
            attention_pe(pe)
            ffn_pe(pe, 1, U_FFN1, pairB, pairA, "n_f1", end=True)
            norm_pe(pe, "fin", bank=4)

        def second_block_act(act):
            a = nc.scalar
            norm_act(act, "na", "a_norm", pairA, lambda e, m: e.wait_ge(S("x2"), count("x2", m + 1)))
            norm_row(act, "na")
            act.wait_ge(S("row_in"), count("row_in", 32))
            a.activation(NEA, rowp[:, 0:8], ACT.Exp).then_inc(S("g_act"), 1)
            act.wait_ge(S("g_z"), count("g_z", 1))
            a.activation(Z2, Z1, ACT.Exp, scale=-1.0).then_inc(S("g_act"), 1)
            a.activation(BETA, BETA, ACT.Tanh, scale=0.5).then_inc(S("g_act"), 1)
            act.wait_ge(S("g_act"), count("g_act", 2))
            a.activation(Z2, Z2, ACT.Ln, bias=1.0).then_inc(S("g_act"), 1)
            act.wait_ge(S("g_sum"), count("g_sum", 1))
            a.activation(EGC, ps[6][:, 64:64 + HC], ACT.Exp).then_inc(S("g_done"), 1)
            a.activation(EGL, ps[6][:, 128:128 + HC], ACT.Exp).then_inc(S("g_done"), 1)
            a.activation(NGC, ps[6][:, 64:64 + HC], ACT.Copy, scale=-1.0).then_inc(S("g_done"), 1)
            act.wait_ge(S("ekd_sub"), count("ekd_sub", 1))
            a.activation(EKD, EKD, ACT.Exp).then_inc(S("g_done"), 1)
            for k in range(SLOTS):
                ahead(act, split_hi, rnd(U_DELTA, 0), k)
                conv_act(act, 0, k)
            with act.Fori(0, HEADS - 1) as h:
                delta_act(act, h, True)
            delta_act(act, HEADS - 1, False)
            residual_act(act, U_AOUT, "nf0", "f_norm0", pairA)
            ffn_act(act, 0, U_FFN0, pairB, "nf0", "kv", "kv_norm", pairA)
            attention_act(act)
            ffn_act(act, 1, U_FFN1, pairA, "n_f1", "fin", None, None, end=True)

        def second_block_dve(dve):
            v = nc.vector
            for m in range(KT):
                dve.wait_ge(S("x2"), count("x2", m + 1))
                norm_lo(dve, "na", "a_norm", pairA, m)
            token_mean(dve, "na", 2, D)
            for u in AU:
                v.memset(u[:, 0:APAD], 0.0).then_inc(S("a_pad"), 1)
            dve.wait_ge(S("na_rt"), count("na_rt", 1))
            dve.wait_ge(S("tail"), count("tail", 1))
            for c in range(NCH):
                v.tensor_scalar(BA[:, c * 16:(c + 1) * 16], ps[6][:, c * 16:(c + 1) * 16],
                                    tok[:, NCH + c:NCH + c + 1], None, ALU.mult).then_inc(S("g_v"), 1)
            dve.wait_ge(S("g_v"), count("g_v", 4))
            dve.wait_ge(S("row_in"), count("row_in", 32))

            def hc(ap):
                return ap.rearrange("p (h c) -> p h c", c=NCH)
            v.tensor_copy(hc(BETA), BAv[:, 0:8, :]).then_inc(S("g_v"), 1)
            v.tensor_tensor(hc(G), BAv[:, 8:16, :], rowp[:, 8:16].unsqueeze(2).broadcast_to([P, HEADS, NCH]),
                                ALU.add).then_inc(S("g_v"), 1)
            dve.wait_ge(S("g_v"), count("g_v", 6))
            v.scalar_tensor_tensor(out=Z1, in0=G, scalar=-1.0, in1=G, op0=ALU.mult, op1=ALU.max).then_inc(S("g_z"), 1)
            dve.wait_ge(S("g_act"), count("g_act", 4))
            v.scalar_tensor_tensor(out=Z1, in0=G, scalar=0.0, in1=Z2, op0=ALU.max, op1=ALU.add).then_inc(S("g_v"), 1)
            v.tensor_scalar(BETA, BETA, 0.5, 0.5, ALU.mult, ALU.add).then_inc(S("g_v"), 1)
            dve.wait_ge(S("g_v"), count("g_v", 8))
            v.tensor_tensor(hc(Z2), hc(Z1), NEA.unsqueeze(2).broadcast_to([P, HEADS, NCH]), ALU.mult).then_inc(S("g_v"), 1)
            dve.wait_ge(S("g_v"), count("g_v", 9))
            v.tensor_scalar(G, Z2, -1.0, None, ALU.mult).then_inc(S("g_tok"), 1)
            dve.wait_ge(S("g_sum"), count("g_sum", 1))
            dve.wait_ge(S("g_done"), count("g_done", 3))
            v.tensor_tensor(EKD, ps[6][:, 128:128 + HC], NGC, ALU.add).then_inc(S("ekd_sub"), 1)
            dve.wait_ge(S("g_done"), count("g_done", 4))
            dve.wait_ge(S("na_R"), count("na_R", 1))
            dve.wait_ge(S("a_pad"), count("a_pad", 2))
            for k in range(SLOTS):
                ahead(dve, split_lo, rnd(U_DELTA, 0), k)
                if k < 3:
                    for step in range(5):
                        conv_dve(dve, 0, k, step)
                else:
                    evacuate(dve, rnd(U_DELTA, 0), k, AC[1], 0.5, R[:])
            with dve.Fori(0, HEADS - 1) as h:
                delta_dve(dve, h, True)
            delta_dve(dve, HEADS - 1, False)
            residual_dve(dve, U_AOUT, "nf0", "f_norm0", pairA)
            ffn_dve(dve, 0, U_FFN0, pairB, "nf0", "kv", "kv_norm", pairA)
            attention_dve(dve)
            ffn_dve(dve, 1, U_FFN1, pairA, "n_f1", "fin", None, None, end=True)
            token_mean(dve, "fin", 4, D)
            dve.wait_ge(S("fin_row"), count("fin_row", 1))
            dve.wait_ge(S("fin_sq"), count("fin_sq", 8))
            for m in range(KT):
                v.scalar_tensor_tensor(out=tile(X, m), in0=tile(X, m), scalar=par_col("final", m), in1=ps[5][:],
                                           op0=ALU.mult, op1=ALU.mult).then_inc(S("final"), 1)

        def second_block_pool(pool):
            sum_squares(pool, "na", KT)
            token_rsqrt(pool, "na")
            with pool.Fori(0, HEADS) as h:
                delta_pool(pool, h)
            sum_squares(pool, "nf0", KT)
            token_rsqrt(pool, "nf0")
            ffn_pool(pool, 0, U_FFN0, pairB)
            sum_squares(pool, "kv", KT)
            token_rsqrt(pool, "kv")
            sum_squares(pool, "n_f1", KT)
            token_rsqrt(pool, "n_f1")
            ffn_pool(pool, 1, U_FFN1, pairA)
            sum_squares(pool, "fin", KT)
            token_rsqrt(pool, "fin")

        @block.sync
        def _(sp):
            sp.dma_start(X[:], io["xT"]).then_inc(S("x_in"), 16)
            sp.dma_start(par[:], io["par"]).then_inc(S("par_in"), 16)
            for s in range(SLOTS):
                sp.dma_start(raw[:, s * 1024:(s + 1) * 1024], io["ws"][s]).then_inc(S(f"raw_in{s}"), 16)
                if s == 0:
                    sp.dma_start(cst[:], io["cst"]).then_inc(S("cst_in"), 16)
                    sp.dma_start(rowp, io["row"].broadcast_to([P, 48])).then_inc(S("row_in"), 16)
                    sp.dma_start(tailw, io["tail"]).then_inc(S("row_in"), 16)
                    sp.dma_start(pwraw, io["pw"]).then_inc(S("pw_in"), 16)
            with sp.Fori(1, U_END // SLOTS) as r:
                for s in range(SLOTS):
                    sp.wait_ge(S(f"w_lo{s}"), count(f"w_lo{s}", r))
                    sp.dma_start(raw[:, s * 1024:(s + 1) * 1024],
                                 io["ws"][bass.ds(r * SLOTS + s, 1)].rearrange("a p n -> p (a n)"))\
                        .then_inc(S(f"raw_in{s}"), 16)
            sp.wait_ge(S("final"), count("final", KT))
            sp.dma_start(io["out"], X[:]).then_inc(S("out"), 16)
            sp.wait_ge(S("out"), 16)

        @block.tensor
        def _(pe):
            credit(pe, "d_os", *(f"unit_done{s}" for s in range(SLOTS)))
            pe.wait_ge(S("const"), count("const", 2))
            pe.wait_ge(S("cst_in"), count("cst_in", 16))

            def glu_round(i, first):
                for s in range(SLOTS):
                    begin = first and s == 0
                    unit(pe, rnd(U_GLU, i), s, pairA, wait=pair_wait("n0")(pe) if begin else None)
                    if begin:
                        norm_pe(pe, "n0")
            glu_round(0, True)
            glu_round(1, False)
            for s in range(SLOTS):
                unit(pe, rnd(U_POOL, 0), s, pairA)
            with pe.Fori(0, 4) as i:
                for s in range(SLOTS):
                    unit(pe, rnd(U_GATE, i), s, pairA)
            pe.wait_ge(S("pw_hi"), count("pw_hi", 1))
            pe.wait_ge(S("pw_lo"), count("pw_lo", 1))
            for g in range(4):
                pe.wait_ge(S("pooled_lo"), count("pooled_lo", g + 1))
                if g > 1:
                    pe.wait_ge(S("mixed_lo"), count("mixed_lo", g - 1))
                c = slice(g * P, (g + 1) * P)
                hi, lo = tile(pairB[0], g), tile(pairB[1], g)
                b = 4 + g % 2
                pe.matmul(ps[b][:], pw[0][:, c], hi, start=True, stop=False)
                pe.matmul(ps[b][:], pw[0][:, c], lo, start=False, stop=False)
                pe.matmul(ps[b][:], pw[1][:, c], hi, start=False, stop=True).then_inc(S("mix_done"), 1)
            for j in range(4):
                pe.wait_ge(S("conv_out"), count("conv_out", j + 1))
                last = pe.matmul(ps[6][:], ones[:], tile(CV, j), start=j == 0, stop=j == 3)
            last.then_inc(S("ln_mean"), 1)
            norm_pe(pe, "ln", 4)
            for i in range(2):
                for s in range(SLOTS):
                    unit_wait(pe, rnd(U_BRANCH, i), s)
                    if i + s == 0:
                        pe.wait_ge(S("mixed_lo"), count("mixed_lo", 4))
                        pe.wait_ge(S("cv_scaled"), count("cv_scaled", 4))
                    blocks(pe, s % 2, s, pairB, 4, 4, 0)
                    blocks(pe, 2 + s % 2, s, pairB, 0, 4, 4, wait=pair_wait("ln")(pe) if i + s == 0 else None)\
                        .then_inc(S(f"unit_done{s}"), 1)
            for i in range(2):
                for s in range(SLOTS):
                    unit(pe, rnd(U_WO, i), s, pairA, wait=pair_wait("br")(pe) if i + s == 0 else None)
            norm_pe(pe, "post0", bank=4)
            def mlp_group(g, first):
                for i in range(2):
                    for s in range(SLOTS):
                        begin = first and i + s == 0
                        unit(pe, rnd(U_MLP, g * 4 + i), s, pairA, wait=pair_wait("n1")(pe) if begin else None)
                        if begin:
                            norm_pe(pe, "n1")
                for i in range(2):
                    for s in range(SLOTS):
                        def wait_mid(k):
                            pe.wait_ge(S("mlp_hi"), count("mlp_hi", g * 8 + k + 1))
                            pe.wait_ge(S("mlp_lo"), count("mlp_lo", g * 8 + k + 1))
                        unit(pe, rnd(U_MLP, g * 4 + 2 + i), s, pairB, wait=wait_mid if i + s == 0 else None)
            mlp_group(0, True)
            with pe.Fori(1, 3) as g:
                mlp_group(g, False)
            mlp_group(3, False)
            norm_pe(pe, "post1", bank=4)
            second_block_pe(pe)

        @block.scalar
        def _(act):
            act.wait_ge(S("par_in"), count("par_in", 16))
            norm_act(act, "n0", "mix_pre", pairA, x_loaded)
            split_hi(act, 0, 0)
            split_hi(act, 0, 1)
            act.wait_ge(S("pw_in"), count("pw_in", 16))
            nc.scalar.activation(pw[0][:], pwraw, ACT.Copy).then_inc(S("pw_hi"), 1)

            def glu_round(i, first):
                for k in range(SLOTS):
                    ahead(act, split_hi, rnd(U_GLU, i), k)
                    if first and k == 0:
                        norm_row(act, "n0")
                    if k % 2:
                        act.wait_ge(S(f"evac{k}"), count(f"evac{k}", rnd(U_GLU, i) + 1))
                        nc.scalar.activation(TH, TG[:, 0:T], ACT.Tanh, scale=0.5).then_inc(S("glu_th"), 1)
            glu_round(0, True)
            glu_round(1, False)
            for k in range(SLOTS):
                ahead(act, split_hi, rnd(U_POOL, 0), k)
            act.wait_ge(S("glu_v"), count("glu_v", 4))

            def conv_tap(j, t):
                act.wait_ge(S("conv_acc"), count("conv_acc", j * (ACC_TAPS - 1) + (max(1, t - 2) if t >= 2 else 0)))
                nc.scalar.activation(CTMP[:, (t % 2) * T:(t % 2 + 1) * T], VP[:, bass.ds(j * VPW + t, T)],
                                     ACT.Copy, scale=par_col("conv_w", j * CONV_K + t)).then_inc(S("conv_tmp"), 1)

            def gate_round(i):
                for k in range(SLOTS):
                    ahead(act, split_hi, rnd(U_GATE, i), k)
                    for t in (2 * k, 2 * k + 1):
                        conv_tap(i, t)
                    act.wait_ge(S(f"evac{k}"), count(f"evac{k}", rnd(U_GATE, i) + 1))
                    nc.scalar.activation(SG[:, bass.ds((4 * i + k) * T, T)], TG[:, (k % 2) * T:(k % 2 + 1) * T],
                                         ACT.Tanh, scale=0.5).then_inc(S("gate_th"), 1)
            with act.Fori(0, 2) as i:
                gate_round(i)
            for g in range(4):
                act.wait_ge(S("pooled"), count("pooled", g + 1))
                nc.scalar.activation(tile(pairB[0], g), PO[g], ACT.Copy).then_inc(S("pooled_hi"), 1)
            act.wait_ge(S("pooled_lo"), count("pooled_lo", 4))
            with act.Fori(2, 4) as i:
                gate_round(i)
            for g in range(4):
                act.wait_ge(S("mix_done"), count("mix_done", g + 1))
                nc.scalar.activation(tile(pairB[0], 4 + g), ps[4 + g % 2][:], ACT.Copy,
                                     scale=par_col("pool_scale", g)).then_inc(S("mixed_hi"), 1)
            for j in range(4):
                act.wait_ge(S("cv_centred"), count("cv_centred", j + 1))
                square(act, "ln", j, tile(CV, j))
            for j in range(4):
                act.wait_ge(S("cv_scaled"), count("cv_scaled", j + 1))
                if j > 1:
                    act.wait_ge(S("ln_z"), count("ln_z", j - 1))
                nc.scalar.activation(TG[:, (j % 2) * T:(j % 2 + 1) * T], tile(CV, j), ACT.Identity,
                                     scale=half[:, j:j + 1], bias=half[:, 4 + j:5 + j]).then_inc(S("ln_y"), 1)
                act.wait_ge(S("ln_y"), count("ln_y", j + 1))
                nc.scalar.activation([VA, TH][j % 2], TG[:, (j % 2) * T:(j % 2 + 1) * T], ACT.Tanh)\
                    .then_inc(S("ln_th"), 1)
                act.wait_ge(S("ln_z"), count("ln_z", j + 1))
                nc.scalar.activation(tile(pairB[0], j), tile(CV, j), ACT.Copy).then_inc(S("ln_hi"), 1)
            act.wait_ge(S("ln_lo"), count("ln_lo", 4))
            act.dma_start(X[:], io["xT"]).then_inc(S("x_back"), 16)
            for i in range(2):
                for k in range(SLOTS):
                    ahead(act, split_hi, rnd(U_BRANCH, i), k)
                    m = 4 * i + k
                    act.wait_ge(S("br_sum"), count("br_sum", m + 1))
                    nc.scalar.activation(tile(pairA[0], m), CTMP[:, (k % 2) * T:(k % 2 + 1) * T], ACT.Copy)\
                        .then_inc(S("br_hi"), 1)
            act.wait_ge(S("br_lo"), count("br_lo", 8))
            for i in range(2):
                for k in range(SLOTS):
                    m = 4 * i + k
                    ahead(act, split_hi, rnd(U_WO, i), k)
                    evac_wait(act, rnd(U_WO, i), k)
                    nc.scalar.activation(tile(Y, m), ps[k % 2][:], ACT.Copy, scale=0.5).then_inc(S(f"evac{k}"), 1)
                    act.wait_ge(S(f"evac{k}"), count(f"evac{k}", rnd(U_WO, i) + 1))
                    square(act, "post0", m, tile(Y, m))
            norm_act(act, "n1", "mlp_pre", pairA, lambda e, m: e.wait_ge(S("x1"), count("x1", m + 1)))

            def mlp_group(g, first, last):
                for i in range(2):
                    for k in range(SLOTS):
                        r = rnd(U_MLP, g * 4 + i)
                        ahead(act, split_hi, r, k)
                        if first and i + k == 0:
                            norm_row(act, "n1")
                        n = g * 8 + 4 * i + k
                        evac_wait(act, r, k)
                        act.wait_ge(S("mlp_sq"), count("mlp_sq", n - 1))
                        nc.scalar.activation(TG[:, (k % 2) * T:(k % 2 + 1) * T], ps[k % 2][:], ACT.Relu)\
                            .then_inc(S(f"evac{k}"), 1)
                        act.wait_ge(S("mlp_sq"), count("mlp_sq", n + 1))
                        nc.scalar.activation(tile(pairB[0], 4 * i + k), MS[:, (k % 2) * T:(k % 2 + 1) * T], ACT.Copy)\
                            .then_inc(S("mlp_hi"), 1)
                for i in range(2):
                    for k in range(SLOTS):
                        ahead(act, split_hi, rnd(U_MLP, g * 4 + 2 + i), k)
                        if last:
                            act.wait_ge(S(f"evac{k}"), count(f"evac{k}", rnd(U_MLP, g * 4 + 2 + i) + 1))
                            square(act, "post1", 4 * i + k, tile(Y, 4 * i + k))
            mlp_group(0, True, False)
            with act.Fori(1, 3) as g:
                mlp_group(g, False, False)
            mlp_group(3, False, True)
            second_block_act(act)

        @block.vector
        def _(dve):
            v = nc.vector
            credit(dve, *(f"evac{s}" for s in range(SLOTS)))
            credit(dve, "mlp_sq", "conv_out", "t_lo", "d_o1", "d_o2")
            v.memset(ones[:], 1.0).then_inc(S("const"), 1)
            v.memset(mhalf[:, 0:NCH], -0.5)
            v.memset(mhalf[:, NCH:2 * NCH], 0.5).then_inc(S("const"), 1)
            v.memset(VP, 0.0).then_inc(S("zeros"), 1)
            dve.wait_ge(S("par_in"), count("par_in", 16))

            def par_range(name, n):
                return par[:, _cols[name][0]:_cols[name][0] + n]
            for at, name, n in ((0, "ln_g", 4), (4, "ln_b", 4), (8, "a_conv", 96)):
                v.tensor_scalar(half[:, at:at + n], par_range(name, n), 0.5, None, ALU.mult).then_inc(S("halved"), 1)
            dve.wait_ge(S("x_in"), count("x_in", 16))
            for m in range(KT):
                norm_lo(dve, "n0", "mix_pre", pairA, m)
            split_lo(dve, 0, 0)
            split_lo(dve, 0, 1)
            dve.wait_ge(S("pw_hi"), count("pw_hi", 1))
            v.tensor_tensor(pw[1][:], pwraw, pw[0][:].bitcast(F32), ALU.subtract).then_inc(S("pw_lo"), 1)
            token_mean(dve, "n0", 2, D)

            def glu_round(i, first):
                for k in range(SLOTS):
                    r = rnd(U_GLU, i)
                    ahead(dve, split_lo, r, k)
                    n = 2 * i + k // 2
                    if k % 2 == 0:
                        if first and k == 0:
                            dve.wait_ge(S("n0_R"), count("n0_R", 1))
                            dve.wait_ge(S("zeros"), count("zeros", 1))
                        evacuate(dve, r, k, VA, 0.5, R[:])
                    else:
                        evacuate(dve, r, k, TG[:, 0:T], 1.0, R[:])
                        dve.wait_ge(S("glu_th"), count("glu_th", n + 1))
                        at = n * VPW + CONV_K - 1
                        v.scalar_tensor_tensor(out=VP[:, at:at + T], in0=TH, scalar=1.0, in1=VA,
                                               op0=ALU.add, op1=ALU.mult).then_inc(S("glu_v"), 1)
                        dve.wait_ge(S("glu_v"), count("glu_v", n + 1))
            glu_round(0, True)
            glu_round(1, False)
            for u in UP:
                v.memset(u[:, 0:16], 0.0).then_inc(S("zeros"), 1)
            for k in range(SLOTS):
                r = rnd(U_POOL, 0)
                ahead(dve, split_lo, r, k)
                if k > 1:
                    dve.wait_ge(S("pooled"), count("pooled", k - 1))
                evacuate(dve, r, k, UP[k % 2][:, 16:UPW], 1.0, R[:])

            def gate_round(i):
                for k in range(SLOTS):
                    r = rnd(U_GATE, i)
                    ahead(dve, split_lo, r, k)
                    dve.wait_ge(S("gate_th"), count("gate_th", 4 * i + k - 1))
                    evacuate(dve, r, k, TG[:, (k % 2) * T:(k % 2 + 1) * T], 1.0, R[:])
                    for t in range(ACC_TAPS + (k * 23 + 3) // 4, ACC_TAPS + ((k + 1) * 23 + 3) // 4):
                        if t >= CONV_K:
                            continue
                        x = VP[:, bass.ds(i * VPW + t, T)]
                        w = par_col("conv_w", i * CONV_K + t)
                        n = i * 23 + t - ACC_TAPS
                        if t == ACC_TAPS:
                            v.tensor_scalar(tile(CV, i), x, w, par_col("conv_b", i), ALU.mult, ALU.add)\
                                .then_inc(S("conv_step"), 1)
                        else:
                            dve.wait_ge(S("conv_step"), count("conv_step", n))
                            v.scalar_tensor_tensor(out=tile(CV, i), in0=x, scalar=w, in1=tile(CV, i),
                                                   op0=ALU.mult, op1=ALU.add).then_inc(S("conv_step"), 1)
                dve.wait_ge(S("conv_step"), count("conv_step", 23 * (i + 1)))
                dve.wait_ge(S("conv_acc"), count("conv_acc", (ACC_TAPS - 1) * (i + 1)))
                v.tensor_tensor(tile(CV, i), tile(CV, i), CVB, ALU.add).then_inc(S("conv_out"), 1)
            with dve.Fori(0, 4) as i:
                gate_round(i)
            for g in range(4):
                dve.wait_ge(S("mixed_hi"), count("mixed_hi", g + 1))
                v.scalar_tensor_tensor(out=tile(pairB[1], 4 + g), in0=ps[4 + g % 2][:], scalar=par_col("pool_scale", g),
                                       in1=tile(pairB[0], 4 + g).bitcast(F32), op0=ALU.mult, op1=ALU.subtract)\
                    .then_inc(S("mixed_lo"), 1)
            dve.wait_ge(S("ln_mean"), count("ln_mean", 1))
            for j in range(4):
                v.scalar_tensor_tensor(out=tile(CV, j), in0=ps[6][:], scalar=-1.0 / (4 * P), in1=tile(CV, j),
                                       op0=ALU.mult, op1=ALU.add).then_inc(S("cv_centred"), 1)
            token_mean(dve, "ln", 2, 4 * P)
            dve.wait_ge(S("ln_row"), count("ln_row", 1))
            for j in range(4):
                dve.wait_ge(S("ln_sq"), count("ln_sq", j + 1))
                v.tensor_tensor(tile(CV, j), tile(CV, j), ps[3][:], ALU.mult).then_inc(S("cv_scaled"), 1)
            for j in range(4):
                dve.wait_ge(S("ln_th"), count("ln_th", j + 1))
                v.scalar_tensor_tensor(out=tile(CV, j), in0=[VA, TH][j % 2], scalar=1.0,
                                       in1=TG[:, (j % 2) * T:(j % 2 + 1) * T], op0=ALU.add, op1=ALU.mult)\
                    .then_inc(S("ln_z"), 1)
                dve.wait_ge(S("ln_hi"), count("ln_hi", j + 1))
                v.tensor_tensor(tile(pairB[1], j), tile(CV, j), tile(pairB[0], j).bitcast(F32), ALU.subtract)\
                    .then_inc(S("ln_lo"), 1)
            for i in range(2):
                for k in range(SLOTS):
                    r = rnd(U_BRANCH, i)
                    m = 4 * i + k
                    ahead(dve, split_lo, r, k)
                    evac_wait(dve, r, k)
                    if m > 1:
                        dve.wait_ge(S("br_lo"), count("br_lo", m - 1))
                    half_sum = CTMP[:, (k % 2) * T:(k % 2 + 1) * T]
                    v.scalar_tensor_tensor(out=half_sum, in0=tile(SG, m), scalar=1.0, in1=ps[k % 2][:],
                                           op0=ALU.add, op1=ALU.mult).then_inc(S("br_part"), 1)
                    v.scalar_tensor_tensor(out=VA, in0=tile(SG, 8 + m), scalar=1.0, in1=ps[2 + k % 2][:],
                                           op0=ALU.add, op1=ALU.mult).then_inc(S(f"evac{k}"), 1)
                    dve.wait_ge(S("br_part"), count("br_part", m + 1))
                    dve.wait_ge(S(f"evac{k}"), count(f"evac{k}", r + 1))
                    v.tensor_tensor(half_sum, half_sum, VA, ALU.add).then_inc(S("br_sum"), 1)
                    dve.wait_ge(S("br_sum"), count("br_sum", m + 1))
            for i in range(2):
                for k in range(SLOTS):
                    ahead(dve, split_lo, rnd(U_WO, i), k)

            def add_normed(tag, xtag, g, bank):
                dve.wait_ge(S(tag + "_row"), count(tag + "_row", 1))
                for m in range(KT):
                    t = TG[:, (m % 2) * T:(m % 2 + 1) * T]
                    if m > 1:
                        dve.wait_ge(S(xtag), count(xtag, m - 1))
                    v.scalar_tensor_tensor(out=t, in0=tile(Y, m), scalar=par_col(g, m), in1=ps[bank][:],
                                           op0=ALU.mult, op1=ALU.mult).then_inc(S(tag + "_t"), 1)
                    dve.wait_ge(S(tag + "_t"), count(tag + "_t", m + 1))
                    v.tensor_tensor(tile(X, m), tile(X, m), t, ALU.add).then_inc(S(xtag), 1)
            dve.wait_ge(S("post0_ss"), count("post0_ss", 8))
            token_mean(dve, "post0", 4, D)
            dve.wait_ge(S("x_back"), count("x_back", 16))
            add_normed("post0", "x1", "mix_post", 5)
            for m in range(KT):
                dve.wait_ge(S("x1"), count("x1", m + 1))
                norm_lo(dve, "n1", "mlp_pre", pairA, m)
            token_mean(dve, "n1", 2, D)

            def mlp_group(g, first):
                for i in range(2):
                    for k in range(SLOTS):
                        ahead(dve, split_lo, rnd(U_MLP, g * 4 + i), k)
                        n = g * 8 + 4 * i + k
                        dve.wait_ge(S(f"evac{k}"), count(f"evac{k}", rnd(U_MLP, g * 4 + i) + 1))
                        t = TG[:, (k % 2) * T:(k % 2 + 1) * T]
                        if not (first and 4 * i + k < 2):
                            dve.wait_ge(S("mlp_lo"), count("mlp_lo", n - 1))
                        v.tensor_tensor(MS[:, (k % 2) * T:(k % 2 + 1) * T], t, t, ALU.mult).then_inc(S("mlp_sq"), 1)
                for i in range(2):
                    for k in range(SLOTS):
                        r = rnd(U_MLP, g * 4 + 2 + i)
                        m = 4 * i + k
                        ahead(dve, split_lo, r, k)
                        evac_wait(dve, r, k)
                        if first:
                            v.tensor_copy(tile(Y, m), ps[k % 2][:]).then_inc(S(f"evac{k}"), 1)
                        else:
                            v.tensor_tensor(tile(Y, m), ps[k % 2][:], tile(Y, m), ALU.add).then_inc(S(f"evac{k}"), 1)
            mlp_group(0, True)
            with dve.Fori(1, 3) as g:
                mlp_group(g, False)
            mlp_group(3, False)
            r1, r2, r4 = tok[:, NCH:2 * NCH], tok[:, 8:12], tok[:, 12:16]
            v.tensor_tensor(r2, r1, r1, ALU.mult).then_inc(S("r_power"), 1)
            dve.wait_ge(S("r_power"), count("r_power", 1))
            v.tensor_tensor(r4, r2, r2, ALU.mult).then_inc(S("r_power"), 1)
            dve.wait_ge(S("r_power"), count("r_power", 2))
            dve.wait_ge(S("post1_sum"), count("post1_sum", 1))
            v.scalar_tensor_tensor(out=tok[:, 16:20], in0=ps[4][:, 0:NCH], scalar=1.0 / D, in1=r4,
                                   op0=ALU.mult, op1=ALU.mult).then_inc(S("r_power"), 1)
            dve.wait_ge(S("r_power"), count("r_power", 3))
            v.tensor_scalar(tok[:, 0:NCH], tok[:, 16:20], EPS, None, ALU.add).then_inc(S("post1_ms"), 1)
            add_normed("post1", "x2", "mlp_post", 5)
            second_block_dve(dve)

        @block.gpsimd
        def _(pool):
            g_ = nc.gpsimd
            credit(pool, "conv_acc", "o_lo")
            pool.sem_inc(S("gate_th"), CREDIT["gate_th"])
            pool.wait_ge(S("const"), count("const", 2))
            pool.wait_ge(S("cst_in"), count("cst_in", 16))
            sum_squares(pool, "n0", KT)
            token_rsqrt(pool, "n0")
            step = 0
            for g, window in enumerate(POOL_WINDOWS):
                u = UP[g % 2]
                pool.wait_ge(S(f"evac{g}"), count(f"evac{g}", rnd(U_POOL, 0) + 1))
                pool.wait_ge(S("zeros"), count("zeros", 3))
                src, shift = u, 1
                while shift < window:
                    dst = PAB[step % 2]
                    lo = 2 * shift - 1
                    if step:
                        pool.wait_ge(S("pool_step"), count("pool_step", step))
                    g_.tensor_tensor(dst[:, lo:UPW], src[:, lo:UPW], src[:, lo - shift:UPW - shift], ALU.add)\
                        .then_inc(S("pool_step"), 1)
                    step += 1
                    src, shift = dst, 2 * shift
                pool.wait_ge(S("pool_step"), count("pool_step", step))
                dst = PAB[step % 2]
                g_.tensor_scalar(dst[:, 16:UPW], src[:, 16:UPW], 1.0 / window, 0.0, ALU.mult, ALU.add)\
                    .then_inc(S("pool_step"), 1)
                step += 1
                pool.wait_ge(S("pool_step"), count("pool_step", step))
                inv = cst[:, C_INV + 16 * g:C_INV + 16 * (g + 1)]
                g_.tensor_tensor(dst[:, 16:32], src[:, 16:32], inv, ALU.mult).then_inc(S("pool_step"), 1)
                step += 1
                pool.wait_ge(S("pool_step"), count("pool_step", step))
                g_.tensor_tensor(PO[g], dst[:, 16:UPW], u[:, 16:UPW], ALU.subtract).then_inc(S("pooled"), 1)
                pool.wait_ge(S("pooled"), count("pooled", g + 1))

            def conv_sum(i):
                for t in range(1, ACC_TAPS):
                    pool.wait_ge(S("conv_tmp"), count("conv_tmp", ACC_TAPS * i + t + 1))
                    tmp = CTMP[:, (t % 2) * T:(t % 2 + 1) * T]
                    if t == 1:
                        pool.wait_ge(S("conv_out"), count("conv_out", i))
                    else:
                        pool.wait_ge(S("conv_acc"), count("conv_acc", (ACC_TAPS - 1) * i + t - 1))
                    g_.tensor_tensor(CVB, CTMP[:, 0:T] if t == 1 else CVB, tmp, ALU.add).then_inc(S("conv_acc"), 1)
            with pool.Fori(0, 2) as i:
                conv_sum(i)
            for g in range(4):
                pool.wait_ge(S("pooled_hi"), count("pooled_hi", g + 1))
                g_.tensor_tensor(tile(pairB[1], g), PO[g], tile(pairB[0], g).bitcast(F32), ALU.subtract)\
                    .then_inc(S("pooled_lo"), 1)
            with pool.Fori(2, 4) as i:
                conv_sum(i)
            sum_squares(pool, "ln", 4)
            token_rsqrt(pool, "ln")

            def lo_part(tag, m, src, dst, ready=None):
                pool.wait_ge(S(tag + "_hi"), count(tag + "_hi", ready if ready is not None else m + 1))
                g_.tensor_tensor(tile(dst[1], m), src, tile(dst[0], m).bitcast(F32), ALU.subtract)\
                    .then_inc(S(tag + "_lo"), 1)
            for m in range(8):
                lo_part("br", m, CTMP[:, (m % 2) * T:(m % 2 + 1) * T], pairA)
            sum_squares(pool, "post0", KT)
            token_rsqrt(pool, "post0")
            sum_squares(pool, "n1", KT)
            token_rsqrt(pool, "n1")
            with pool.Fori(0, 4) as g:
                for m in range(8):
                    lo_part("mlp", m, MS[:, (m % 2) * T:(m % 2 + 1) * T], pairB, g * 8 + m + 1)
            sum_squares(pool, "post1", KT)
            pool.wait_ge(S("post1_ms"), count("post1_ms", 1))
            g_.tensor_tensor(tok[:, 20:24], tok[:, 0:NCH], mhalf[:, 0:NCH], ALU.pow).then_inc(S("post1_pow"), 1)
            pool.wait_ge(S("post1_pow"), count("post1_pow", 1))
            g_.tensor_tensor(tok[:, NCH:2 * NCH], tok[:, 20:24], tok[:, 8:12], ALU.mult).then_inc(S("post1_rt"), 1)
            second_block_pool(pool)


def _blocks(w, k0, n, m):
    b = w[k0 * P:(k0 + n) * P, m * P:(m + 1) * P].reshape(n, P, P)
    return b.transpose(1, 0, 2).reshape(P, n * P)


def _pack(inp):
    f = np.float32
    ws = np.zeros((U_END, P, 1024), f)
    at = [0]

    def put(*parts):
        a = np.concatenate(parts, axis=1)
        ws[at[0], :, :a.shape[1]] = a
        at[0] += 1
    w_in = inp["w_in"][0]
    for j in range(4):
        put(_blocks(w_in, 0, 8, 4 + j))
        put(_blocks(w_in, 0, 8, 8 + j))
    for j in range(4):
        put(_blocks(w_in, 0, 8, j))
    for j in range(16):
        put(_blocks(w_in, 0, 8, 12 + j))
    for m in range(8):
        put(_blocks(inp["w_pool_out"][0], 0, 4, m), _blocks(inp["w_conv_out"][0], 0, 4, m))
    for m in range(8):
        put(_blocks(inp["w_o"][0], 0, 8, m))
    for g in range(4):
        for m in range(8):
            put(_blocks(inp["w_up"][0], 0, 8, 8 * g + m))
        for m in range(8):
            put(_blocks(inp["w_down"][0], 8 * g, 8, m))
    a_in = inp["a_w_in_2"][0]
    for h in range(HEADS):
        for part in range(4):
            put(_blocks(a_in, 0, 8, 8 * part + h))
    for m in range(8):
        put(_blocks(inp["a_w_out_2"][0], 0, 8, m))

    def ffn(layer):
        up, down = inp["f_w_up_2"][layer], inp["f_w_down_2"][layer]
        first = 0
        for n in MID_GROUPS:
            for m in range(first, first + n):
                put(_blocks(up, 0, 8, m))
                put(_blocks(up, 0, 8, 22 + m))
            for m in range(8):
                put(_blocks(down, first, n, m))
            first += n
    ffn(0)
    for m in range(4):
        put(_blocks(inp["kv_w_2"], 0, 8, m))
    heads = [h for pair in ATT_TILE_HEADS for h in pair]
    by_head = lambda w, axis: np.concatenate(
        [np.take(w, range(64 * h, 64 * h + 64), axis=axis) for h in heads], axis=axis)
    wq = by_head(inp["b_w_q_2"][0], 1)
    for m in range(8):
        put(_blocks(wq, 0, 8, m))
    wo = by_head(inp["b_w_o_2"][0], 0)
    for m in range(8):
        put(_blocks(wo, 0, 8, m))
    ffn(1)
    assert at[0] == U_END, at

    par = np.zeros((P, NPAR), f)

    def col(name, vec):
        c, n = _cols[name]
        par[:, c:c + n] = np.asarray(vec).reshape(n, P).T
    for name, key in (("mix_pre", "norm_mix_pre"), ("mix_post", "norm_mix_post"), ("mlp_pre", "norm_mlp_pre"),
                      ("mlp_post", "norm_mlp_post"), ("a_norm", "a_norm_2"), ("kv_norm", "kv_norm_2"),
                      ("b_norm", "b_norm_2"), ("final", "final_norm_2"), ("pool_scale", "pool_scale"),
                      ("conv_b", "conv_b"), ("ln_g", "conv_ln_g"), ("ln_b", "conv_ln_b"), ("onorm", "a_onorm_2"),
                      ("kv_b", "kv_b_2"), ("b_o", "b_b_o_2")):
        col(name, inp[key])
    col("b_q", by_head(inp["b_b_q_2"][0], 0))
    for layer in range(2):
        col(f"f_norm{layer}", inp["f_norm_2"][layer])
        col(f"f_bias{layer}", inp["f_conv_b_2"][layer])

    def taps(name, w):
        c, n = _cols[name]
        par[:, c:c + n] = w.reshape(w.shape[0], -1, P).transpose(2, 1, 0).reshape(P, n)
    taps("conv_w", inp["conv_w"][0])
    taps("a_conv", inp["a_conv_w_2"][0])
    taps("f_conv0", inp["f_conv_w_2"][0])
    taps("f_conv1", inp["f_conv_w_2"][1])

    cst = np.zeros((P, NCONST), f)
    i, j = np.arange(P)[:, None], np.arange(P)[None, :]
    cst[:, C_ID:C_ID + P] = i == j
    cst[:, C_TRI:C_TRI + P] = i <= j
    cst[:, C_NEG:C_NEG + P] = np.where(j >= i, 0, -FAR)
    for lvl in range(7):
        m = (i >> (lvl + 1) == j >> (lvl + 1)) & ((i >> lvl) & 1 == 1) & ((j >> lvl) & 1 == 0)
        cst[:, C_LVL + lvl * P:C_LVL + (lvl + 1) * P] = m.T if lvl == 0 else m
    dist = i + P - np.arange(2 * P)[None, :]
    cst[:, C_DIST:C_DIST + 2 * P] = np.where((dist >= 0) & (dist < P), dist, FAR)
    for g, window in enumerate(POOL_WINDOWS):
        cst[:, C_INV + 16 * g:C_INV + 16 * g + 16] = 1.0 / np.minimum(np.arange(16) + 1, window)
    slopes = (2.0 ** (-8.0 * np.arange(1, 17) / 16)).astype(f)
    row = np.concatenate([inp["a_A_log_2"][0], inp["a_dt_bias_2"][0], inp["b_sinks_2"][0][heads], -slopes[heads]])
    return {
        "xT": np.asarray(inp["x"])[0].T.reshape(KT, P, T).transpose(1, 0, 2).reshape(P, KT * T),
        "ws": ws, "par": par, "cst": cst,
        "pw": np.asarray(inp["pool_w"])[0].transpose(1, 0, 2).reshape(P, 4 * P),
        "tail": a_in[:, 4 * D:].reshape(KT, P, 16).transpose(1, 0, 2).reshape(P, KT * 16),
        "row": row.reshape(1, 48),
    }


def kernel(**inputs):
    import concourse.bacc as bacc
    from concourse.bass_utils import run_bass_kernel_spmd

    packed = {k: np.ascontiguousarray(v) for k, v in _pack({k: np.asarray(v) for k, v in inputs.items()}).items()}
    nc = bacc.Bacc("TRN2", target_bir_lowering=False, num_devices=1)
    io = {k: nc.dram_tensor("d_" + k, v.shape, F32, kind="ExternalInput").ap() for k, v in packed.items()}
    io["out"] = nc.dram_tensor("d_out", (P, KT * T), F32, kind="ExternalOutput").ap()
    build(nc, io)
    r = run_bass_kernel_spmd(nc, [{"d_" + k: v for k, v in packed.items()}], core_ids=[0])
    out = r.results[0]["d_out"]
    return out.reshape(P, KT, T).transpose(2, 1, 0).reshape(1, T, D)
```

```python
from contextlib import ExitStack

import numpy as np

import concourse.bass as bass
from concourse import mybir
from concourse.alu_op_type import AluOpType as ALU

ACT = mybir.ActivationFunctionType
F32 = mybir.dt.float32
F32R = mybir.dt.float32r

P = 128
T = 512
NCH = T // P
D = 1024
KT = D // P
EPS = 1e-6
CONV_K = 31
FPAD = 2
APAD = 3
HEADS = 8
SLOTS = 4
LEAD = 2
ACC_TAPS = 11
DVE_TAPS = CONV_K - ACC_TAPS

U_GLU = 0
U_POOL = U_GLU + 8
U_GATE = U_POOL + 4
U_BRANCH = U_GATE + 16
U_WO = U_BRANCH + 8
U_MLP = U_WO + 8
U_DELTA = U_MLP + 64
U_AOUT = U_DELTA + 32
U_FFN0 = U_AOUT + 8
MID_GROUPS = (8, 8, 6)
U_KV = U_FFN0 + sum(2 * g + 8 for g in MID_GROUPS)
U_Q = U_KV + 4
U_BO = U_Q + 8
U_FFN1 = U_BO + 8
U_END = U_FFN1 + sum(2 * g + 8 for g in MID_GROUPS)

_cols = {}
_n = 0
for _name, _width in (
    ("mix_pre", KT), ("mix_post", KT), ("mlp_pre", KT), ("mlp_post", KT), ("a_norm", KT), ("kv_norm", KT),
    ("b_norm", KT), ("f_norm0", KT), ("f_norm1", KT), ("final", KT),
    ("pool_scale", 4), ("conv_w", 4 * CONV_K), ("conv_b", 4), ("ln_g", 4), ("ln_b", 4),
    ("a_conv", 24 * 4), ("onorm", 1), ("b_q", 8), ("kv_b", 4), ("b_o", 8),
    ("f_conv0", 44 * 3), ("f_bias0", 44), ("f_conv1", 44 * 3), ("f_bias1", 44),
):
    _cols[_name] = (_n, _width)
    _n += _width
NPAR = _n

C_ID = 0
C_TRI = C_ID + P
C_NEG = C_TRI + P
C_LVL = C_NEG + P
C_DIST = C_LVL + 7 * P
C_INV = C_DIST + 2 * P
NCONST = C_INV + 4 * 16
POOL_WINDOWS = (2, 4, 8, 16)
FAR = 1e30
ATT_TILE_HEADS = [(4 * (2 * a) + r, 4 * (2 * a + 1) + r) for r in range(4) for a in range(2)]


def build(nc, io):
    with ExitStack() as ctx:
        def sb(name, cols, dt=F32):
            return ctx.enter_context(nc.sbuf_tensor(name, [P, cols], dt))

        sems = {}

        NORMS = {}
        count = {"one": 0, "ss": 0, "hi": 0}
        for tag, squared, split in (("n0", 8, 8), ("ln", 4, 4), ("post0", 8, 0), ("n1", 8, 8), ("post1", 8, 0),
                                    ("na", 8, 8), ("nf0", 8, 8), ("kv", 8, 8), ("bn", 0, 8), ("n_f1", 8, 8),
                                    ("fin", 8, 0)):
            NORMS[tag] = dict(count)
            NORMS[tag]["R"] = count.get("R", 0)
            count["one"] += squared > 0
            count["ss"] += squared
            count["hi"] += split
            count["R"] = NORMS[tag]["R"] + (tag in ("n0", "n1", "na", "nf0", "kv", "n_f1"))
        KINDS = {"hi": "hi", "lo": "hi", "sq": "ss", "ss": "ss", "sum": "one", "ms": "one", "rt": "one", "row": "one",
                 "R": "R"}
        FFN_STEPS = dict(half=2, pad=2, c0=44, tap=88, th=22, gate=22, prod=22, hi=22, lo=22)

        def shared(name):
            tag, _, kind = name.rpartition("_")
            if tag in NORMS and kind in KINDS:
                return "norm_" + kind, NORMS[tag][KINDS[kind]]
            if tag in ("f0", "f1") and kind in FFN_STEPS:
                return "ffn_" + kind, FFN_STEPS[kind] if tag == "f1" else 0
            return name, 0

        def S(name):
            name = shared(name)[0]
            if name not in sems:
                sems[name] = ctx.enter_context(nc.semaphore(name))
            return sems[name]

        X = sb("X", KT * T)
        pairA = (sb("A_hi", KT * T, F32R), sb("A_lo", KT * T, F32R))
        pairB = (sb("B_hi", KT * T, F32R), sb("B_lo", KT * T, F32R))
        Y = sb("Y", KT * T)
        raw = sb("w_raw", SLOTS * 1024)
        w_hi = sb("w_hi", SLOTS * 1024, F32R)
        w_lo = sb("w_lo", SLOTS * 1024, F32R)
        par = sb("par", NPAR)
        half = sb("half", 8 + 96 + 22 * 3 + 22)
        cst = sb("cst", NCONST)
        ones = sb("ones", P)
        mhalf = sb("mhalf", 2 * NCH)
        R = sb("R", T)
        SQ = sb("SQ", 2 * T)
        SS = sb("SS", T)
        tok = sb("tok", 64)
        NSCR = 10260
        scr = sb("scr", NSCR)
        small = sb("small", 48 + KT * 16)
        rowp, tailw = small[:, 0:48], small[:, 48:48 + KT * 16]
        pw = (sb("pw_hi", 512, F32R), sb("pw_lo", 512, F32R))
        ps = [ctx.enter_context(nc.psum_tensor(f"ps{b}", [P, 512], F32)) for b in range(8)]

        def par_col(name, k=0):
            c = _cols[name][0] + k
            return par[:, c:c + 1] if isinstance(c, int) else par[:, bass.ds(c, 1)]

        def tile(buf, m, n=1):
            return buf[:, m * T:(m + n) * T] if isinstance(m, int) else buf[:, bass.ds(m * T, n * T)]

        ident = cst[:, C_ID:C_ID + P]
        tri = cst[:, C_TRI:C_TRI + P]

        TW = (pw[0][:, 0:KT * 16], pw[1][:, 0:KT * 16])

        o = 0

        def carve(n):
            nonlocal o
            o += n
            assert o <= NSCR, (o, NSCR)
            return scr[:, o - n:o]

        SG = carve(16 * T)
        UPW = T + 16
        VATH = carve(2 * T)
        VA, TH = VATH[:, 0:T], VATH[:, T:2 * T]
        TG = carve(2 * T)
        UP = [X[:, 4 * T + 2 * UPW:4 * T + 3 * UPW], VATH[:, 0:UPW]]
        pwraw = SG[:, 0:512]
        PO = [SG[:, (8 + g) * T:(9 + g) * T] for g in range(4)]
        VPW = T + CONV_K - 1
        VP = Y[:, 0:4 * VPW]
        CVB = Y[:, 4 * VPW:4 * VPW + T]
        CTMP = Y[:, 4 * VPW + T:4 * VPW + 3 * T]
        CVC = SQ[:, 0:T]
        CV = X[:, 0:4 * T]
        PAB = [X[:, 4 * T:4 * T + UPW], X[:, 4 * T + UPW:4 * T + 2 * UPW]]
        HS = [tile(Y, m) for m in range(4)] + [tile(X, m) for m in range(4, 8)]
        MS = SG[:, 0:2 * T]
        assert 4 * VPW + 3 * T <= KT * T

        block = ctx.enter_context(nc.Block())

        CREDIT = {"o_lo": 1, "t_lo": 1, "d_o1": 1, "d_o2": 1, "d_os": 1}
        for s in range(SLOTS):
            CREDIT[f"unit_done{s}"] = 1
            CREDIT[f"evac{s}"] = 1
        for name in ("mlp_sq", "conv_acc", "conv_out", "gate_th"):
            CREDIT[name] = 4

        def count(name, n):
            return n + CREDIT.get(name, 0) + shared(name)[1]

        def credit(eng, *names):
            for name in names:
                eng.sem_inc(S(name), CREDIT[name])

        def rnd(base, i):
            assert base % SLOTS == 0
            return base // SLOTS + i

        def split_hi(act, r, s):
            act.wait_ge(S(f"raw_in{s}"), 16 * (r + 1))
            act.wait_ge(S(f"unit_done{s}"), count(f"unit_done{s}", r))
            c = slice(s * 1024, (s + 1) * 1024)
            nc.scalar.activation(w_hi[:, c], raw[:, c], ACT.Copy).then_inc(S(f"w_hi{s}"), 1)

        def split_lo(dve, r, s):
            dve.wait_ge(S(f"w_hi{s}"), count(f"w_hi{s}", r + 1))
            c = slice(s * 1024, (s + 1) * 1024)
            nc.vector.tensor_tensor(w_lo[:, c], raw[:, c], w_hi[:, c].bitcast(F32), ALU.subtract)\
                .then_inc(S(f"w_lo{s}"), 1)

        def ahead(eng, split, r, k):
            split(eng, r + (k + LEAD) // SLOTS, (k + LEAD) % SLOTS)

        def unit_wait(pe, r, s):
            pe.wait_ge(S(f"w_hi{s}"), count(f"w_hi{s}", r + 1))
            pe.wait_ge(S(f"w_lo{s}"), count(f"w_lo{s}", r + 1))
            pe.wait_ge(S(f"evac{(s + 2) % SLOTS}"), count(f"evac{(s + 2) % SLOTS}", r + 1 if s >= 2 else r))

        def blocks(pe, bank, s, pair, first, n, at=0, wait=None):
            for k in range(n):
                if wait:
                    wait(k)
                c = slice(s * 1024 + (at + k) * P, s * 1024 + (at + k + 1) * P)
                hi, lo = tile(pair[0], first + k), tile(pair[1], first + k)
                pe.matmul(ps[bank][:], w_hi[:, c], hi, start=k == 0, stop=False)
                pe.matmul(ps[bank][:], w_hi[:, c], lo, start=False, stop=False)
                last = pe.matmul(ps[bank][:], w_lo[:, c], hi, start=False, stop=k == n - 1)
            return last

        def part_blocks(pe, bank, s, pair, first, end, total=KT, wait=None):
            for k in range(first, end):
                if wait:
                    wait(k)
                c = slice(s * 1024 + k * P, s * 1024 + (k + 1) * P)
                hi, lo = tile(pair[0], k), tile(pair[1], k)
                pe.matmul(ps[bank][:], w_hi[:, c], hi, start=k == 0, stop=False)
                pe.matmul(ps[bank][:], w_hi[:, c], lo, start=False, stop=False)
                last = pe.matmul(ps[bank][:], w_lo[:, c], hi, start=False, stop=k == total - 1)
            return last

        def two_units(pe, r, pair, wait, late, n=KT, norm=None):
            for s in range(2):
                unit_wait(pe, r, s)
                part_blocks(pe, s, s, pair, 0, n - late, n, wait)
            part_blocks(pe, 0, 0, pair, n - late, n, n, wait).then_inc(S("unit_done0"), 1)
            if norm:
                token_sums(pe, norm, KT, 2)
            part_blocks(pe, 1, 1, pair, n - late, n, n, wait).then_inc(S("unit_done1"), 1)
            if norm:
                pe.wait_ge(S(norm + "_rt"), count(norm + "_rt", 1))
                spread(pe, tok[:, NCH:2 * NCH], 3).then_inc(S(norm + "_row"), 1)

        def unit(pe, r, s, pair, n=KT, wait=None):
            unit_wait(pe, r, s)
            blocks(pe, s % 2, s, pair, 0, n, wait=wait).then_inc(S(f"unit_done{s}"), 1)

        def evac_wait(eng, r, s):
            eng.wait_ge(S(f"unit_done{s}"), count(f"unit_done{s}", r + 1))

        def norm_act(act, tag, g, pair, xready, splits=False):
            for m in range(KT):
                if splits and m in (1, 3):
                    split_hi(act, 0, m // 2)
                xready(act, m)
                nc.scalar.activation(tile(pair[0], m), tile(X, m), ACT.Copy, scale=par_col(g, m))\
                    .then_inc(S(tag + "_hi"), 1)
                square(act, tag, m, tile(X, m))

        def square(act, tag, m, src, scale=1.0):
            if m > 1:
                act.wait_ge(S(tag + "_ss"), count(tag + "_ss", m - 1))
            nc.scalar.activation(tile(SQ, m % 2), src, ACT.Square, scale=scale).then_inc(S(tag + "_sq"), 1)

        def norm_lo(dve, tag, g, pair, m):
            dve.wait_ge(S(tag + "_hi"), count(tag + "_hi", m + 1))
            nc.vector.scalar_tensor_tensor(out=tile(pair[1], m), in0=tile(X, m), scalar=par_col(g, m),
                                           in1=tile(pair[0], m).bitcast(F32), op0=ALU.mult, op1=ALU.subtract)\
                .then_inc(S(tag + "_lo"), 1)

        def sum_squares(pool, tag, n):
            for m in range(n):
                pool.wait_ge(S(tag + "_sq"), count(tag + "_sq", m + 1))
                if m == 0:
                    nc.gpsimd.tensor_copy(SS[:], tile(SQ, 0)).then_inc(S(tag + "_ss"), 1)
                else:
                    pool.wait_ge(S(tag + "_ss"), count(tag + "_ss", m))
                    nc.gpsimd.tensor_tensor(SS[:], SS[:], tile(SQ, m % 2), ALU.add).then_inc(S(tag + "_ss"), 1)

        def token_sums(pe, tag, n, bank):
            pe.wait_ge(S(tag + "_ss"), count(tag + "_ss", n))
            for c in range(NCH):
                last = pe.matmul(ps[bank][:, c:c + 1], SS[:, c * P:(c + 1) * P], ones[:, 0:1], start=True, stop=True)
            last.then_inc(S(tag + "_sum"), 1)

        def token_mean(dve, tag, bank, n):
            dve.wait_ge(S(tag + "_sum"), count(tag + "_sum", 1))
            nc.vector.tensor_scalar(tok[:, 0:NCH], ps[bank][:, 0:NCH], 1.0 / n, EPS, ALU.mult, ALU.add)\
                .then_inc(S(tag + "_ms"), 1)

        def token_rsqrt(pool, tag):
            pool.wait_ge(S(tag + "_ms"), count(tag + "_ms", 1))
            nc.gpsimd.tensor_tensor(tok[:, NCH:2 * NCH], tok[:, 0:NCH], mhalf[:, 0:NCH], ALU.pow)\
                .then_inc(S(tag + "_rt"), 1)

        def spread(pe, src, bank):
            for c in range(NCH):
                last = pe.matmul(ps[bank][:, c * P:(c + 1) * P], src[:, c:c + 1].broadcast_to([P, P]), ident,
                                 start=True, stop=True)
            return last

        def norm_pe(pe, tag, n=KT, bank=2):
            token_sums(pe, tag, n, bank)
            pe.wait_ge(S(tag + "_rt"), count(tag + "_rt", 1))
            spread(pe, tok[:, NCH:2 * NCH], bank + 1).then_inc(S(tag + "_row"), 1)

        def norm_row(act, tag, bank=2):
            act.wait_ge(S(tag + "_row"), count(tag + "_row", 1))
            nc.scalar.activation(R[:], ps[bank + 1][:], ACT.Copy).then_inc(S(tag + "_R"), 1)

        def pair_wait(tag):
            def wait(pe):
                def at(k):
                    pe.wait_ge(S(tag + "_hi"), count(tag + "_hi", k + 1))
                    pe.wait_ge(S(tag + "_lo"), count(tag + "_lo", k + 1))
                return at
            return wait

        def x_loaded(eng, m):
            eng.wait_ge(S(f"x_in{m // 2}"), 16)

        o = 0
        yo = 0

        def carve_y(n):
            nonlocal yo
            yo += n
            assert yo <= KT * T
            return Y[:, yo - n:yo]
        AU = [carve(T + APAD + 1) for _ in range(2)]
        AC = [carve(T) for _ in range(2)]
        AT = [carve(T) for _ in range(2)]
        KQ = carve(2 * T)
        KQv = KQ.rearrange("p (c n t) -> p c n t", c=NCH, n=2)
        VT, GT = carve(T), carve(T)
        KG, KD, VR = carve(T), carve(T), carve(T)
        DT, EG, QD = carve(T), carve(T), carve(T)
        LA = carve_y(2 * T)
        LAv = LA.rearrange("p (c n t) -> p c n t", c=NCH, n=2)
        XB, WT = carve_y(T), carve_y(T)
        TX = carve_y(2 * T)
        VN = [carve_y(P) for _ in range(2)]
        ST = [carve_y(P) for _ in range(2)]
        O2 = carve_y(T)
        HC = HEADS * NCH
        BA = carve(NCH * 16)
        BAv = BA.rearrange("p (c n) -> p n c", c=NCH)
        BETA, G, NGC, EGC, EGL, EKD, Z1, Z2 = (carve(HC) for _ in range(8))
        NEA = carve(HEADS)
        TK = carve(32)
        assert o <= NSCR

        def v3(ap):
            return ap.rearrange("p (c t) -> p c t", c=NCH)

        def over_tokens(ap):
            return ap.unsqueeze(2).broadcast_to([P, NCH, P])

        def over_chunks(ap):
            return ap.unsqueeze(1).broadcast_to([P, NCH, P])

        PER = dict(d_c0=3, d_tap=9, d_th=4, d_qkv=3, d_gate=1, d_sq=2, d_ssq=2, d_tr=2, d_gcol=1, d_gb=1, d_gram=1,
                   d_s1=4, d_sq_eps=1, d_sqk=1, d_mask=1, d_dt=4, d_eg=1, d_la=8, d_tt=14, d_t=2, d_ptr=2, d_px=12,
                   d_x=14, d_pt=12, d_pw=2, d_wt=2, d_pv=4, d_vn=4, d_po=1, d_ps=3, d_s=3, d_osq=1, d_os=1, d_oms=1,
                   d_orow=1, d_ro=1, d_o1=1, d_o2=1, o_hi=1, o_lo=1)

        def head_count(h):
            def at(name, k):
                return count(name, h * PER[name] + k)
            return at

        def chunk(ap, c):
            return ap[:, c * P:(c + 1) * P]

        def halfx(i):
            return TX[:, i * T:(i + 1) * T]

        def t_of(c):
            return TX[:, (c // 2) * T + (c % 2) * P:(c // 2) * T + (c % 2 + 1) * P]

        def tt_of(c):
            return TX[:, (c // 2) * T + (c % 2 + 2) * P:(c // 2) * T + (c % 2 + 3) * P]

        def two(ap):
            return ap.rearrange("p (c t) -> p c t", c=2)

        def columns(ap, l, bit):
            return ap.rearrange("p (b two w) -> p b two w", two=2, w=2 ** l)[:, :, bit, :]

        def level(l):
            return cst[:, C_LVL + l * P:C_LVL + (l + 1) * P].unsqueeze(1).broadcast_to([P, 2, P])

        def o_wait(pe):
            def at(k):
                pe.wait_ge(S("o_hi"), count("o_hi", k + 1))
                pe.wait_ge(S("o_lo"), count("o_lo", k + 1))
            return at

        def delta_pe(pe, h, more):
            at = head_count(h)
            r = rnd(U_DELTA, h + 1)

            def part(s, first, n):
                if not more:
                    if s < 2:
                        if first == 0:
                            unit_wait(pe, rnd(U_AOUT, 0), s)
                        if first < KT - 1:
                            part_blocks(pe, s, s, pairB, first, min(first + n, KT - 1), wait=o_wait(pe))
                    return
                if first == 0:
                    unit_wait(pe, r, s)
                last = part_blocks(pe, s % 2, s, pairA, first, first + n)
                if first + n == KT:
                    last.then_inc(S(f"unit_done{s}"), 1)
            pe.wait_ge(S("d_gcol"), at("d_gcol", 1))
            for c in range(NCH):
                last = pe.matmul(chunk(ps[5], c), TK[:, c:c + 1].broadcast_to([P, P]), tri, start=True, stop=True)
            last.then_inc(S("d_gb"), 1)
            pe.wait_ge(S("d_sq"), at("d_sq", 1))
            for c in range(NCH):
                last = pe.matmul(ps[2][:, c:c + 1], SQ[:, T + c * P:T + (c + 1) * P], ones[:, 0:1], start=True, stop=True)
            last.then_inc(S("d_ssq"), 1)
            pe.wait_ge(S("d_qkv"), at("d_qkv", 2))
            for c in range(NCH):
                last = pe.matmul(ps[4 - c // 2][:, (c % 2) * 256:(c % 2 + 1) * 256], KQv[:, c, 0, :],
                                 KQ[:, c * 256:(c + 1) * 256], start=True, stop=True)
            last.then_inc(S("d_gram"), 1)
            part(0, 0, 3)
            pe.wait_ge(S("d_o1"), at("d_o1", 0))
            for c in range(NCH):
                last = pe.transpose(chunk(ps[6], c), KQv[:, c, 0, :], ident)
            last.then_inc(S("d_tr"), 1)
            pe.wait_ge(S("d_qkv"), at("d_qkv", 3))
            pe.wait_ge(S("d_o2"), at("d_o2", 0))
            for c in range(NCH):
                last = pe.transpose(chunk(ps[7], c), chunk(VT, c), ident)
            last.then_inc(S("d_tr"), 1)
            part(0, 3, 3)
            pe.wait_ge(S("d_sq"), at("d_sq", 2))
            pe.wait_ge(S("d_s1"), at("d_s1", 1))
            for c in range(NCH):
                last = pe.matmul(ps[2][:, NCH + c:NCH + c + 1], SQ[:, c * P:(c + 1) * P], ones[:, 0:1],
                                 start=True, stop=True)
            last.then_inc(S("d_ssq"), 1)
            for i in range(2):
                pe.wait_ge(S("d_tt"), at("d_tt", i + 1))
                for c in (2 * i, 2 * i + 1):
                    last = pe.transpose(chunk(ps[4 + i], c % 2), tt_of(c), ident)
                last.then_inc(S("d_ptr"), 1)
                if i == 0:
                    part(0, 6, 2)
            for l in range(1, 7):
                for i in range(2):
                    pe.wait_ge(S("d_tt"), at("d_tt", 2 * l - 1 + i))
                    if l == 1:
                        pe.wait_ge(S("d_t"), at("d_t", i + 1))
                    for c in (2 * i, 2 * i + 1):
                        last = pe.matmul(chunk(ps[4 + i], c % 2), LAv[:, c, 0, :], t_of(c), start=True, stop=True)
                    last.then_inc(S("d_px"), 1)
                    if l < 5:
                        part(1, 2 * (l - 1) + i, 1)
                    else:
                        part(2, 2 * (l - 5) + i, 1)
                for i in range(2):
                    pe.wait_ge(S("d_x"), at("d_x", 2 * l + 1 + i))
                    if l == 1:
                        pe.wait_ge(S("d_la"), at("d_la", 7))
                    for c in (2 * i, 2 * i + 1):
                        if l < 6:
                            pe.matmul(columns(chunk(ps[6 + i], c % 2), l, 0), tt_of(c), columns(chunk(XB, c), l, 0),
                                      start=True, stop=True)
                        last = pe.matmul(columns(chunk(ps[6 + i], c % 2 + 2), l, 1), chunk(XB, c),
                                         columns(tt_of(c), l, 1), start=True, stop=True)
                    last.then_inc(S("d_pt"), 1)
            for i in range(2):
                pe.wait_ge(S("d_tt"), at("d_tt", 13 + i))
                if i == 0:
                    pe.matmul(chunk(ps[3], 0), tt_of(0), chunk(VR, 0), start=True, stop=True).then_inc(S("d_pv"), 1)
                for c in (2 * i, 2 * i + 1):
                    last = pe.matmul(chunk(ps[4 + i], c % 2), chunk(KG, c), tt_of(c), start=True, stop=True)
                last.then_inc(S("d_pw"), 1)
            for c in range(NCH):
                val = ps[3 + 4 * (c % 2)][:, 0:P]
                if c:
                    pe.wait_ge(S("d_wt"), at("d_wt", c // 2 + 1))
                    pe.wait_ge(S("d_s"), at("d_s", c))
                    pe.matmul(val, chunk(WT, c), ST[c % 2], start=False, stop=True).then_inc(S("d_pv"), 1)
                    pe.matmul(chunk(ps[6], c), ST[c % 2], chunk(QD, c), start=True, stop=False)
                if c < NCH - 1:
                    pe.matmul(ps[3 + 4 * ((c + 1) % 2)][:, 0:P], tt_of(c + 1), chunk(VR, c + 1), start=True, stop=False)
                pe.wait_ge(S("d_vn"), at("d_vn", c + 1))
                if c < NCH - 1:
                    pe.matmul(ps[2][:, (c % 2 + 1) * P:(c % 2 + 2) * P], chunk(KD, c), VN[c % 2],
                              start=True, stop=True).then_inc(S("d_ps"), 1)
                part(2, 4 + c, 1)
                last = pe.matmul(chunk(ps[6], c), VN[c % 2], LAv[:, c, 1, :], start=c == 0, stop=True)
            last.then_inc(S("d_po"), 1)
            part(3, 0, 3)
            pe.wait_ge(S("d_osq"), at("d_osq", 1))
            for c in range(NCH):
                last = pe.matmul(ps[2][:, 8 + c:9 + c], SQ[:, c * P:(c + 1) * P], ones[:, 0:1], start=True, stop=True)
            last.then_inc(S("d_os"), 1)
            part(3, 3, 3)
            pe.wait_ge(S("d_orow"), at("d_orow", 1))
            for c in range(NCH):
                last = pe.matmul(chunk(ps[7], c), TK[:, 28 + c:29 + c].broadcast_to([P, P]), ident,
                                 start=True, stop=True)
            last.then_inc(S("d_ro"), 1)
            part(3, 6, 2)

        def head_col(ap, h, c=0, n=1):
            return ap[:, bass.ds(h * NCH + c, n)]

        def conv_act(act, h, k):
            at = head_count(h)
            act.wait_ge(S(f"evac{k}"), count(f"evac{k}", rnd(U_DELTA, h) + 1))
            if k < 3:
                nc.scalar.activation(AC[k % 2], AU[k % 2][:, APAD:APAD + T], ACT.Copy,
                                     scale=half[:, bass.ds(8 + (k * 8 + h) * 4 + 3, 1)]).then_inc(S("d_c0"), 1)
                act.wait_ge(S("d_tap"), at("d_tap", 3 * (k + 1)))
            nc.scalar.activation(AT[k % 2], AC[k % 2], ACT.Tanh).then_inc(S("d_th"), 1)

        def square_of(n):
            nc.scalar.activation(v3(tile(SQ, 1 - n)), KQv[:, :, n, :], ACT.Square).then_inc(S("d_sq"), 1)

        def delta_act(act, h, more):
            at = head_count(h)
            a = nc.scalar
            r = rnd(U_DELTA, h + 1)

            act.wait_ge(S("d_gb"), at("d_gb", 1))
            a.activation(EG, ps[5][:], ACT.Exp).then_inc(S("d_eg"), 1)
            act.wait_ge(S("d_mask"), at("d_mask", 1))
            for c in range(NCH):
                a.activation(chunk(DT, c), chunk(DT, c), ACT.Exp, bias=head_col(NGC, h, c)).then_inc(S("d_dt"), 1)
            act.wait_ge(S("d_os"), at("d_os", 0))
            square_of(1)
            if more:
                ahead(act, split_hi, r, 0)
            for i in range(2):
                act.wait_ge(S("d_ptr"), at("d_ptr", i + 1))
                a.activation(halfx(i)[:, 0:2 * P], ps[4 + i][:, 0:2 * P], ACT.Copy).then_inc(S("d_t"), 1)
            if more:
                ahead(act, split_hi, r, 1)
                conv_act(act, h + 1, 0)
                ahead(act, split_hi, r, 2)
                conv_act(act, h + 1, 1)
            for i in range(2):
                act.wait_ge(S("d_pw"), at("d_pw", i + 1))
                a.activation(WT[:, 2 * i * P:2 * (i + 1) * P], ps[4 + i][:, 0:2 * P], ACT.Copy, scale=-1.0)\
                    .then_inc(S("d_wt"), 1)
            if more:
                ahead(act, split_hi, r, 3)
                act.wait_ge(S("d_qkv"), head_count(h + 1)("d_qkv", 2))
                square_of(0)
            act.wait_ge(S("d_po"), at("d_po", 1))
            a.activation(SQ[:, 0:T], ps[6][:], ACT.Square).then_inc(S("d_osq"), 1)
            if more:
                conv_act(act, h + 1, 2)
            act.wait_ge(S("d_o2"), at("d_o2", 1))
            a.activation(tile(pairB[0], h), O2, ACT.Copy).then_inc(S("o_hi"), 1)
            if more:
                conv_act(act, h + 1, 3)

        def conv_dve(dve, h, k, step):
            at = head_count(h)
            v = nc.vector
            if step == 0:
                evacuate(dve, rnd(U_DELTA, h), k, AU[k % 2][:, APAD:APAD + T], 1.0, R[:])
            elif step < 4:
                tap = 3 - step
                if step == 1:
                    dve.wait_ge(S("d_c0"), at("d_c0", k + 1))
                else:
                    dve.wait_ge(S("d_tap"), at("d_tap", 3 * k + step - 1))
                v.scalar_tensor_tensor(out=AC[k % 2], in0=AU[k % 2][:, tap:tap + T],
                                       scalar=half[:, bass.ds(8 + (k * 8 + h) * 4 + tap, 1)],
                                       in1=AC[k % 2], op0=ALU.mult, op1=ALU.add).then_inc(S("d_tap"), 1)
            else:
                dve.wait_ge(S("d_th"), at("d_th", k + 1))
                out = [KQv[:, :, 1, :], KQv[:, :, 0, :], v3(VT)][k]
                v.scalar_tensor_tensor(out=out, in0=v3(AT[k % 2]), scalar=1.0, in1=v3(AC[k % 2]),
                                       op0=ALU.add, op1=ALU.mult).then_inc(S("d_qkv"), 1)

        def delta_dve(dve, h, more):
            at = head_count(h)
            v = nc.vector
            r = rnd(U_DELTA, h + 1)

            def conv(k, *steps):
                if more:
                    for step in steps:
                        conv_dve(dve, h + 1, k, step)

            def split(k):
                if more:
                    ahead(dve, split_lo, r, k)
            dve.wait_ge(S("d_th"), at("d_th", 4))
            v.scalar_tensor_tensor(out=GT, in0=AT[1], scalar=1.0, in1=AC[1], op0=ALU.add, op1=ALU.mult)\
                .then_inc(S("d_gate"), 1)
            dve.wait_ge(S("d_eg"), at("d_eg", 1))
            v.tensor_tensor(v3(DT), v3(ps[5][:]), over_chunks(cst[:, C_NEG:C_NEG + P]), ALU.add)\
                .then_inc(S("d_mask"), 1)
            dve.wait_ge(S("d_ssq"), at("d_ssq", 1))
            v.tensor_scalar(TK[:, 4:8], ps[2][:, 0:4], EPS, None, ALU.add).then_inc(S("d_s1"), 1)
            dve.wait_ge(S("d_s1"), at("d_s1", 1))
            v.reciprocal(TK[:, 12:16], TK[:, 4:8]).then_inc(S("d_s1"), 1)
            dve.wait_ge(S("d_s1"), at("d_s1", 2))
            v.tensor_tensor(TK[:, 16:20], TK[:, 12:16], head_col(BETA, h, 0, 4), ALU.mult).then_inc(S("d_s1"), 1)
            dve.wait_ge(S("d_s1"), at("d_s1", 3))
            v.tensor_tensor(TK[:, 20:24], TK[:, 16:20], head_col(EKD, h, 0, 4), ALU.mult).then_inc(S("d_s1"), 1)
            dve.wait_ge(S("d_gram"), at("d_gram", 1))
            for c in range(NCH):
                dve.wait_ge(S("d_dt"), at("d_dt", c + 1))
                g = ps[4 - c // 2][:, (c % 2) * 256:(c % 2 + 1) * 256].rearrange("p (n t) -> p n t", n=2)
                v.scalar_tensor_tensor(out=LAv[:, c, :, :], in0=g, scalar=TK[:, 16 + c:17 + c],
                                       in1=chunk(DT, c).unsqueeze(1).broadcast_to([P, 2, P]),
                                       op0=ALU.mult, op1=ALU.mult).then_inc(S("d_la"), 1)
                if c % 2:
                    i = c // 2
                    x = XB[:, 2 * i * P:2 * (i + 1) * P]
                    dve.wait_ge(S("d_la"), at("d_la", c + 1))
                    v.tensor_tensor(two(x), LAv[:, 2 * i:2 * i + 2, 0, :], level(0), ALU.mult).then_inc(S("d_x"), 1)
                    dve.wait_ge(S("d_x"), at("d_x", i + 1))
                    v.tensor_tensor(two(halfx(i)[:, 2 * P:4 * P]), ident.unsqueeze(1).broadcast_to([P, 2, P]), two(x),
                                    ALU.subtract).then_inc(S("d_tt"), 1)
            dve.wait_ge(S("d_tr"), at("d_tr", 1))
            v.tensor_tensor(v3(KG), v3(ps[6][:]), over_tokens(head_col(EGC, h, 0, 4)), ALU.mult).then_inc(S("d_la"), 1)
            dve.wait_ge(S("d_s1"), at("d_s1", 4))
            v.tensor_tensor(v3(KD), v3(ps[6][:]), over_tokens(TK[:, 20:24]), ALU.mult).then_inc(S("d_la"), 1)
            dve.wait_ge(S("d_sqk"), at("d_sqk", 1))
            dve.wait_ge(S("d_tr"), at("d_tr", 2))
            v.tensor_tensor(v3(VR), v3(ps[7][:]), over_tokens(TK[:, 24:28]), ALU.mult).then_inc(S("d_la"), 1)
            v.tensor_tensor(v3(QD), KQv[:, :, 1, :], v3(EG), ALU.mult).then_inc(S("d_la"), 1)
            split(0)
            for l in range(1, 7):
                for i in range(2):
                    dve.wait_ge(S("d_px"), at("d_px", 2 * l - 1 + i))
                    v.tensor_tensor(two(XB[:, 2 * i * P:2 * (i + 1) * P]), two(ps[4 + i][:, 0:2 * P]), level(l), ALU.mult)\
                        .then_inc(S("d_x"), 1)
                if l == 1:
                    dve.wait_ge(S("d_ssq"), at("d_ssq", 2))
                    v.tensor_scalar(TK[:, 8:12], ps[2][:, 4:8], EPS, EPS * P, ALU.add, ALU.mult)\
                        .then_inc(S("d_sq_eps"), 1)
                    conv(0, 0)
                elif l == 2:
                    split(1)
                elif l == 4:
                    dve.wait_ge(S("d_la"), at("d_la", 8))
                    dve.wait_ge(S("d_sq"), at("d_sq", 2))
                    conv(0, 4)
                elif l == 5:
                    conv(1, 0)
                elif l == 6:
                    conv(1, 2)
                for i in range(2):
                    dve.wait_ge(S("d_pt"), at("d_pt", 2 * l - 1 + i))
                    if l < 6:
                        t = columns(halfx(i)[:, 0:2 * P], l, 0)
                        v.tensor_tensor(t, t, columns(ps[6 + i][:, 0:2 * P], l, 0), ALU.subtract)
                    t = columns(halfx(i)[:, 2 * P:T], l, 1)
                    v.tensor_tensor(t, t, columns(ps[6 + i][:, 2 * P:T], l, 1), ALU.subtract).then_inc(S("d_tt"), 1)
                if l == 2:
                    conv(0, 1)
                elif l == 3:
                    conv(0, 2, 3)
                elif l == 4:
                    split(2)
                elif l == 5:
                    conv(1, 1)
                elif l == 6:
                    conv(1, 3)
            for c in range(NCH):
                dve.wait_ge(S("d_pv"), at("d_pv", c + 1))
                v.tensor_copy(VN[c % 2], ps[3 + 4 * (c % 2)][:, 0:P]).then_inc(S("d_vn"), 1)
                if c < NCH - 1:
                    dve.wait_ge(S("d_ps"), at("d_ps", c + 1))
                    add = ps[2][:, (c % 2 + 1) * P:(c % 2 + 2) * P]
                    if c == 0:
                        v.tensor_copy(ST[1], add).then_inc(S("d_s"), 1)
                    else:
                        dve.wait_ge(S("d_s"), at("d_s", c))
                        v.scalar_tensor_tensor(out=ST[(c + 1) % 2], in0=ST[c % 2], scalar=head_col(EGL, h, c),
                                               in1=add, op0=ALU.mult, op1=ALU.add).then_inc(S("d_s"), 1)
                if c == 0:
                    conv(1, 4)
                if c == 1 and more:
                    v.tensor_copy(TK[:, 0:4], head_col(G, h + 1, 0, 4)).then_inc(S("d_gcol"), 1)
            split(3)
            conv(2, 0)
            dve.wait_ge(S("d_os"), at("d_os", 1))
            dve.wait_ge(S("d_sq_eps"), at("d_sq_eps", 1))
            v.scalar_tensor_tensor(out=TK[:, 12:16], in0=ps[2][:, 8:12], scalar=1.0 / P, in1=TK[:, 8:12],
                                   op0=ALU.mult, op1=ALU.add).then_inc(S("d_oms"), 1)
            dve.wait_ge(S("o_lo"), at("o_lo", 0))
            v.scalar_tensor_tensor(out=O2, in0=ps[6][:], scalar=par_col("onorm"), in1=GT,
                                   op0=ALU.mult, op1=ALU.mult).then_inc(S("d_o1"), 1)
            conv(2, 1, 2)
            dve.wait_ge(S("d_o1"), at("d_o1", 1))
            dve.wait_ge(S("d_ro"), at("d_ro", 1))
            v.tensor_tensor(O2, O2, ps[7][:], ALU.mult).then_inc(S("d_o2"), 1)
            conv(2, 3)
            if more:
                evacuate(dve, r, 3, AC[1], 0.5, R[:])
            conv(2, 4)

        def delta_pool(pool, h):
            at = head_count(h)
            pool.wait_ge(S("d_s1"), at("d_s1", 1))
            nc.gpsimd.tensor_tensor(TK[:, 24:28], TK[:, 4:8], mhalf[:, 4:8], ALU.pow).then_inc(S("d_sqk"), 1)
            pool.wait_ge(S("d_oms"), at("d_oms", 1))
            nc.gpsimd.tensor_tensor(TK[:, 28:32], TK[:, 12:16], mhalf[:, 0:4], ALU.pow).then_inc(S("d_orow"), 1)
            pool.wait_ge(S("o_hi"), at("o_hi", 1))
            nc.gpsimd.tensor_tensor(tile(pairB[1], h), O2, tile(pairB[0], h).bitcast(F32), ALU.subtract).then_inc(S("o_lo"), 1)

        def evacuate(dve, r, k, out, scalar, in1, op1=ALU.mult, op0=ALU.mult):
            evac_wait(dve, r, k)
            return nc.vector.scalar_tensor_tensor(out=out, in0=ps[k % 2][:], scalar=scalar, in1=in1,
                                                  op0=op0, op1=op1).then_inc(S(f"evac{k}"), 1)

        def residual_pe(pe, base, pair, wait, n=KT, late=2, begun=False):
            if begun:
                for s in range(2):
                    part_blocks(pe, s, s, pair, n - late, n, n, wait).then_inc(S(f"unit_done{s}"), 1)
            else:
                two_units(pe, rnd(base, 0), pair, wait, late, n)
            for i in range(2):
                for s in range(0 if i else 2, SLOTS):
                    unit(pe, rnd(base, i), s, pair, n)

        def residual_act(act, base, tag, g, pair, end=False):
            for i in range(2):
                for k in range(SLOTS):
                    m, r = 4 * i + k, rnd(base, i)
                    if not (end and m >= KT - LEAD):
                        ahead(act, split_hi, r, k)
                    act.wait_ge(S(f"evac{k}"), count(f"evac{k}", r + 1))
                    if g:
                        nc.scalar.activation(tile(pair[0], m), tile(X, m), ACT.Copy, scale=par_col(g, m)).then_inc(S(tag + "_hi"), 1)
                    square(act, tag, m, tile(X, m))

        def residual_dve(dve, base, tag, g, pair, bias=None, end=False):
            for i in range(2):
                for k in range(SLOTS):
                    m, r = 4 * i + k, rnd(base, i)
                    if not (end and m >= KT - LEAD):
                        ahead(dve, split_lo, r, k)
                    evacuate(dve, r, k, tile(X, m), par_col(bias, m) if bias else 0.0, tile(X, m), ALU.add, ALU.add)
                    if g and m:
                        norm_lo(dve, tag, g, pair, m - 1)
            if g:
                norm_lo(dve, tag, g, pair, KT - 1)

        FU = [AU[0][:, 0:T + FPAD], AU[1][:, 0:T + FPAD]]
        FC = AC
        FT = AT[0]
        PR = [KQ[:, 0:T], KQ[:, T:2 * T]]

        def ffn_bases(base):
            first = 0
            for n in MID_GROUPS:
                yield base, base + 2 * n, first, n
                base, first = base + 2 * n + 8, first + n

        def hidden_rounds(eng, base, first, n, one_round):
            start = 0
            if first == 0:
                one_round(0, True)
                start = 1
            with eng.Fori(start, n // 2) as i:
                one_round(i, False)

        def ffn_pe(pe, L, base, inpair, mid, ntag, end=False):
            t = f"f{L}"
            for up, down, first, n in ffn_bases(base):
                def one_round(i, begin):
                    if begin:
                        two_units(pe, rnd(up, i), inpair, pair_wait(ntag)(pe), 1, norm=ntag)
                    for s in range(2 if begin else 0, SLOTS):
                        unit(pe, rnd(up, i), s, inpair)
                hidden_rounds(pe, up, first, n, one_round)

                def wait_mid(k):
                    pe.wait_ge(S(t + "_hi"), count(t + "_hi", first + k + 1))
                    pe.wait_ge(S(t + "_lo"), count(t + "_lo", first + k + 1))
                residual_pe(pe, down, mid, wait_mid, n)

        def ffn_act(act, L, base, mid, ntag, next_tag, next_g, next_pair, end=False):
            t = f"f{L}"
            for up, down, first, n in ffn_bases(base):
                def one_round(i, begin):
                    for k in range(SLOTS):
                        r = rnd(up, i)
                        ahead(act, split_hi, r, k)
                        if begin and k == 0:
                            norm_row(act, ntag)
                            act.wait_ge(S(t + "_half"), count(t + "_half", 2))
                        q, side = first + 2 * i + k // 2, k % 2
                        act.wait_ge(S(f"evac{k}"), count(f"evac{k}", r + 1))
                        if not begin or k > 1:
                            act.wait_ge(S(t + "_prod"), count(t + "_prod", q))
                        if side == 0:
                            w3, b = half[:, bass.ds(104 + q * 3 + 2, 1)], half[:, bass.ds(170 + q, 1)]
                        else:
                            w3, b = par_col(f"f_conv{L}", (22 + q) * 3 + 2), par_col(f"f_bias{L}", 22 + q)
                        nc.scalar.activation(FC[side], FU[side][:, FPAD:FPAD + T], ACT.Identity, scale=w3, bias=b).then_inc(S(t + "_c0"), 1)
                        if side == 0:
                            act.wait_ge(S(t + "_tap"), count(t + "_tap", 4 * q + 2))
                            nc.scalar.activation(FT, FC[0], ACT.Tanh).then_inc(S(t + "_th"), 1)
                        else:
                            act.wait_ge(S(t + "_prod"), count(t + "_prod", q + 1))
                            nc.scalar.activation(tile(mid[0], 2 * i + k // 2), PR[k // 2], ACT.Copy).then_inc(S(t + "_hi"), 1)
                hidden_rounds(act, up, first, n, one_round)
                if first + n < 22:
                    with act.Fori(0, 2) as i:
                        for k in range(SLOTS):
                            ahead(act, split_hi, rnd(down, i), k)
                else:
                    residual_act(act, down, next_tag, next_g, next_pair, end)

        def ffn_dve(dve, L, base, mid, ntag, next_tag, next_g, next_pair, end=False):
            t = f"f{L}"
            v = nc.vector
            c, b = _cols[f"f_conv{L}"][0], _cols[f"f_bias{L}"][0]
            v.tensor_scalar(half[:, 104:170], par[:, c:c + 66], 0.5, None, ALU.mult).then_inc(S(t + "_half"), 1)
            v.tensor_scalar(half[:, 170:192], par[:, b:b + 22], 0.5, None, ALU.mult).then_inc(S(t + "_half"), 1)
            dve.wait_ge(S(t + "_half"), count(t + "_half", 2))
            for u in FU:
                v.memset(u[:, 0:FPAD], 0.0).then_inc(S(t + "_pad"), 1)
            token_mean(dve, ntag, 2, D)
            for up, down, first, n in ffn_bases(base):
                def one_round(i, begin):
                    for k in range(SLOTS):
                        r = rnd(up, i)
                        if begin and k == 0:
                            dve.wait_ge(S(ntag + "_R"), count(ntag + "_R", 1))
                            dve.wait_ge(S(t + "_pad"), count(t + "_pad", 2))
                        q, side = first + 2 * i + k // 2, k % 2
                        evacuate(dve, r, k, FU[side][:, FPAD:FPAD + T], 1.0, R[:])
                        ahead(dve, split_lo, r, k)
                        if side:
                            dve.wait_ge(S(t + "_th"), count(t + "_th", q + 1))
                            v.scalar_tensor_tensor(out=FC[0], in0=FT, scalar=1.0, in1=FC[0], op0=ALU.add,
                                                   op1=ALU.mult).then_inc(S(t + "_gate"), 1)
                        dve.wait_ge(S(t + "_c0"), count(t + "_c0", 2 * q + side + 1))
                        for n_, tap in enumerate((1, 0)):
                            w = half[:, bass.ds(104 + q * 3 + tap, 1)] if side == 0 else \
                                par_col(f"f_conv{L}", (22 + q) * 3 + tap)
                            if n_:
                                dve.wait_ge(S(t + "_tap"), count(t + "_tap", 4 * q + 2 * side + 1))
                            v.scalar_tensor_tensor(out=FC[side], in0=FU[side][:, tap:tap + T], scalar=w,
                                                   in1=FC[side], op0=ALU.mult, op1=ALU.add)\
                                .then_inc(S(t + "_tap"), 1)
                        if side:
                            dve.wait_ge(S(t + "_gate"), count(t + "_gate", q + 1))
                            dve.wait_ge(S(t + "_tap"), count(t + "_tap", 4 * q + 4))
                            if not begin:
                                dve.wait_ge(S(t + "_lo"), count(t + "_lo", q - 1))
                            v.tensor_tensor(PR[k // 2], FC[0], FC[1], ALU.mult).then_inc(S(t + "_prod"), 1)
                hidden_rounds(dve, up, first, n, one_round)
                if first + n < 22:
                    with dve.Fori(0, 2) as i:
                        for k in range(SLOTS):
                            r = rnd(down, i)
                            ahead(dve, split_lo, r, k)
                            evacuate(dve, r, k, tile(X, 4 * i + k), 0.0, tile(X, 4 * i + k), ALU.add, ALU.add)
                else:
                    residual_dve(dve, down, next_tag, next_g, next_pair, end=end)

        def ffn_pool(pool, L, base, mid):
            t = f"f{L}"
            for up, down, first, n in ffn_bases(base):
                with pool.Fori(0, n // 2) as i:
                    for j in range(2):
                        pool.wait_ge(S(t + "_hi"), count(t + "_hi", first + 2 * i + j + 1))
                        nc.gpsimd.tensor_tensor(tile(mid[1], 2 * i + j), PR[j],
                                                    tile(mid[0], 2 * i + j).bitcast(F32), ALU.subtract).then_inc(S(t + "_lo"), 1)

        o = 0
        KA = [carve(T) for _ in range(2)]
        VF = carve(T)
        VA_T = [carve(T) for _ in range(2)]
        QT = [carve(T) for _ in range(2)]
        AW = carve(T)
        SC = [carve(2 * T) for _ in range(2)]
        PT = [carve(2 * T) for _ in range(2)]
        MX = carve(64)
        DD = carve(T)
        def sc3(e):
            return SC[e].rearrange("p (b s) -> p b s", b=NCH)

        def half_rows(ap, e):
            return ap[64 * e:64 * e + 64, :]

        def scores_pe(pe, j):
            t, e = j // 2, j % 2
            pe.wait_ge(S("q_t"), count("q_t", t + 1))
            if j:
                pe.wait_ge(S("s_sc"), count("s_sc", 2 * j))
            for b in range(NCH):
                lo = max(b - 1, 0) * P
                n = P if b == 0 else 2 * P
                out = ps[2 + b // 2][:, (b % 2) * 256 + 256 - n:(b % 2) * 256 + 256]
                last = pe.matmul(out, half_rows(QT[t % 2], e)[:, b * P:(b + 1) * P],
                                 half_rows(KA[t % 2], e)[:, lo:lo + n], start=True, stop=True)
                if b % 2:
                    last.then_inc(S("s_p"), 1)

        def transpose_pe(pe, j):
            e = j % 2
            pe.wait_ge(S("s_n"), count("s_n", 4 * j + 4))
            for b in range(NCH):
                for half_ in range(0 if b else 1, 2):
                    col = b * 256 + half_ * P
                    last = pe.transpose(ps[4 + b // 2][:, col % T:col % T + P], SC[e][:, col:col + P], ident)
                if b % 2:
                    last.then_inc(S("s_tr"), 1)

        def values_pe(pe, j):
            t, e = j // 2, j % 2
            if t > 1 and e == 0:
                pe.wait_ge(S("t_lo"), count("t_lo", t - 1))
            for b in range(NCH):
                if b % 2 == 0:
                    pe.wait_ge(S("s_pt"), count("s_pt", 2 * j + b // 2 + 1))
                for half_ in range(0 if b else 1, 2):
                    key = (b - 1 + half_) * P + 64 * e
                    col = b * 256 + half_ * P
                    last = pe.matmul(ps[6 + t % 2][64 * e:64 * e + 64, b * P:(b + 1) * P], VA_T[t % 2][:, key:key + 64],
                                     PT[e][:, col:col + P], start=half_ == 0 or b == 0, stop=half_ == 1)
            if e:
                last.then_inc(S("s_o"), 1)

        def attention_pe(pe):
            two_units(pe, rnd(U_KV, 0), pairA, pair_wait("kv")(pe), 1, norm="kv")
            for s in range(2, SLOTS):
                unit(pe, rnd(U_KV, 0), s, pairA)
            for m in range(2):
                pe.wait_ge(S("v_f"), count("v_f", m + 1))
                if m:
                    pe.wait_ge(S("v_t"), count("v_t", m))
                for c in range(NCH):
                    last = pe.transpose(chunk(ps[4], c), chunk(VF, c), ident)
                last.then_inc(S("v_tr"), 1)

            pe.wait_ge(S("v_t"), count("v_t", 2))
            pe.wait_ge(S("bn_lo"), count("bn_lo", 8))
            def wait_o(k):
                pe.wait_ge(S("t_hi"), count("t_hi", k + 1))
                pe.wait_ge(S("t_lo"), count("t_lo", k + 1))

            def part(m, first, end):
                s = m % SLOTS
                if m < KT:
                    if first == 0:
                        unit_wait(pe, rnd(U_Q, m // SLOTS), s)
                    last = part_blocks(pe, m % 2, s, pairB, first, end)
                    if end == KT:
                        last.then_inc(S(f"unit_done{s}"), 1)
                elif first == 0:
                    unit_wait(pe, rnd(U_BO, 0), s)
                    part_blocks(pe, s, s, pairA, 0, KT - 2, wait=wait_o)
            part(0, 0, KT)
            part(1, 0, KT // 2)
            scores_pe(pe, 0)
            for j in range(2 * KT):
                t, e = j // 2, j % 2
                if j < 2 * KT - 1:
                    scores_pe(pe, j + 1)
                transpose_pe(pe, j)
                if e == 0:
                    part(t + 1, KT // 2, KT)
                else:
                    part(t + 2, 0, KT // 2)
                values_pe(pe, j)

            residual_pe(pe, U_BO, pairA, wait_o, late=2, begun=True)

        def attention_act(act):
            a = nc.scalar
            for k in range(SLOTS):
                ahead(act, split_hi, rnd(U_KV, 0), k)
                if k == 0:
                    norm_row(act, "kv")
                for m in (2 * k, 2 * k + 1):
                    a.activation(tile(pairB[0], m), tile(X, m), ACT.Copy, scale=par_col("b_norm", m)).then_inc(S("bn_hi"), 1)
            for m in range(2):
                act.wait_ge(S("v_tr"), count("v_tr", m + 1))
                a.activation(VA_T[m], ps[4][:], ACT.Copy).then_inc(S("v_t"), 1)

            def exps(j):
                e = j % 2
                act.wait_ge(S("s_mx"), count("s_mx", 2 * j + 2))
                den = MX[:, 8 * e:8 * e + 8]
                neg = MX[:, 16 + 4 * e:20 + 4 * e]
                a.activation(MX[:, 24 + 4 * e:28 + 4 * e], neg, ACT.Exp, bias=rowp[:, 16 + j:17 + j])\
                    .then_inc(S("s_e"), 1)
                for b in range(NCH):
                    sc = SC[e][:, b * 256 + (0 if b else P):(b + 1) * 256]
                    a.activation(sc, sc, ACT.Exp, bias=neg[:, b:b + 1], accum_out=den[:, b:b + 1])\
                        .then_inc(S("s_e"), 1)
            exps(0)
            for j in range(2 * KT):
                t, e = j // 2, j % 2
                if e == 0:
                    ahead(act, split_hi, rnd(U_Q, t // SLOTS), t % SLOTS)
                for n in range(2):
                    act.wait_ge(S("s_tr"), count("s_tr", 2 * j + n + 1))
                    lo = 0 if n else P
                    a.activation(PT[e][:, n * T + lo:(n + 1) * T], ps[4 + n][:, lo:T], ACT.Copy)\
                        .then_inc(S("s_pt"), 1)
                if j < 2 * KT - 1:
                    exps(j + 1)
                if e:
                    act.wait_ge(S("s_o"), count("s_o", t + 1))
                    a.activation(tile(pairA[0], t), ps[6 + t % 2][:], ACT.Copy).then_inc(S("t_hi"), 1)
            residual_act(act, U_BO, "n_f1", "f_norm1", pairB)

        def attention_dve(dve):
            v = nc.vector
            token_mean(dve, "kv", 2, D)
            for e in range(2):
                v.memset(SC[e][:, 0:P], -FAR).then_inc(S("sc_far"), 1)
                v.tensor_copy(DD[:, e * 256:(e + 1) * 256], cst[:, C_DIST:C_DIST + 256]).then_inc(S("sc_far"), 1)
            dve.wait_ge(S("sc_far"), count("sc_far", 4))
            for k in range(SLOTS):
                r = rnd(U_KV, 0)
                ahead(dve, split_lo, r, k)
                if k == 0:
                    dve.wait_ge(S("kv_R"), count("kv_R", 1))
                evacuate(dve, r, k, AW, 1.0, R[:])
                dve.wait_ge(S(f"evac{k}"), count(f"evac{k}", r + 1))
                if k > 2:
                    dve.wait_ge(S("v_tr"), count("v_tr", k - 2))
                v.tensor_scalar(KA[k] if k < 2 else VF, AW, par_col("kv_b", k), None, ALU.add).then_inc(S("k_f" if k < 2 else "v_f"), 1)
                for m in (2 * k, 2 * k + 1):
                    norm_lo(dve, "bn", "b_norm", pairB, m)
                dve.wait_ge(S("k_f" if k < 2 else "v_f"), count("k_f" if k < 2 else "v_f", k % 2 + 1))

            def q_tile(t):
                r, k = rnd(U_Q, t // SLOTS), t % SLOTS
                if t:
                    dve.wait_ge(S("q_t"), count("q_t", t))
                evacuate(dve, r, k, AW, 1.0, R[:])
                dve.wait_ge(S(f"evac{k}"), count(f"evac{k}", r + 1))
                v.tensor_scalar(QT[t % 2], AW, par_col("b_q", t), 0.125, ALU.add, ALU.mult).then_inc(S("q_t"), 1)

            def maxima(j):
                e = j % 2
                for n in range(2):
                    dve.wait_ge(S("s_p"), count("s_p", 2 * j + n + 1))
                    lo = 0 if n else P
                    v.scalar_tensor_tensor(out=SC[e][:, n * T + lo:(n + 1) * T], in0=DD[:, lo:T],
                                           scalar=rowp[:, 32 + j:33 + j], in1=ps[2 + n][:, lo:T],
                                           op0=ALU.mult, op1=ALU.add).then_inc(S("s_sc"), 1)
                dve.wait_ge(S("s_sc"), count("s_sc", 2 * j + 2))
                mx = MX[:, 32 + 4 * e:36 + 4 * e]
                v.tensor_reduce(mx, sc3(e), mybir.AxisListType.X, ALU.max).then_inc(S("s_mx"), 1)
                dve.wait_ge(S("s_mx"), count("s_mx", 2 * j + 1))
                v.tensor_scalar(MX[:, 16 + 4 * e:20 + 4 * e], mx, rowp[:, 16 + j:17 + j], -1.0, ALU.max, ALU.mult)\
                    .then_inc(S("s_mx"), 1)

            def normalise(j):
                e = j % 2
                dve.wait_ge(S("s_e"), count("s_e", 5 * j + 5))
                den, inv = MX[:, 40 + 4 * e:44 + 4 * e], MX[:, 52 + 4 * e:56 + 4 * e]
                v.tensor_tensor(den, MX[:, 8 * e:8 * e + 4], MX[:, 24 + 4 * e:28 + 4 * e], ALU.add)\
                    .then_inc(S("s_n"), 1)
                dve.wait_ge(S("s_n"), count("s_n", 4 * j + 1))
                v.reciprocal(inv, den).then_inc(S("s_n"), 1)
                dve.wait_ge(S("s_n"), count("s_n", 4 * j + 2))
                v.tensor_scalar(SC[e][:, P:2 * P], SC[e][:, P:2 * P], inv[:, 0:1], None, ALU.mult)\
                    .then_inc(S("s_n"), 1)
                v.tensor_tensor(sc3(e)[:, 1:NCH], sc3(e)[:, 1:NCH],
                                inv[:, 1:NCH].unsqueeze(2).broadcast_to([P, NCH - 1, 256]), ALU.mult)\
                    .then_inc(S("s_n"), 1)

            def output_lo(t):
                dve.wait_ge(S("t_hi"), count("t_hi", t + 1))
                v.tensor_tensor(tile(pairA[1], t), ps[6 + t % 2][:], tile(pairA[0], t).bitcast(F32), ALU.subtract)\
                    .then_inc(S("t_lo"), 1)
            q_tile(0)
            maxima(0)
            normalise(0)
            for j in range(2 * KT):
                t, e = j // 2, j % 2
                if j < 2 * KT - 1:
                    maxima(j + 1)
                if e == 0:
                    ahead(dve, split_lo, rnd(U_Q, t // SLOTS), t % SLOTS)
                    if t:
                        output_lo(t - 1)
                    if t < KT - 1:
                        q_tile(t + 1)
                if j < 2 * KT - 1:
                    normalise(j + 1)
            output_lo(KT - 1)
            residual_dve(dve, U_BO, "n_f1", "f_norm1", pairB, bias="b_o")

        def second_block_pe(pe):
            two_units(pe, rnd(U_DELTA, 0), pairA, pair_wait("na")(pe), 1, norm="na")
            pe.wait_ge(S("tw_lo"), count("tw_lo", 1))
            for k in range(KT):
                hi, lo = tile(pairA[0], k), tile(pairA[1], k)
                c = slice(k * 16, (k + 1) * 16)
                pe.matmul(ps[6][0:16, :], TW[0][:, c], hi, start=k == 0, stop=False)
                pe.matmul(ps[6][0:16, :], TW[0][:, c], lo, start=False, stop=False)
                last = pe.matmul(ps[6][0:16, :], TW[1][:, c], hi, start=False, stop=k == KT - 1)
            last.then_inc(S("tail"), 1)
            unit(pe, rnd(U_DELTA, 0), 2, pairA)
            pe.wait_ge(S("tail_copy"), count("tail_copy", 1))
            for c in range(NCH):
                last = pe.transpose(ps[6][:, c * 16:(c + 1) * 16], DT[0:16, c * P:(c + 1) * P], ident[0:16, 0:16])
            last.then_inc(S("tail_tok"), 1)
            unit(pe, rnd(U_DELTA, 0), 3, pairA)
            pe.wait_ge(S("g_tok"), count("g_tok", 1))
            pe.matmul(ps[6][:, 64:64 + HC], tri, G, start=True, stop=True)
            pe.matmul(ps[6][:, 128:128 + HC], ones[:], G, start=True, stop=True).then_inc(S("g_sum"), 1)
            pe.wait_ge(S("g_done"), count("g_done", 4))
            pe.wait_ge(S("ekd_sub"), count("ekd_sub", 1))
            with pe.Fori(0, HEADS - 1) as h:
                delta_pe(pe, h, True)
            delta_pe(pe, HEADS - 1, False)

            residual_pe(pe, U_AOUT, pairB, o_wait(pe), late=1, begun=True)
            ffn_pe(pe, 0, U_FFN0, pairA, pairB, "nf0")
            attention_pe(pe)
            ffn_pe(pe, 1, U_FFN1, pairB, pairA, "n_f1", end=True)
            norm_pe(pe, "fin", bank=4)

        def second_block_act(act):
            a = nc.scalar
            act.wait_ge(S("row_in"), 32)
            a.activation(TW[0], tailw, ACT.Copy).then_inc(S("tw_hi"), 1)
            norm_act(act, "na", "a_norm", pairA, lambda e, m: e.wait_ge(S("x2"), count("x2", m + 1)))
            norm_row(act, "na")
            for k in range(SLOTS):
                ahead(act, split_hi, rnd(U_DELTA, 0), k)
                conv_act(act, 0, k)
                if k == 0:
                    a.activation(NEA, rowp[:, 0:8], ACT.Exp).then_inc(S("g_act"), 1)
                elif k == 1:
                    act.wait_ge(S("d_qkv"), count("d_qkv", 2))
                    square_of(0)
                    act.wait_ge(S("g_z"), count("g_z", 1))
                    a.activation(Z2, Z1, ACT.Exp, scale=-1.0).then_inc(S("g_act"), 1)
                    a.activation(BETA, BETA, ACT.Tanh, scale=0.5).then_inc(S("g_act"), 1)
                    act.wait_ge(S("g_act"), count("g_act", 2))
                    a.activation(Z2, Z2, ACT.Ln, bias=1.0).then_inc(S("g_act"), 1)
            act.wait_ge(S("g_sum"), count("g_sum", 1))
            a.activation(EGC, ps[6][:, 64:64 + HC], ACT.Exp).then_inc(S("g_done"), 1)
            a.activation(EGL, ps[6][:, 128:128 + HC], ACT.Exp).then_inc(S("g_done"), 1)
            a.activation(NGC, ps[6][:, 64:64 + HC], ACT.Copy, scale=-1.0).then_inc(S("g_done"), 1)
            act.wait_ge(S("ekd_sub"), count("ekd_sub", 1))
            a.activation(EKD, EKD, ACT.Exp).then_inc(S("g_done"), 1)
            with act.Fori(0, HEADS - 1) as h:
                delta_act(act, h, True)
            delta_act(act, HEADS - 1, False)
            residual_act(act, U_AOUT, "nf0", "f_norm0", pairA)
            ffn_act(act, 0, U_FFN0, pairB, "nf0", "kv", "kv_norm", pairA)
            attention_act(act)
            ffn_act(act, 1, U_FFN1, pairA, "n_f1", "fin", None, None, end=True)

        def second_block_dve(dve):
            v = nc.vector
            for u in AU:
                v.memset(u[:, 0:APAD], 0.0).then_inc(S("a_pad"), 1)
            token_mean(dve, "na", 2, D)
            dve.wait_ge(S("na_R"), count("na_R", 1))
            dve.wait_ge(S("a_pad"), count("a_pad", 2))

            def hc(ap):
                return ap.rearrange("p (h c) -> p h c", c=NCH)
            for k in range(SLOTS):
                ahead(dve, split_lo, rnd(U_DELTA, 0), k)
                if k < 3:
                    for step in range(5):
                        conv_dve(dve, 0, k, step)
                else:
                    evacuate(dve, rnd(U_DELTA, 0), k, AC[1], 0.5, R[:])
                if k == 0:
                    dve.wait_ge(S("tail"), count("tail", 1))
                    v.tensor_copy(DT[0:16, :], ps[6][0:16, :]).then_inc(S("tail_copy"), 1)
                elif k == 1:
                    dve.wait_ge(S("na_rt"), count("na_rt", 1))
                    dve.wait_ge(S("tail_tok"), count("tail_tok", 1))
                    for c in range(NCH):
                        v.tensor_scalar(BA[:, c * 16:(c + 1) * 16], ps[6][:, c * 16:(c + 1) * 16],
                                        tok[:, NCH + c:NCH + c + 1], None, ALU.mult).then_inc(S("g_v"), 1)
                    dve.wait_ge(S("g_v"), count("g_v", 4))
                    v.tensor_copy(hc(BETA), BAv[:, 0:8, :]).then_inc(S("g_v"), 1)
                    v.tensor_tensor(hc(G), BAv[:, 8:16, :], rowp[:, 8:16].unsqueeze(2).broadcast_to([P, HEADS, NCH]),
                                    ALU.add).then_inc(S("g_v"), 1)
                    dve.wait_ge(S("g_v"), count("g_v", 6))
                    v.scalar_tensor_tensor(out=Z1, in0=G, scalar=-1.0, in1=G, op0=ALU.mult, op1=ALU.max)\
                        .then_inc(S("g_z"), 1)
                elif k == 2:
                    dve.wait_ge(S("g_act"), count("g_act", 4))
                    v.scalar_tensor_tensor(out=Z1, in0=G, scalar=0.0, in1=Z2, op0=ALU.max, op1=ALU.add)\
                        .then_inc(S("g_v"), 1)
                    v.tensor_scalar(BETA, BETA, 0.5, 0.5, ALU.mult, ALU.add).then_inc(S("g_v"), 1)
                    dve.wait_ge(S("g_v"), count("g_v", 8))
                    v.tensor_tensor(hc(Z2), hc(Z1), NEA.unsqueeze(2).broadcast_to([P, HEADS, NCH]), ALU.mult)\
                        .then_inc(S("g_v"), 1)
                    dve.wait_ge(S("g_v"), count("g_v", 9))
                    v.tensor_scalar(G, Z2, -1.0, None, ALU.mult).then_inc(S("g_tok"), 1)
            dve.wait_ge(S("g_sum"), count("g_sum", 1))
            dve.wait_ge(S("g_done"), count("g_done", 3))
            v.tensor_tensor(EKD, ps[6][:, 128:128 + HC], NGC, ALU.add).then_inc(S("ekd_sub"), 1)
            dve.wait_ge(S("g_done"), count("g_done", 4))
            v.tensor_copy(TK[:, 0:4], G[:, 0:4]).then_inc(S("d_gcol"), 1)
            with dve.Fori(0, HEADS - 1) as h:
                delta_dve(dve, h, True)
            delta_dve(dve, HEADS - 1, False)
            residual_dve(dve, U_AOUT, "nf0", "f_norm0", pairA)
            ffn_dve(dve, 0, U_FFN0, pairB, "nf0", "kv", "kv_norm", pairA)
            attention_dve(dve)
            ffn_dve(dve, 1, U_FFN1, pairA, "n_f1", "fin", None, None, end=True)
            token_mean(dve, "fin", 4, D)
            dve.wait_ge(S("fin_row"), count("fin_row", 1))
            dve.wait_ge(S("fin_sq"), count("fin_sq", 8))
            for m in range(KT):
                v.scalar_tensor_tensor(out=tile(X, m), in0=tile(X, m), scalar=par_col("final", m), in1=ps[5][:],
                                           op0=ALU.mult, op1=ALU.mult).then_inc(S("final"), 1)

        def second_block_pool(pool):
            sum_squares(pool, "na", KT)
            token_rsqrt(pool, "na")
            with pool.Fori(0, HEADS) as h:
                delta_pool(pool, h)
            sum_squares(pool, "nf0", KT)
            token_rsqrt(pool, "nf0")
            ffn_pool(pool, 0, U_FFN0, pairB)
            sum_squares(pool, "kv", KT)
            token_rsqrt(pool, "kv")
            sum_squares(pool, "n_f1", KT)
            token_rsqrt(pool, "n_f1")
            ffn_pool(pool, 1, U_FFN1, pairA)
            sum_squares(pool, "fin", KT)
            token_rsqrt(pool, "fin")

        @block.sync
        def _(sp):
            sp.dma_start(par[:], io["par"]).then_inc(S("par_in"), 16)
            for q in range(KT // 2):
                sp.dma_start(tile(X, 2 * q, 2), io["xT"][:, 2 * q * T:2 * (q + 1) * T]).then_inc(S(f"x_in{q}"), 16)
                if q < 2:
                    sp.dma_start(raw[:, q * 1024:(q + 1) * 1024], io["ws"][q]).then_inc(S(f"raw_in{q}"), 16)
            for s in range(2, SLOTS):
                sp.dma_start(raw[:, s * 1024:(s + 1) * 1024], io["ws"][s]).then_inc(S(f"raw_in{s}"), 16)
                if s == 2:
                    sp.dma_start(cst[:], io["cst"]).then_inc(S("cst_in"), 16)
                    sp.dma_start(rowp, io["row"].broadcast_to([P, 48])).then_inc(S("row_in"), 16)
                    sp.dma_start(tailw, io["tail"]).then_inc(S("row_in"), 16)
                    sp.dma_start(pwraw, io["pw"]).then_inc(S("pw_in"), 16)
            with sp.Fori(1, U_END // SLOTS) as r:
                for s in range(SLOTS):
                    sp.wait_ge(S(f"w_lo{s}"), count(f"w_lo{s}", r))
                    sp.dma_start(raw[:, s * 1024:(s + 1) * 1024],
                                 io["ws"][bass.ds(r * SLOTS + s, 1)].rearrange("a p n -> p (a n)"))\
                        .then_inc(S(f"raw_in{s}"), 16)
            sp.wait_ge(S("final"), count("final", KT))
            sp.dma_start(io["out"], X[:]).then_inc(S("out"), 16)
            sp.wait_ge(S("out"), 16)

        @block.tensor
        def _(pe):
            credit(pe, "d_os", *(f"unit_done{s}" for s in range(SLOTS)))
            pe.wait_ge(S("const"), count("const", 2))
            pe.wait_ge(S("cst_in"), count("cst_in", 16))

            def glu_round(i, first):
                if first:
                    two_units(pe, rnd(U_GLU, i), pairA, pair_wait("n0")(pe), 1, norm="n0")
                for s in range(2 if first else 0, SLOTS):
                    unit(pe, rnd(U_GLU, i), s, pairA)
            glu_round(0, True)
            glu_round(1, False)
            for s in range(SLOTS):
                unit(pe, rnd(U_POOL, 0), s, pairA)
            def gate_round(i):
                for s in range(SLOTS):
                    unit(pe, rnd(U_GATE, i), s, pairA)
            with pe.Fori(0, 3) as i:
                gate_round(i)
            pe.wait_ge(S("pw_hi"), count("pw_hi", 1))
            pe.wait_ge(S("pw_lo"), count("pw_lo", 1))
            for g in range(4):
                pe.wait_ge(S("pooled_lo"), count("pooled_lo", g + 1))
                c = slice(g * P, (g + 1) * P)
                hi, lo = tile(pairB[0], g), tile(pairB[1], g)
                b = 4 + g
                pe.matmul(ps[b][:], pw[0][:, c], hi, start=True, stop=False)
                pe.matmul(ps[b][:], pw[0][:, c], lo, start=False, stop=False)
                pe.matmul(ps[b][:], pw[1][:, c], hi, start=False, stop=True).then_inc(S("mix_done"), 1)
            gate_round(3)

            def branch(s, half_, first, wait=None):
                return blocks(pe, s % 2 + 4 * half_, s, pairB, first, 4, 4 * half_, wait=wait)
            pe.wait_ge(S("mixed_lo"), count("mixed_lo", 4))
            for s in range(SLOTS):
                unit_wait(pe, rnd(U_BRANCH, 0), s)
                branch(s, 0, 4)
                if s == 3:
                    pe.wait_ge(S("ln_rt"), count("ln_rt", 1))
                    spread(pe, tok[:, NCH:2 * NCH], 3).then_inc(S("ln_row"), 1)
                branch(s, 1, 4).then_inc(S(f"unit_done{s}"), 1)
                if s == 1:
                    for j in range(4):
                        pe.wait_ge(S("conv_out"), count("conv_out", j + 1))
                        last = pe.matmul(ps[6][:], ones[:], tile(CV, j), start=j == 0, stop=j == 3)
                    last.then_inc(S("ln_mean"), 1)
                elif s == 2:
                    token_sums(pe, "ln", 4, 2)
            for s in range(SLOTS):
                unit_wait(pe, rnd(U_BRANCH, 1), s)
                branch(s, 0, 0, wait=pair_wait("ln")(pe) if s == 0 else None)
                branch(s, 1, 0).then_inc(S(f"unit_done{s}"), 1)
            two_units(pe, rnd(U_WO, 0), pairA, pair_wait("br")(pe), 2)
            for i in range(2):
                for s in range(0 if i else 2, SLOTS):
                    unit(pe, rnd(U_WO, i), s, pairA)
            norm_pe(pe, "post0", bank=4)
            def mlp_group(g, first):
                if first:
                    two_units(pe, rnd(U_MLP, 0), pairA, pair_wait("n1")(pe), 1, norm="n1")
                for i in range(2):
                    for s in range(2 if first and i == 0 else 0, SLOTS):
                        unit(pe, rnd(U_MLP, g * 4 + i), s, pairA)

                def wait_mid(k):
                    pe.wait_ge(S("mlp_hi"), count("mlp_hi", g * 8 + k + 1))
                    pe.wait_ge(S("mlp_lo"), count("mlp_lo", g * 8 + k + 1))
                two_units(pe, rnd(U_MLP, g * 4 + 2), pairB, wait_mid, 2)
                for i in range(2):
                    for s in range(0 if i else 2, SLOTS):
                        unit(pe, rnd(U_MLP, g * 4 + 2 + i), s, pairB)
            mlp_group(0, True)
            with pe.Fori(1, 3) as g:
                mlp_group(g, False)
            mlp_group(3, False)
            norm_pe(pe, "post1", bank=4)
            second_block_pe(pe)

        @block.scalar
        def _(act):
            act.wait_ge(S("par_in"), count("par_in", 16))
            norm_act(act, "n0", "mix_pre", pairA, x_loaded, splits=True)
            act.wait_ge(S("pw_in"), count("pw_in", 16))
            nc.scalar.activation(pw[0][:], pwraw, ACT.Copy).then_inc(S("pw_hi"), 1)

            def glu_round(i, first):
                for k in range(SLOTS):
                    ahead(act, split_hi, rnd(U_GLU, i), k)
                    if first and k == 0:
                        norm_row(act, "n0")
                    if k % 2:
                        act.wait_ge(S(f"evac{k}"), count(f"evac{k}", rnd(U_GLU, i) + 1))
                        nc.scalar.activation(TH, TG[:, 0:T], ACT.Tanh, scale=0.5).then_inc(S("glu_th"), 1)
            glu_round(0, True)
            glu_round(1, False)
            for k in range(SLOTS):
                ahead(act, split_hi, rnd(U_POOL, 0), k)
            act.wait_ge(S("glu_v"), count("glu_v", 4))

            def conv_tap(j, t):
                act.wait_ge(S("conv_acc"), count("conv_acc", j * (ACC_TAPS - 1) + (max(1, t - 2) if t >= 2 else 0)))
                nc.scalar.activation(CTMP[:, (t % 2) * T:(t % 2 + 1) * T], VP[:, bass.ds(j * VPW + t, T)],
                                     ACT.Copy, scale=par_col("conv_w", j * CONV_K + t)).then_inc(S("conv_tmp"), 1)

            def gate_round(i):
                for k in range(SLOTS):
                    ahead(act, split_hi, rnd(U_GATE, i), k)
                    for t in range(k * ACC_TAPS // 4, (k + 1) * ACC_TAPS // 4):
                        conv_tap(i, t)
                    act.wait_ge(S(f"evac{k}"), count(f"evac{k}", rnd(U_GATE, i) + 1))
                    nc.scalar.activation(SG[:, bass.ds((4 * i + k) * T, T)], TG[:, (k % 2) * T:(k % 2 + 1) * T],
                                         ACT.Tanh, scale=0.5).then_inc(S("gate_th"), 1)
            with act.Fori(0, 2) as i:
                gate_round(i)
            for g in range(4):
                act.wait_ge(S("pooled"), count("pooled", g + 1))
                nc.scalar.activation(tile(pairB[0], g), PO[g], ACT.Copy).then_inc(S("pooled_hi"), 1)
            act.wait_ge(S("pooled_lo"), count("pooled_lo", 4))
            gate_round(2)
            for g in range(4):
                act.wait_ge(S("mix_done"), count("mix_done", g + 1))
                nc.scalar.activation(tile(pairB[0], 4 + g), ps[4 + g][:], ACT.Copy,
                                     scale=par_col("pool_scale", g)).then_inc(S("mixed_hi"), 1)
            gate_round(3)
            for k in range(SLOTS):
                ahead(act, split_hi, rnd(U_BRANCH, 0), k)
            for j in range(4):
                act.wait_ge(S("cv_centred"), count("cv_centred", j + 1))
                square(act, "ln", j, tile(CV, j))
            for j in range(4):
                act.wait_ge(S("cv_scaled"), count("cv_scaled", j + 1))
                if j > 1:
                    act.wait_ge(S("ln_z"), count("ln_z", j - 1))
                nc.scalar.activation(TG[:, (j % 2) * T:(j % 2 + 1) * T], tile(CV, j), ACT.Identity,
                                     scale=half[:, j:j + 1], bias=half[:, 4 + j:5 + j]).then_inc(S("ln_y"), 1)
                act.wait_ge(S("ln_y"), count("ln_y", j + 1))
                nc.scalar.activation([VA, TH][j % 2], TG[:, (j % 2) * T:(j % 2 + 1) * T], ACT.Tanh)\
                    .then_inc(S("ln_th"), 1)
                act.wait_ge(S("ln_z"), count("ln_z", j + 1))
                nc.scalar.activation(tile(pairB[0], j), tile(CV, j), ACT.Copy).then_inc(S("ln_hi"), 1)
            for k in range(SLOTS):
                ahead(act, split_hi, rnd(U_BRANCH, 1), k)
                for m in (2 * k, 2 * k + 1):
                    act.wait_ge(S("br_sum"), count("br_sum", m + 1))
                    nc.scalar.activation(tile(pairA[0], m), CTMP[:, (m % 2) * T:(m % 2 + 1) * T], ACT.Copy)\
                        .then_inc(S("br_hi"), 1)
            act.dma_start(X[:], io["xT"]).then_inc(S("x_back"), 16)
            act.wait_ge(S("br_lo"), count("br_lo", 8))
            for i in range(2):
                for k in range(SLOTS):
                    m = 4 * i + k
                    ahead(act, split_hi, rnd(U_WO, i), k)
                    evac_wait(act, rnd(U_WO, i), k)
                    nc.scalar.activation(tile(Y, m), ps[k % 2][:], ACT.Copy, scale=0.5).then_inc(S(f"evac{k}"), 1)
                    act.wait_ge(S(f"evac{k}"), count(f"evac{k}", rnd(U_WO, i) + 1))
                    square(act, "post0", m, tile(Y, m))
            norm_act(act, "n1", "mlp_pre", pairA, lambda e, m: e.wait_ge(S("x1"), count("x1", m + 1)))

            def mlp_group(g, first, last):
                for i in range(2):
                    for k in range(SLOTS):
                        r = rnd(U_MLP, g * 4 + i)
                        ahead(act, split_hi, r, k)
                        if first and i + k == 0:
                            norm_row(act, "n1")
                        n = g * 8 + 4 * i + k
                        evac_wait(act, r, k)
                        act.wait_ge(S("mlp_sq"), count("mlp_sq", n - 1))
                        nc.scalar.activation(TG[:, (k % 2) * T:(k % 2 + 1) * T], ps[k % 2][:], ACT.Relu)\
                            .then_inc(S(f"evac{k}"), 1)
                        act.wait_ge(S("mlp_sq"), count("mlp_sq", n + 1))
                        nc.scalar.activation(tile(pairB[0], 4 * i + k), MS[:, (k % 2) * T:(k % 2 + 1) * T], ACT.Copy)\
                            .then_inc(S("mlp_hi"), 1)
                for i in range(2):
                    for k in range(SLOTS):
                        ahead(act, split_hi, rnd(U_MLP, g * 4 + 2 + i), k)
                        if last:
                            act.wait_ge(S(f"evac{k}"), count(f"evac{k}", rnd(U_MLP, g * 4 + 2 + i) + 1))
                            square(act, "post1", 4 * i + k, tile(Y, 4 * i + k))
            mlp_group(0, True, False)
            with act.Fori(1, 3) as g:
                mlp_group(g, False, False)
            mlp_group(3, False, True)
            second_block_act(act)

        @block.vector
        def _(dve):
            v = nc.vector
            credit(dve, *(f"evac{s}" for s in range(SLOTS)))
            credit(dve, "mlp_sq", "conv_out", "t_lo", "d_o1", "d_o2")
            v.memset(ones[:], 1.0).then_inc(S("const"), 1)
            v.memset(mhalf[:, 0:NCH], -0.5)
            v.memset(mhalf[:, NCH:2 * NCH], 0.5).then_inc(S("const"), 1)
            v.memset(VP, 0.0).then_inc(S("zeros"), 1)
            dve.wait_ge(S("par_in"), count("par_in", 16))

            def par_range(name, n):
                return par[:, _cols[name][0]:_cols[name][0] + n]
            for at, name, n in ((0, "ln_g", 4), (4, "ln_b", 4), (8, "a_conv", 96)):
                v.tensor_scalar(half[:, at:at + n], par_range(name, n), 0.5, None, ALU.mult).then_inc(S("halved"), 1)
            for m in range(KT):
                x_loaded(dve, m)
                norm_lo(dve, "n0", "mix_pre", pairA, m)
                if m in (1, 3):
                    split_lo(dve, 0, m // 2)
            dve.wait_ge(S("pw_hi"), count("pw_hi", 1))
            v.tensor_tensor(pw[1][:], pwraw, pw[0][:].bitcast(F32), ALU.subtract).then_inc(S("pw_lo"), 1)
            token_mean(dve, "n0", 2, D)

            def glu_round(i, first):
                for k in range(SLOTS):
                    r = rnd(U_GLU, i)
                    ahead(dve, split_lo, r, k)
                    n = 2 * i + k // 2
                    if k % 2 == 0:
                        if first and k == 0:
                            dve.wait_ge(S("n0_R"), count("n0_R", 1))
                            dve.wait_ge(S("zeros"), count("zeros", 1))
                        evacuate(dve, r, k, VA, 0.5, R[:])
                    else:
                        evacuate(dve, r, k, TG[:, 0:T], 1.0, R[:])
                        dve.wait_ge(S("glu_th"), count("glu_th", n + 1))
                        at = n * VPW + CONV_K - 1
                        v.scalar_tensor_tensor(out=VP[:, at:at + T], in0=TH, scalar=1.0, in1=VA,
                                               op0=ALU.add, op1=ALU.mult).then_inc(S("glu_v"), 1)
                        dve.wait_ge(S("glu_v"), count("glu_v", n + 1))
            glu_round(0, True)
            glu_round(1, False)
            for u in UP:
                v.memset(u[:, 0:16], 0.0).then_inc(S("zeros"), 1)
            for k in range(SLOTS):
                r = rnd(U_POOL, 0)
                ahead(dve, split_lo, r, k)
                if k > 1:
                    dve.wait_ge(S("pooled"), count("pooled", k - 1))
                evacuate(dve, r, k, UP[k % 2][:, 16:UPW], 1.0, R[:])

            def gate_round(i):
                for k in range(SLOTS):
                    r = rnd(U_GATE, i)
                    ahead(dve, split_lo, r, k)
                    dve.wait_ge(S("gate_th"), count("gate_th", 4 * i + k - 1))
                    evacuate(dve, r, k, TG[:, (k % 2) * T:(k % 2 + 1) * T], 1.0, R[:])
                    for n in range(k * DVE_TAPS // 4, (k + 1) * DVE_TAPS // 4):
                        t = ACC_TAPS + n
                        x = VP[:, bass.ds(i * VPW + t, T)]
                        w = par_col("conv_w", i * CONV_K + t)
                        acc = CVC if n % 2 else tile(CV, i)
                        if n > 1:
                            dve.wait_ge(S("conv_step"), count("conv_step", i * (DVE_TAPS + 1) + n - 1))
                        if n == 0:
                            v.tensor_scalar(acc, x, w, par_col("conv_b", i), ALU.mult, ALU.add)\
                                .then_inc(S("conv_step"), 1)
                        elif n == 1:
                            v.tensor_scalar(acc, x, w, None, ALU.mult).then_inc(S("conv_step"), 1)
                        else:
                            v.scalar_tensor_tensor(out=acc, in0=x, scalar=w, in1=acc,
                                                   op0=ALU.mult, op1=ALU.add).then_inc(S("conv_step"), 1)
                dve.wait_ge(S("conv_step"), count("conv_step", (DVE_TAPS + 1) * i + DVE_TAPS))
                v.tensor_tensor(tile(CV, i), tile(CV, i), CVC, ALU.add).then_inc(S("conv_step"), 1)
                dve.wait_ge(S("conv_step"), count("conv_step", (DVE_TAPS + 1) * (i + 1)))
                dve.wait_ge(S("conv_acc"), count("conv_acc", (ACC_TAPS - 1) * (i + 1)))
                v.tensor_tensor(tile(CV, i), tile(CV, i), CVB, ALU.add).then_inc(S("conv_out"), 1)
            with dve.Fori(0, 3) as i:
                gate_round(i)
            for g in range(4):
                dve.wait_ge(S("mixed_hi"), count("mixed_hi", g + 1))
                v.scalar_tensor_tensor(out=tile(pairB[1], 4 + g), in0=ps[4 + g][:], scalar=par_col("pool_scale", g),
                                       in1=tile(pairB[0], 4 + g).bitcast(F32), op0=ALU.mult, op1=ALU.subtract)\
                    .then_inc(S("mixed_lo"), 1)
            gate_round(3)

            def gated_pool(k):
                r = rnd(U_BRANCH, 0)
                evac_wait(dve, r, k)
                v.scalar_tensor_tensor(out=HS[2 * k], in0=tile(SG, 2 * k), scalar=1.0, in1=ps[k % 2][:],
                                       op0=ALU.add, op1=ALU.mult).then_inc(S("br_part"), 1)
                v.scalar_tensor_tensor(out=HS[2 * k + 1], in0=tile(SG, 2 * k + 1), scalar=1.0, in1=ps[k % 2 + 4][:],
                                       op0=ALU.add, op1=ALU.mult).then_inc(S(f"evac{k}"), 1)
            ahead(dve, split_lo, rnd(U_BRANCH, 0), 0)
            gated_pool(0)
            gated_pool(1)
            ahead(dve, split_lo, rnd(U_BRANCH, 0), 1)
            dve.wait_ge(S("ln_mean"), count("ln_mean", 1))
            for j in range(4):
                v.scalar_tensor_tensor(out=tile(CV, j), in0=ps[6][:], scalar=-1.0 / (4 * P), in1=tile(CV, j),
                                       op0=ALU.mult, op1=ALU.add).then_inc(S("cv_centred"), 1)
            ahead(dve, split_lo, rnd(U_BRANCH, 0), 2)
            gated_pool(2)
            token_mean(dve, "ln", 2, 4 * P)
            ahead(dve, split_lo, rnd(U_BRANCH, 0), 3)
            dve.wait_ge(S("ln_row"), count("ln_row", 1))
            for j in range(4):
                dve.wait_ge(S("ln_sq"), count("ln_sq", j + 1))
                v.tensor_tensor(tile(CV, j), tile(CV, j), ps[3][:], ALU.mult).then_inc(S("cv_scaled"), 1)
            gated_pool(3)
            for j in range(4):
                dve.wait_ge(S("ln_th"), count("ln_th", j + 1))
                v.scalar_tensor_tensor(out=tile(CV, j), in0=[VA, TH][j % 2], scalar=1.0,
                                       in1=TG[:, (j % 2) * T:(j % 2 + 1) * T], op0=ALU.add, op1=ALU.mult)\
                    .then_inc(S("ln_z"), 1)
                dve.wait_ge(S("ln_hi"), count("ln_hi", j + 1))
                v.tensor_tensor(tile(pairB[1], j), tile(CV, j), tile(pairB[0], j).bitcast(F32), ALU.subtract)\
                    .then_inc(S("ln_lo"), 1)
            dve.wait_ge(S("br_part"), count("br_part", 4))
            for k in range(SLOTS):
                r = rnd(U_BRANCH, 1)
                ahead(dve, split_lo, r, k)
                evac_wait(dve, r, k)
                for half_, (bank, name) in enumerate(((k % 2, "br_part"), (k % 2 + 4, f"evac{k}"))):
                    m = 2 * k + half_
                    v.scalar_tensor_tensor(out=[VA, TH][half_], in0=tile(SG, 8 + m), scalar=1.0, in1=ps[bank][:],
                                           op0=ALU.add, op1=ALU.mult).then_inc(S(name), 1)
                dve.wait_ge(S("br_part"), count("br_part", 4 + k + 1))
                dve.wait_ge(S(f"evac{k}"), count(f"evac{k}", r + 1))
                for half_ in range(2):
                    m = 2 * k + half_
                    if m > 1:
                        dve.wait_ge(S("br_lo"), count("br_lo", m - 1))
                    v.tensor_tensor(CTMP[:, half_ * T:(half_ + 1) * T], HS[m], [VA, TH][half_], ALU.add)\
                        .then_inc(S("br_sum"), 1)
                dve.wait_ge(S("br_sum"), count("br_sum", 2 * k + 2))
            for i in range(2):
                for k in range(SLOTS):
                    ahead(dve, split_lo, rnd(U_WO, i), k)

            def add_normed(tag, xtag, g, bank, next_tag, next_g):
                dve.wait_ge(S(tag + "_row"), count(tag + "_row", 1))
                for m in range(KT):
                    t = TG[:, (m % 2) * T:(m % 2 + 1) * T]
                    if m > 1:
                        dve.wait_ge(S(xtag), count(xtag, m - 1))
                    v.scalar_tensor_tensor(out=t, in0=tile(Y, m), scalar=par_col(g, m), in1=ps[bank][:],
                                           op0=ALU.mult, op1=ALU.mult).then_inc(S(tag + "_t"), 1)
                    dve.wait_ge(S(tag + "_t"), count(tag + "_t", m + 1))
                    v.tensor_tensor(tile(X, m), tile(X, m), t, ALU.add).then_inc(S(xtag), 1)
                    if m:
                        norm_lo(dve, next_tag, next_g, pairA, m - 1)
                norm_lo(dve, next_tag, next_g, pairA, KT - 1)
            dve.wait_ge(S("post0_ss"), count("post0_ss", 8))
            token_mean(dve, "post0", 4, D)
            dve.wait_ge(S("x_back"), count("x_back", 16))
            add_normed("post0", "x1", "mix_post", 5, "n1", "mlp_pre")
            token_mean(dve, "n1", 2, D)

            def mlp_group(g, first):
                for i in range(2):
                    for k in range(SLOTS):
                        ahead(dve, split_lo, rnd(U_MLP, g * 4 + i), k)
                        n = g * 8 + 4 * i + k
                        dve.wait_ge(S(f"evac{k}"), count(f"evac{k}", rnd(U_MLP, g * 4 + i) + 1))
                        t = TG[:, (k % 2) * T:(k % 2 + 1) * T]
                        if not (first and 4 * i + k < 2):
                            dve.wait_ge(S("mlp_lo"), count("mlp_lo", n - 1))
                        v.tensor_tensor(MS[:, (k % 2) * T:(k % 2 + 1) * T], t, t, ALU.mult).then_inc(S("mlp_sq"), 1)
                for i in range(2):
                    for k in range(SLOTS):
                        r = rnd(U_MLP, g * 4 + 2 + i)
                        m = 4 * i + k
                        ahead(dve, split_lo, r, k)
                        evac_wait(dve, r, k)
                        if first:
                            v.tensor_copy(tile(Y, m), ps[k % 2][:]).then_inc(S(f"evac{k}"), 1)
                        else:
                            v.tensor_tensor(tile(Y, m), ps[k % 2][:], tile(Y, m), ALU.add).then_inc(S(f"evac{k}"), 1)
            mlp_group(0, True)
            with dve.Fori(1, 3) as g:
                mlp_group(g, False)
            mlp_group(3, False)
            dve.wait_ge(S("tw_hi"), count("tw_hi", 1))
            v.tensor_tensor(TW[1], tailw, TW[0].bitcast(F32), ALU.subtract).then_inc(S("tw_lo"), 1)
            r1, r2, r4 = tok[:, NCH:2 * NCH], tok[:, 8:12], tok[:, 12:16]
            v.tensor_tensor(r2, r1, r1, ALU.mult).then_inc(S("r_power"), 1)
            dve.wait_ge(S("r_power"), count("r_power", 1))
            v.tensor_tensor(r4, r2, r2, ALU.mult).then_inc(S("r_power"), 1)
            dve.wait_ge(S("r_power"), count("r_power", 2))
            dve.wait_ge(S("post1_sum"), count("post1_sum", 1))
            v.scalar_tensor_tensor(out=tok[:, 16:20], in0=ps[4][:, 0:NCH], scalar=1.0 / D, in1=r4,
                                   op0=ALU.mult, op1=ALU.mult).then_inc(S("r_power"), 1)
            dve.wait_ge(S("r_power"), count("r_power", 3))
            v.tensor_scalar(tok[:, 0:NCH], tok[:, 16:20], EPS, None, ALU.add).then_inc(S("post1_ms"), 1)
            add_normed("post1", "x2", "mlp_post", 5, "na", "a_norm")
            second_block_dve(dve)

        @block.gpsimd
        def _(pool):
            g_ = nc.gpsimd
            credit(pool, "conv_acc", "o_lo")
            pool.sem_inc(S("gate_th"), CREDIT["gate_th"])
            pool.wait_ge(S("const"), count("const", 2))
            pool.wait_ge(S("cst_in"), count("cst_in", 16))
            sum_squares(pool, "n0", KT)
            token_rsqrt(pool, "n0")
            step = 0
            for g, window in enumerate(POOL_WINDOWS):
                u = UP[g % 2]
                pool.wait_ge(S(f"evac{g}"), count(f"evac{g}", rnd(U_POOL, 0) + 1))
                pool.wait_ge(S("zeros"), count("zeros", 3))
                src, shift = u, 1
                while shift < window:
                    dst = PAB[step % 2]
                    lo = 2 * shift - 1
                    if step:
                        pool.wait_ge(S("pool_step"), count("pool_step", step))
                    g_.tensor_tensor(dst[:, lo:UPW], src[:, lo:UPW], src[:, lo - shift:UPW - shift], ALU.add)\
                        .then_inc(S("pool_step"), 1)
                    step += 1
                    src, shift = dst, 2 * shift
                pool.wait_ge(S("pool_step"), count("pool_step", step))
                dst = PAB[step % 2]
                g_.tensor_scalar(dst[:, 16:UPW], src[:, 16:UPW], 1.0 / window, 0.0, ALU.mult, ALU.add)\
                    .then_inc(S("pool_step"), 1)
                step += 1
                pool.wait_ge(S("pool_step"), count("pool_step", step))
                inv = cst[:, C_INV + 16 * g:C_INV + 16 * (g + 1)]
                g_.tensor_tensor(dst[:, 16:32], src[:, 16:32], inv, ALU.mult).then_inc(S("pool_step"), 1)
                step += 1
                pool.wait_ge(S("pool_step"), count("pool_step", step))
                g_.tensor_tensor(PO[g], dst[:, 16:UPW], u[:, 16:UPW], ALU.subtract).then_inc(S("pooled"), 1)
                pool.wait_ge(S("pooled"), count("pooled", g + 1))

            def conv_sum(i):
                for t in range(1, ACC_TAPS):
                    pool.wait_ge(S("conv_tmp"), count("conv_tmp", ACC_TAPS * i + t + 1))
                    tmp = CTMP[:, (t % 2) * T:(t % 2 + 1) * T]
                    if t == 1:
                        pool.wait_ge(S("conv_out"), count("conv_out", i))
                    else:
                        pool.wait_ge(S("conv_acc"), count("conv_acc", (ACC_TAPS - 1) * i + t - 1))
                    g_.tensor_tensor(CVB, CTMP[:, 0:T] if t == 1 else CVB, tmp, ALU.add).then_inc(S("conv_acc"), 1)
            with pool.Fori(0, 2) as i:
                conv_sum(i)
            for g in range(4):
                pool.wait_ge(S("pooled_hi"), count("pooled_hi", g + 1))
                g_.tensor_tensor(tile(pairB[1], g), PO[g], tile(pairB[0], g).bitcast(F32), ALU.subtract)\
                    .then_inc(S("pooled_lo"), 1)
            with pool.Fori(2, 4) as i:
                conv_sum(i)
            sum_squares(pool, "ln", 4)
            token_rsqrt(pool, "ln")

            def lo_part(tag, m, src, dst, ready=None):
                pool.wait_ge(S(tag + "_hi"), count(tag + "_hi", ready if ready is not None else m + 1))
                g_.tensor_tensor(tile(dst[1], m), src, tile(dst[0], m).bitcast(F32), ALU.subtract)\
                    .then_inc(S(tag + "_lo"), 1)
            for m in range(8):
                lo_part("br", m, CTMP[:, (m % 2) * T:(m % 2 + 1) * T], pairA)
            sum_squares(pool, "post0", KT)
            token_rsqrt(pool, "post0")
            sum_squares(pool, "n1", KT)
            token_rsqrt(pool, "n1")
            with pool.Fori(0, 4) as g:
                for m in range(8):
                    lo_part("mlp", m, MS[:, (m % 2) * T:(m % 2 + 1) * T], pairB, g * 8 + m + 1)
            sum_squares(pool, "post1", KT)
            pool.wait_ge(S("post1_ms"), count("post1_ms", 1))
            g_.tensor_tensor(tok[:, 20:24], tok[:, 0:NCH], mhalf[:, 0:NCH], ALU.pow).then_inc(S("post1_pow"), 1)
            pool.wait_ge(S("post1_pow"), count("post1_pow", 1))
            g_.tensor_tensor(tok[:, NCH:2 * NCH], tok[:, 20:24], tok[:, 8:12], ALU.mult).then_inc(S("post1_rt"), 1)
            second_block_pool(pool)


def _blocks(w, k0, n, m):
    b = w[k0 * P:(k0 + n) * P, m * P:(m + 1) * P].reshape(n, P, P)
    return b.transpose(1, 0, 2).reshape(P, n * P)


def _pack(inp):
    f = np.float32
    ws = np.zeros((U_END, P, 1024), f)
    at = [0]

    def put(*parts):
        a = np.concatenate(parts, axis=1)
        ws[at[0], :, :a.shape[1]] = a
        at[0] += 1
    w_in = inp["w_in"][0]
    for j in range(4):
        put(_blocks(w_in, 0, 8, 4 + j))
        put(_blocks(w_in, 0, 8, 8 + j))
    for j in range(4):
        put(_blocks(w_in, 0, 8, j))
    for j in range(16):
        put(_blocks(w_in, 0, 8, 12 + j))
    for w in (inp["w_pool_out"][0], inp["w_conv_out"][0]):
        for m in range(0, 8, 2):
            put(_blocks(w, 0, 4, m), _blocks(w, 0, 4, m + 1))
    for m in range(8):
        put(_blocks(inp["w_o"][0], 0, 8, m))
    for g in range(4):
        for m in range(8):
            put(_blocks(inp["w_up"][0], 0, 8, 8 * g + m))
        for m in range(8):
            put(_blocks(inp["w_down"][0], 8 * g, 8, m))
    a_in = inp["a_w_in_2"][0]
    for h in range(HEADS):
        for part in range(4):
            put(_blocks(a_in, 0, 8, 8 * part + h))
    for m in range(8):
        put(_blocks(inp["a_w_out_2"][0], 0, 8, m))

    def ffn(layer):
        up, down = inp["f_w_up_2"][layer], inp["f_w_down_2"][layer]
        first = 0
        for n in MID_GROUPS:
            for m in range(first, first + n):
                put(_blocks(up, 0, 8, m))
                put(_blocks(up, 0, 8, 22 + m))
            for m in range(8):
                put(_blocks(down, first, n, m))
            first += n
    ffn(0)
    for m in range(4):
        put(_blocks(inp["kv_w_2"], 0, 8, m))
    heads = [h for pair in ATT_TILE_HEADS for h in pair]
    by_head = lambda w, axis: np.concatenate(
        [np.take(w, range(64 * h, 64 * h + 64), axis=axis) for h in heads], axis=axis)
    wq = by_head(inp["b_w_q_2"][0], 1)
    for m in range(8):
        put(_blocks(wq, 0, 8, m))
    wo = by_head(inp["b_w_o_2"][0], 0)
    for m in range(8):
        put(_blocks(wo, 0, 8, m))
    ffn(1)
    assert at[0] == U_END, at

    par = np.zeros((P, NPAR), f)

    def col(name, vec):
        c, n = _cols[name]
        par[:, c:c + n] = np.asarray(vec).reshape(n, P).T
    for name, key in (("mix_pre", "norm_mix_pre"), ("mix_post", "norm_mix_post"), ("mlp_pre", "norm_mlp_pre"),
                      ("mlp_post", "norm_mlp_post"), ("a_norm", "a_norm_2"), ("kv_norm", "kv_norm_2"),
                      ("b_norm", "b_norm_2"), ("final", "final_norm_2"), ("pool_scale", "pool_scale"),
                      ("conv_b", "conv_b"), ("ln_g", "conv_ln_g"), ("ln_b", "conv_ln_b"), ("onorm", "a_onorm_2"),
                      ("kv_b", "kv_b_2"), ("b_o", "b_b_o_2")):
        col(name, inp[key])
    col("b_q", by_head(inp["b_b_q_2"][0], 0))
    for layer in range(2):
        col(f"f_norm{layer}", inp["f_norm_2"][layer])
        col(f"f_bias{layer}", inp["f_conv_b_2"][layer])

    def taps(name, w):
        c, n = _cols[name]
        par[:, c:c + n] = w.reshape(w.shape[0], -1, P).transpose(2, 1, 0).reshape(P, n)
    taps("conv_w", inp["conv_w"][0])
    taps("a_conv", inp["a_conv_w_2"][0])
    taps("f_conv0", inp["f_conv_w_2"][0])
    taps("f_conv1", inp["f_conv_w_2"][1])

    cst = np.zeros((P, NCONST), f)
    i, j = np.arange(P)[:, None], np.arange(P)[None, :]
    cst[:, C_ID:C_ID + P] = i == j
    cst[:, C_TRI:C_TRI + P] = i <= j
    cst[:, C_NEG:C_NEG + P] = np.where(j >= i, 0, -FAR)
    for lvl in range(7):
        m = (i >> (lvl + 1) == j >> (lvl + 1)) & ((i >> lvl) & 1 == 1) & ((j >> lvl) & 1 == 0)
        cst[:, C_LVL + lvl * P:C_LVL + (lvl + 1) * P] = m.T if lvl == 0 else m
    dist = i + P - np.arange(2 * P)[None, :]
    cst[:, C_DIST:C_DIST + 2 * P] = np.where((dist >= 0) & (dist < P), dist, FAR)
    for g, window in enumerate(POOL_WINDOWS):
        cst[:, C_INV + 16 * g:C_INV + 16 * g + 16] = 1.0 / np.minimum(np.arange(16) + 1, window)
    slopes = (2.0 ** (-8.0 * np.arange(1, 17) / 16)).astype(f)
    row = np.concatenate([inp["a_A_log_2"][0], inp["a_dt_bias_2"][0], inp["b_sinks_2"][0][heads], -slopes[heads]])
    return {
        "xT": np.asarray(inp["x"])[0].T.reshape(KT, P, T).transpose(1, 0, 2).reshape(P, KT * T),
        "ws": ws, "par": par, "cst": cst,
        "pw": np.asarray(inp["pool_w"])[0].transpose(1, 0, 2).reshape(P, 4 * P),
        "tail": a_in[:, 4 * D:].reshape(KT, P, 16).transpose(1, 0, 2).reshape(P, KT * 16),
        "row": row.reshape(1, 48),
    }


def kernel(**inputs):
    import concourse.bacc as bacc
    from concourse.bass_utils import run_bass_kernel_spmd

    packed = {k: np.ascontiguousarray(v) for k, v in _pack({k: np.asarray(v) for k, v in inputs.items()}).items()}
    nc = bacc.Bacc("TRN2", target_bir_lowering=False, num_devices=1)
    io = {k: nc.dram_tensor("d_" + k, v.shape, F32, kind="ExternalInput").ap() for k, v in packed.items()}
    io["out"] = nc.dram_tensor("d_out", (P, KT * T), F32, kind="ExternalOutput").ap()
    build(nc, io)
    r = run_bass_kernel_spmd(nc, [{"d_" + k: v for k, v in packed.items()}], core_ids=[0])
    out = r.results[0]["d_out"]
    return out.reshape(P, KT, T).transpose(2, 1, 0).reshape(1, T, D)
```
